# Optimizing a Trainium2 kernel written in Bass

```python
import math
import jax, jax.numpy as jnp
from jax import lax
import numpy as np

D_MODEL = 1024
BATCH = 1
SEQ = 256
DEPTH = 2

HEAD_DIM = 64
MLA_HEADS = 6
MLA_NOPE = 64
MLA_ROPE = 32
MLA_V = 64
MLA_QK = MLA_NOPE + MLA_ROPE
Q_LORA = 256
KV_LORA = 128
SWA_HEADS = 6
SWA_KV_HEADS = 2
SWA_GROUP = SWA_HEADS // SWA_KV_HEADS
WINDOW = 128
SB_HEADS = 4
BLOCK = 128
NUM_BUCKETS = 32
MAX_DISTANCE = 128
D_FF = 2816
ROPE_THETA = 10000.0
EPS = 1e-6

MLA_WIDTH = MLA_HEADS * MLA_V
SWA_WIDTH = SWA_HEADS * HEAD_DIM
SB_WIDTH = SB_HEADS * HEAD_DIM
D_MIX = MLA_WIDTH + SWA_WIDTH + SB_WIDTH
IN_SIZES = (Q_LORA, KV_LORA, MLA_ROPE,
            SWA_HEADS * HEAD_DIM, SWA_KV_HEADS * HEAD_DIM, SWA_KV_HEADS * HEAD_DIM,
            3 * SB_HEADS * HEAD_DIM)
D_IN = Q_LORA + KV_LORA + MLA_ROPE + (SWA_HEADS + 2 * SWA_KV_HEADS) * HEAD_DIM + 3 * SB_HEADS * HEAD_DIM


def _split_cols(x, sizes):
    offs = np.cumsum(np.array(sizes))[:-1].tolist()
    return jnp.split(x, offs, axis=-1)

def rms_norm(x, g):
    xf = x.astype(jnp.float32)
    y = xf * lax.rsqrt(jnp.mean(xf * xf, axis=-1, keepdims=True) + EPS)
    return (y * g.astype(jnp.float32)).astype(x.dtype)

def modulate(x, g, shift, scale):
    return rms_norm(x, g) * (1.0 + scale[:, None, :]) + shift[:, None, :]

def rope(x, pos):
    half = x.shape[-1] // 2
    freqs = ROPE_THETA ** (-jnp.arange(half, dtype=jnp.float32) / half)
    ang = pos.astype(jnp.float32)[:, :, None, None] * freqs
    cos, sin = jnp.cos(ang), jnp.sin(ang)
    xf = x.astype(jnp.float32)
    x1, x2 = xf[..., :half], xf[..., half:]
    return jnp.concatenate([x1 * cos - x2 * sin, x2 * cos + x1 * sin], axis=-1).astype(x.dtype)

def t5_bucket(rel):
    n = jnp.maximum(rel, 0)
    max_exact = NUM_BUCKETS // 2
    nf = jnp.maximum(n, 1).astype(jnp.float32)
    large = max_exact + (jnp.log(nf / max_exact) / math.log(MAX_DISTANCE / max_exact)
                         * (NUM_BUCKETS - max_exact)).astype(jnp.int32)
    large = jnp.minimum(large, NUM_BUCKETS - 1)
    return jnp.where(n < max_exact, n, large)

def swiglu(h, w_gu, w_down):
    g, u = jnp.split(h @ w_gu, 2, axis=-1)
    return (jax.nn.silu(g) * u) @ w_down

def mla_attention(q, k, v):
    B, S, H, Dq = q.shape
    nb = S // BLOCK
    qb = q.reshape(B, nb, BLOCK, H, Dq).transpose(1, 0, 2, 3, 4)
    key_idx = jnp.arange(S)
    scale = Dq ** -0.5

    def one_block(args):
        i, qi = args
        s = jnp.einsum('bqhd,bkhd->bhqk', qi, k).astype(jnp.float32) * scale
        q_idx = i * BLOCK + jnp.arange(BLOCK)
        mask = key_idx[None, :] <= q_idx[:, None]
        p = jax.nn.softmax(jnp.where(mask, s, -jnp.inf), axis=-1)
        return jnp.einsum('bhqk,bkhd->bqhd', p.astype(v.dtype), v)

    out = lax.map(one_block, (jnp.arange(nb), qb))
    return out.transpose(1, 0, 2, 3, 4).reshape(B, S, H * v.shape[-1])

def swa_attention(q, k, v, pos, sinks, rel_table):
    B, S, Hq, D = q.shape
    nb = S // WINDOW

    def band(x):
        xb = x.reshape((B, nb, WINDOW) + x.shape[2:])
        prev = jnp.concatenate([jnp.zeros_like(xb[:, :1]), xb[:, :-1]], axis=1)
        return jnp.concatenate([prev, xb], axis=2)

    kb, vb = band(k), band(v)
    qb = q.reshape(B, nb, WINDOW, SWA_KV_HEADS, SWA_GROUP, D)
    s = jnp.einsum('bnqkgd,bnskd->bnkgqs', qb, kb).astype(jnp.float32) * (D ** -0.5)
    rel = pos.reshape(B, nb, WINDOW)[..., :, None] - band(pos)[..., None, :]
    bias = rel_table[t5_bucket(rel)].astype(jnp.float32)
    bias = bias.reshape(B, nb, WINDOW, 2 * WINDOW, SWA_KV_HEADS, SWA_GROUP).transpose(0, 1, 4, 5, 2, 3)
    q_in = jnp.arange(WINDOW)[:, None] + WINDOW
    k_in = jnp.arange(2 * WINDOW)[None, :]
    d = q_in - k_in
    in_win = (d >= 0) & (d < WINDOW)
    not_pad = (jnp.arange(nb)[:, None, None] > 0) | (k_in[None] >= WINDOW)
    mask = (in_win[None] & not_pad)[None, :, None, None]
    s = jnp.where(mask, s + bias, -jnp.inf)
    sink = sinks.astype(jnp.float32).reshape(SWA_KV_HEADS, SWA_GROUP)[None, None, :, :, None, None]
    m = jnp.maximum(jnp.max(s, axis=-1, keepdims=True), sink)
    p = jnp.exp(s - m)
    p = p / (jnp.sum(p, axis=-1, keepdims=True) + jnp.exp(sink - m))
    o = jnp.einsum('bnkgqs,bnskd->bnqkgd', p.astype(v.dtype), vb)
    return o.reshape(B, S, Hq * D)

def stick_breaking_attention(q, k, v):
    B, S, H, D = q.shape
    nb = S // BLOCK
    qb = q.reshape(B, nb, BLOCK, H, D).transpose(1, 0, 2, 3, 4)
    key_idx = jnp.arange(S)
    scale = D ** -0.5

    def one_block(args):
        i, qi = args
        z = jnp.einsum('bqhd,bkhd->bhqk', qi, k).astype(jnp.float32) * scale
        q_idx = i * BLOCK + jnp.arange(BLOCK)
        mask = key_idx[None, :] < q_idx[:, None]
        log_not = jnp.where(mask, jax.nn.log_sigmoid(-z), 0.0)
        after = lax.cumsum(log_not, axis=3, reverse=True) - log_not
        a = jnp.where(mask, jnp.exp(jax.nn.log_sigmoid(z) + after), 0.0)
        return jnp.einsum('bhqk,bkhd->bqhd', a.astype(v.dtype), v)

    out = lax.map(one_block, (jnp.arange(nb), qb))
    return out.transpose(1, 0, 2, 3, 4).reshape(B, S, H * D)

def first_inputs(seed: int = 0) -> dict:
    key = jax.random.key(seed)
    ks = jax.random.split(key, 24)
    f32 = jnp.float32

    def nrm(k, shape, scale):
        return jax.random.normal(k, shape, f32) * scale

    def gain(k, shape):
        return 1.0 + 0.1 * jax.random.normal(k, shape, f32)

    x = jax.random.normal(ks[0], (BATCH, SEQ, D_MODEL), f32)
    c = jax.random.normal(ks[1], (BATCH, D_MODEL), f32)
    offset = jax.random.randint(ks[2], (BATCH, 1), 0, 4096, dtype=jnp.int32)
    positions = offset + jnp.arange(SEQ, dtype=jnp.int32)[None, :]
    return {
        "x": x,
        "c": c,
        "positions": positions,
        "rel_bias": nrm(ks[3], (NUM_BUCKETS, SWA_HEADS), 0.5),
        "norm_g": gain(ks[4], (DEPTH, 3, D_MODEL)),
        "w_mod": nrm(ks[5], (DEPTH, D_MODEL, 9 * D_MODEL), 0.5 * D_MODEL ** -0.5),
        "b_mod": nrm(ks[6], (DEPTH, 9 * D_MODEL), 0.02),
        "w_ffn1_gu": nrm(ks[7], (DEPTH, D_MODEL, 2 * D_FF), D_MODEL ** -0.5),
        "w_ffn1_down": nrm(ks[8], (DEPTH, D_FF, D_MODEL), D_FF ** -0.5),
        "w_in": nrm(ks[9], (DEPTH, D_MODEL, D_IN), D_MODEL ** -0.5),
        "q_a_norm": gain(ks[10], (DEPTH, Q_LORA)),
        "kv_a_norm": gain(ks[11], (DEPTH, KV_LORA)),
        "w_uq": nrm(ks[12], (DEPTH, Q_LORA, MLA_HEADS * MLA_QK), Q_LORA ** -0.5),
        "w_ukv": nrm(ks[13], (DEPTH, KV_LORA, MLA_HEADS * (MLA_NOPE + MLA_V)), KV_LORA ** -0.5),
        "mla_q_norm": gain(ks[14], (DEPTH, MLA_QK)),
        "mla_k_norm": gain(ks[15], (DEPTH, MLA_QK)),
        "swa_q_norm": gain(ks[16], (DEPTH, HEAD_DIM)),
        "swa_k_norm": gain(ks[17], (DEPTH, HEAD_DIM)),
        "sinks": nrm(ks[18], (DEPTH, SWA_HEADS), 0.5),
        "out_norm": gain(ks[19], (DEPTH, D_MIX)),
        "w_out": nrm(ks[20], (DEPTH, D_MIX, D_MODEL), D_MIX ** -0.5),
        "w_ffn2_gu": nrm(ks[21], (DEPTH, D_MODEL, 2 * D_FF), D_MODEL ** -0.5),
        "w_ffn2_down": nrm(ks[22], (DEPTH, D_FF, D_MODEL), D_FF ** -0.5),
    }

def first_block(x, c, positions, rel_bias, norm_g, w_mod, b_mod, w_ffn1_gu, w_ffn1_down,
              w_in, q_a_norm, kv_a_norm, w_uq, w_ukv, mla_q_norm, mla_k_norm,
              swa_q_norm, swa_k_norm, sinks, out_norm, w_out, w_ffn2_gu, w_ffn2_down):
    B, S, _ = x.shape
    cond = jax.nn.silu(c)
    for l in range(DEPTH):
        mod = cond @ w_mod[l] + b_mod[l]
        sh1, sc1, g1, sh2, sc2, g2, sh3, sc3, g3 = jnp.split(mod, 9, axis=-1)

        h = modulate(x, norm_g[l, 0], sh1, sc1)
        x = x + 0.5 * g1[:, None, :] * swiglu(h, w_ffn1_gu[l], w_ffn1_down[l])

        h = modulate(x, norm_g[l, 1], sh2, sc2)
        proj = h @ w_in[l]
        c_q, c_kv, k_pe, q_s, k_s, v_s, qkv_sb = _split_cols(proj, IN_SIZES)

        qa = (rms_norm(c_q, q_a_norm[l]) @ w_uq[l]).reshape(B, S, MLA_HEADS, MLA_QK)
        qa = rms_norm(qa, mla_q_norm[l])
        qa = jnp.concatenate([qa[..., :MLA_NOPE], rope(qa[..., MLA_NOPE:], positions)], axis=-1)
        kv = (rms_norm(c_kv, kv_a_norm[l]) @ w_ukv[l]).reshape(B, S, MLA_HEADS, MLA_NOPE + MLA_V)
        k_nope, va = kv[..., :MLA_NOPE], kv[..., MLA_NOPE:]
        k_pe_h = jnp.broadcast_to(k_pe[:, :, None, :], (B, S, MLA_HEADS, MLA_ROPE))
        ka = rms_norm(jnp.concatenate([k_nope, k_pe_h], axis=-1), mla_k_norm[l])
        ka = jnp.concatenate([ka[..., :MLA_NOPE], rope(ka[..., MLA_NOPE:], positions)], axis=-1)
        o_a = mla_attention(qa, ka, va)

        qb = rms_norm(q_s.reshape(B, S, SWA_HEADS, HEAD_DIM), swa_q_norm[l])
        kb = rms_norm(k_s.reshape(B, S, SWA_KV_HEADS, HEAD_DIM), swa_k_norm[l])
        vb = v_s.reshape(B, S, SWA_KV_HEADS, HEAD_DIM)
        o_b = swa_attention(qb, kb, vb, positions, sinks[l], rel_bias)

        qc, kc, vc = jnp.split(qkv_sb.reshape(B, S, 3, SB_HEADS, HEAD_DIM), 3, axis=2)
        o_c = stick_breaking_attention(qc[:, :, 0], kc[:, :, 0], vc[:, :, 0])

        on = out_norm[l]
        mix = jnp.concatenate([
            rms_norm(o_a, on[:MLA_WIDTH]),
            rms_norm(o_b, on[MLA_WIDTH:MLA_WIDTH + SWA_WIDTH]),
            rms_norm(o_c, on[MLA_WIDTH + SWA_WIDTH:]),
        ], axis=-1)
        x = x + g2[:, None, :] * (mix @ w_out[l])

        h = modulate(x, norm_g[l, 2], sh3, sc3)
        x = x + 0.5 * g3[:, None, :] * swiglu(h, w_ffn2_gu[l], w_ffn2_down[l])
    return x


RET_HEADS = D_MODEL // 128
RET_QK_DIM = 64
RET_V_DIM = 128
RET_QK = RET_HEADS * RET_QK_DIM
RET_V = RET_HEADS * RET_V_DIM
CHUNK = 128
ROPE_BASE = 10000.0
POOL_WINDOWS = (2, 4, 8, 16)
POOL_GROUPS = len(POOL_WINDOWS)
POOL_DIM = D_MODEL // 2
POOL_GROUP_DIM = POOL_DIM // POOL_GROUPS
N_BRANCH = 2
IN_COLS = 2 * RET_QK + 2 * RET_V + POOL_DIM + N_BRANCH * D_MODEL
IN_SPLITS = (RET_QK, 2 * RET_QK, 2 * RET_QK + RET_V, 2 * RET_QK + 2 * RET_V,
             2 * RET_QK + 2 * RET_V + POOL_DIM)
_FF_RAW = -(-8 * D_MODEL // 3)
D_FF_2 = -(-_FF_RAW // 256) * 256
N_MOD = 6


def rmsnorm(x, w):
    xf = x.astype(jnp.float32)
    y = xf * lax.rsqrt(jnp.mean(xf * xf, axis=-1, keepdims=True) + EPS)
    return (y * w.astype(jnp.float32)).astype(x.dtype)

def head_rmsnorm(x):
    xf = x.astype(jnp.float32)
    y = xf * lax.rsqrt(jnp.mean(xf * xf, axis=-1, keepdims=True) + EPS)
    return y.astype(x.dtype)

def modulate_2(h, shift, scale):
    return h * (1.0 + scale[:, None, :]) + shift[:, None, :]

def rotary(x, cos, sin):
    x1, x2 = jnp.split(x, 2, axis=-1)
    return jnp.concatenate([x1 * cos - x2 * sin, x2 * cos + x1 * sin], axis=-1)

def retention_chunkwise(q, k, v):
    bsz, s, h, dk = q.shape
    dv = v.shape[-1]
    n = s // CHUNK
    dt = q.dtype
    log_g = jnp.log1p(-(2.0 ** (-5.0 - jnp.arange(h, dtype=jnp.float32))))
    idx = jnp.arange(CHUNK, dtype=jnp.float32)
    diff = idx[:, None] - idx[None, :]
    intra = jnp.where(diff >= 0, jnp.exp(log_g[:, None, None] * jnp.maximum(diff, 0.0)), 0.0).astype(dt)
    q_dec = jnp.exp(log_g[:, None] * (idx + 1.0)).astype(dt)
    k_dec = jnp.exp(log_g[:, None] * (CHUNK - 1.0 - idx)).astype(dt)
    chunk_dec = jnp.exp(log_g * CHUNK).astype(dt)
    qc = (q * (dk ** -0.5)).reshape(bsz, n, CHUNK, h, dk)
    kc = k.reshape(bsz, n, CHUNK, h, dk)
    vc = v.reshape(bsz, n, CHUNK, h, dv)
    scores = jnp.einsum('bncha,bnmha->bnhcm', qc, kc) * intra[None, None]
    inner = jnp.einsum('bnhcm,bnmhd->bnchd', scores, vc)
    kv = jnp.einsum('bnmha,hm,bnmhd->bnhad', kc, k_dec, vc)

    def step(state, kv_i):
        return state * chunk_dec[None, :, None, None] + kv_i, state

    init = jnp.zeros((bsz, h, dk, dv), dtype=kv.dtype)
    _, prev = lax.scan(step, init, jnp.moveaxis(kv, 1, 0))
    prev = jnp.moveaxis(prev, 0, 1)
    cross = jnp.einsum('bncha,hc,bnhad->bnchd', qc, q_dec, prev)
    return (inner + cross).reshape(bsz, s, h, dv)

def causal_multiscale_pool(p):
    bsz, s, _ = p.shape
    pg = p.reshape(bsz, s, POOL_GROUPS, POOL_GROUP_DIM)
    cs = jnp.cumsum(pg.astype(jnp.float32), axis=1)
    t = jnp.arange(s, dtype=jnp.float32)
    outs = []
    for g, w in enumerate(POOL_WINDOWS):
        csg = cs[:, :, g]
        lag = jnp.pad(csg[:, :s - w], ((0, 0), (w, 0), (0, 0)))
        cnt = jnp.minimum(t + 1.0, float(w))
        outs.append((csg - lag) / cnt[None, :, None])
    mean = jnp.stack(outs, axis=2).astype(p.dtype)
    return mean - pg

def second_inputs(seed: int = 0) -> dict:
    key = jax.random.key(seed)
    ks = jax.random.split(key, 16)
    f32 = jnp.float32
    d = D_MODEL

    def w(k, shape, fan_in, mult=1.0):
        return jax.random.normal(k, shape, f32) * (mult * fan_in ** -0.5)

    return {
        "x": jax.random.normal(ks[0], (BATCH, SEQ, d), f32),
        "c": jax.random.normal(ks[1], (BATCH, d), f32),
        "w_ada": w(ks[2], (DEPTH, d, N_MOD * d), d, 0.5),
        "b_ada": 0.01 * jax.random.normal(ks[3], (DEPTH, N_MOD * d), f32),
        "norm1": 1.0 + 0.02 * jax.random.normal(ks[4], (DEPTH, d), f32),
        "w_in": w(ks[5], (DEPTH, d, IN_COLS), d),
        "w_ret_o": w(ks[6], (DEPTH, RET_V, d), RET_V),
        "w_pool_grp": w(ks[7], (DEPTH, POOL_GROUPS, POOL_GROUP_DIM, POOL_GROUP_DIM), POOL_GROUP_DIM),
        "pool_scale": 1.0 + 0.1 * jax.random.normal(ks[8], (DEPTH, POOL_DIM), f32),
        "w_pool_o": w(ks[9], (DEPTH, POOL_DIM, d), POOL_DIM),
        "w_out": w(ks[10], (DEPTH, d, d), d),
        "norm2": 1.0 + 0.02 * jax.random.normal(ks[11], (DEPTH, d), f32),
        "w_ffn_in": w(ks[12], (DEPTH, d, 2 * D_FF_2), d),
        "w_ffn_out": w(ks[13], (DEPTH, D_FF_2, d), D_FF_2),
        "final_norm": 1.0 + 0.02 * jax.random.normal(ks[14], (d,), f32),
    }

def second_block(x, c, w_ada, b_ada, norm1, w_in, w_ret_o, w_pool_grp, pool_scale, w_pool_o,
              w_out, norm2, w_ffn_in, w_ffn_out, final_norm):
    bsz, s, _ = x.shape
    half = RET_QK_DIM // 2
    inv_freq = ROPE_BASE ** (-jnp.arange(half, dtype=jnp.float32) / half)
    ang = jnp.arange(s, dtype=jnp.float32)[:, None] * inv_freq[None, :]
    cos = jnp.cos(ang)[:, None, :].astype(x.dtype)
    sin = jnp.sin(ang)[:, None, :].astype(x.dtype)
    c_act = jax.nn.silu(c)

    for l in range(DEPTH):
        mod = c_act @ w_ada[l] + b_ada[l]
        sh1, sc1, g1, sh2, sc2, g2 = jnp.split(mod, N_MOD, axis=-1)

        h = modulate_2(rmsnorm(x, norm1[l]), sh1, sc1)
        proj = h @ w_in[l]
        q, k, v, g_sw, p_in, gates = jnp.split(proj, IN_SPLITS, axis=-1)
        q = rotary(q.reshape(bsz, s, RET_HEADS, RET_QK_DIM), cos, sin)
        k = rotary(k.reshape(bsz, s, RET_HEADS, RET_QK_DIM), cos, sin)
        v = v.reshape(bsz, s, RET_HEADS, RET_V_DIM)
        ret = head_rmsnorm(retention_chunkwise(q, k, v)).reshape(bsz, s, RET_V)
        ret_d = (jax.nn.silu(g_sw) * ret) @ w_ret_o[l]

        pooled = causal_multiscale_pool(p_in)
        pooled = jnp.einsum('bsgi,gio->bsgo', pooled, w_pool_grp[l]).reshape(bsz, s, POOL_DIM)
        pool_d = (pooled * pool_scale[l]) @ w_pool_o[l]

        a_ret, a_pool = jnp.split(gates, N_BRANCH, axis=-1)
        merged = jax.nn.sigmoid(a_ret) * ret_d + jax.nn.sigmoid(a_pool) * pool_d
        x = x + g1[:, None, :] * (merged @ w_out[l])

        h2 = modulate_2(rmsnorm(x, norm2[l]), sh2, sc2)
        gate, up = jnp.split(h2 @ w_ffn_in[l], 2, axis=-1)
        x = x + g2[:, None, :] * ((jax.nn.silu(gate) * up) @ w_ffn_out[l])

    return rmsnorm(x, final_norm)


def setup_inputs(seed=0):
    out = dict(first_inputs(seed))
    for name, value in second_inputs(seed + 1).items():
        if name != "x":
            out[name + "_2"] = value
    return out


def reference(
    x, c, positions, rel_bias, norm_g, w_mod, b_mod, w_ffn1_gu, w_ffn1_down, w_in, q_a_norm,
    kv_a_norm, w_uq, w_ukv, mla_q_norm, mla_k_norm, swa_q_norm, swa_k_norm, sinks, out_norm,
    w_out, w_ffn2_gu, w_ffn2_down, c_2, w_ada_2, b_ada_2, norm1_2, w_in_2, w_ret_o_2,
    w_pool_grp_2, pool_scale_2, w_pool_o_2, w_out_2, norm2_2, w_ffn_in_2, w_ffn_out_2,
    final_norm_2,
):
    x = first_block(
        x, c, positions, rel_bias, norm_g, w_mod, b_mod, w_ffn1_gu, w_ffn1_down, w_in, q_a_norm,
        kv_a_norm, w_uq, w_ukv, mla_q_norm, mla_k_norm, swa_q_norm, swa_k_norm, sinks, out_norm,
        w_out, w_ffn2_gu, w_ffn2_down,
    )
    return second_block(
        x, c_2, w_ada_2, b_ada_2, norm1_2, w_in_2, w_ret_o_2, w_pool_grp_2, pool_scale_2,
        w_pool_o_2, w_out_2, norm2_2, w_ffn_in_2, w_ffn_out_2, final_norm_2,
    )


_drawn_inputs = setup_inputs


def setup_inputs(seed=0):
    import zlib

    import numpy as np

    out = dict(_drawn_inputs(seed))
    spreads = {}
    factors = {'q_a_norm': 4.73,
     'mla_q_norm': 5.117,
     'mla_k_norm': 5.285,
     'swa_q_norm': 4.613,
     'swa_k_norm': 5.065,
     'sinks': 8.0,
     'b_ada_2': 4.198,
     'norm1_2': 8.0,
     'pool_scale_2': 3.045,
     'norm2_2': 7.736,
     'final_norm_2': 2.843}
    for name, (base, spread) in spreads.items():
        noise = np.random.default_rng([zlib.crc32(name.encode()), seed]).standard_normal(out[name].shape)
        drawn = base * np.exp(spread * noise) if base else spread * noise
        out[name] = __import__('jax').numpy.asarray(drawn.astype(out[name].dtype))
    for name, factor in factors.items():
        out[name] = (out[name] * factor).astype(out[name].dtype)
    return out
```

```python
from contextlib import ExitStack
import math

import numpy as np

import concourse.bass as bass
from concourse import mybir

F32 = mybir.dt.float32
F32R = mybir.dt.float32r
I32 = mybir.dt.int32
BF16 = mybir.dt.bfloat16
ALU = mybir.AluOpType
ACT = mybir.ActivationFunctionType
AX = mybir.AxisListType.X

P = 128
SEQ = 256
NT = SEQ // P
D = 1024
KD = D // P
DFF = 2816
DEPTH = 2
EPS = 1e-6

MH, MQK, MNOPE, MROPE, MV = 6, 96, 64, 32, 64
QL, KVL = 256, 128
WH, WKV, HD = 6, 2, 64
SH = 4
D_IN = QL + KVL + MROPE + (WH + 2 * WKV) * HD + 3 * SH * HD
O_CKV, O_KPE = QL, QL + KVL
O_WQ = O_KPE + MROPE
O_WK = O_WQ + WH * HD
O_WV = O_WK + WKV * HD
O_SB = O_WV + WKV * HD
NBUCKET, MAXDIST = 32, 128
MASKED = -1e30

RH, RQK, RV = 8, 64, 128
POOLW = (2, 4, 8, 16)
D_IN2 = 2 * RH * RQK + 2 * RH * RV + 512 + 2 * D

SLOT = 1024
RING = 6
STRIPS = DFF // 256
UNITS_FFN = 4 * STRIPS + 2 * STRIPS
UNITS_MID1 = 16 + 2 + 2 + 8
UNITS_MID2 = 44 + 8 + 2 + 4 + 8
MOD_RING = 4

MOD_FIRST = [0, 9, 18, 24]
N_MOD = 30

MOD_START = [(("w_mod", 0), 0, 2)]
MOD_BESIDE = [[(("w_mod", 0), 2, 8)],
              [(("w_mod", 0), 8, 9), (("w_mod", 1), 0, 4)],
              [(("w_mod", 1), 4, 9)],
              [(("w_ada_2", 0), 0, 5)],
              [(("w_ada_2", 0), 5, 6), (("w_ada_2", 1), 0, 5)],
              [(("w_ada_2", 1), 5, 6)]]
MOD_PLAN = [(2, 3), (None, 8), (None, 13), (None, 18), (23, 24), (29, None)]

C_ID, C_TRI, C_ONES = 0, 128, 256
C_MASKC, C_MASKW, C_MASKS = 384, 768, 1152
C_MASKA = 1536
C_FREQ = 1920
C_ROPE2 = C_FREQ + 16
C_THR = C_ROPE2 + 4 * 32
C_END = C_THR + 1
C2_DECAY, C2_POOL = 0, RH * 256
C2_END = C2_POOL + 4 * 384

A_T = 0
A_S = 3072
A_X = 4608
A_MOD = A_X + 2048
A_BIAS = A_MOD + 4096
A_PROJ = A_X
A_QK = A_PROJ + NT * D_IN
A_KV = A_QK + NT * 2 * MH * MQK
A_T2 = A_KV + NT * MH * 128
A_KDUP = A_T2 + 9 * 256
A_END1 = A_KDUP + 512
A_QK2 = A_X
A_V2 = A_QK2 + 2048
A_RET = A_V2 + 2048
A_P2 = A_RET + 2048
A_C2 = A_P2 + 1024
A_END = max(A_END1, A_C2 + C2_END)


def bucket_thresholds():
    n = np.arange(0, MAXDIST + 1)
    half = NBUCKET // 2
    large = half + (np.log(np.maximum(n, 1).astype(np.float32) / half) / math.log(MAXDIST / half)
                    * (NBUCKET - half)).astype(np.int32)
    b = np.where(n < half, n, np.minimum(large, NBUCKET - 1))
    return [int(np.argmax(b >= k)) for k in range(NBUCKET)]


def constants():
    c = np.zeros((P, C_END), np.float32)
    i = np.arange(P)
    row, col = i[:, None], i[None, :]
    c[:, C_ID:C_ID + P] = row == col
    c[:, C_TRI:C_TRI + P] = row >= col
    c[:, C_ONES:C_ONES + P] = 1.0
    causal = np.where(col <= row, 0.0, MASKED)
    c[:, C_MASKC:C_MASKC + P] = causal
    c[:, C_MASKC + 2 * P:C_MASKC + 3 * P] = causal
    c[:, C_MASKW:C_MASKW + P] = causal
    c[:, C_MASKW + P:C_MASKW + 2 * P] = np.where(col > row, 0.0, MASKED)
    c[:, C_MASKW + 2 * P:C_MASKW + 3 * P] = causal
    c[:, C_MASKS:C_MASKS + P] = row < col
    c[:, C_MASKS + P:C_MASKS + 2 * P] = 1.0
    c[:, C_MASKS + 2 * P:C_MASKS + 3 * P] = row < col
    c[:, C_MASKA:C_MASKA + 384] = np.where(c[:, C_MASKS:C_MASKS + 384] > 0, 0.0, MASKED)
    half = MROPE // 2
    c[:, C_FREQ:C_FREQ + half] = np.float32(10000.0) ** (-np.arange(half, dtype=np.float32) / np.float32(half))
    thr = bucket_thresholds()
    thr[0] = -2.0 ** 30
    c[:, C_THR] = np.tile(np.array(thr, np.float32), P // NBUCKET)
    half = RQK // 2
    f = np.float32(10000.0) ** (-np.arange(half, dtype=np.float32) / np.float32(half))
    ang = (np.arange(SEQ, dtype=np.float32)[:, None] * f[None, :]).astype(np.float64).reshape(NT, P, half)
    c[:, C_ROPE2:C_ROPE2 + 64] = np.cos(ang).transpose(1, 0, 2).reshape(P, 64)
    c[:, C_ROPE2 + 64:C_ROPE2 + 128] = np.sin(ang).transpose(1, 0, 2).reshape(P, 64)

    c2 = np.zeros((P, C2_END), np.float32)
    q = np.arange(SEQ)[None, :]
    for h in range(RH):
        g = np.log1p(-(2.0 ** (-5.0 - h)))
        d = q - row
        c2[:, C2_DECAY + 256 * h:C2_DECAY + 256 * (h + 1)] = np.where(d >= 0, np.exp(g * np.maximum(d, 0)), 0.0) * RQK ** -0.5
    for n, w in enumerate(POOLW):
        t = np.arange(SEQ)
        m = ((t[:, None] <= t[None, :]) & (t[None, :] - t[:, None] < w)) / np.minimum(t + 1.0, w)[None, :] - np.eye(SEQ)
        c2[:, C2_POOL + 384 * n:C2_POOL + 384 * n + 256] = m[0:P, :]
        c2[:, C2_POOL + 384 * n + 256:C2_POOL + 384 * (n + 1)] = m[P:, P:]
    return c, c2


V_C1, V_C2 = 240, 248
V_NORMG = 256
V_N1, V_N2, V_ON = V_NORMG + 48, V_NORMG + 64, V_NORMG + 80
V_QA, V_KVA, V_PS = V_NORMG + 96, V_NORMG + 100, V_NORMG + 102
V_ROWS2 = V_PS + 8 - 256
TRB = (6, 7, 4, 5)


def need(eng, sem, value):
    if not isinstance(value, int) or value > 0:
        eng.wait_ge(sem, value)


def build(nc, A, out):
    with ExitStack() as ctx:
        def sb(name, shape, dt=F32):
            return ctx.enter_context(nc.sbuf_tensor(name, shape, dt))

        sems = {}

        def S(name):
            if name not in sems:
                sems[name] = ctx.enter_context(nc.semaphore(name))
            return sems[name]

        raw = sb("weights_raw", [P, RING, SLOT])
        whi = sb("weights_hi", [P, RING, SLOT], F32R)
        wlo = sb("weights_lo", [P, RING, SLOT], F32R)
        hhi = sb("hT_hi", [P, KD, SEQ], F32R)
        hlo = sb("hT_lo", [P, KD, SEQ], F32R)
        ahi = sb("actT_hi", [P, 2, SEQ], F32R)
        alo = sb("actT_lo", [P, 2, SEQ], F32R)
        x = sb("x", [P, NT, D])
        con = sb("con", [P, C_END])
        bias = sb("window_bias", [P, WH, 384])
        modacc = sb("mod_acc", [P, D])
        modc = sb("mod_cols", [P, 8 * N_MOD])
        vec = sb("vectors", [P, 3 * P])
        silc = sb("silu_cond", [P, 16])
        gq96 = sb("gain_mla", [P, 2, MQK])
        gw64 = sb("gain_window", [P, 2, HD])
        sink = sb("sinks_row", [P, WH])
        rope1 = sb("rope_first", [P, 2, NT, 16])
        stat = sb("stat", [P, 96])
        sclA = sb("scale_cols", [P, 8])
        nmax = sb("neg_max", [P, 24])
        rsum = sb("row_sums", [P, 24])
        esink = sb("sink_exp_t", [P, 12])[:, :]
        latg = sb("latent_gains", [P, 3])
        zero_hi = sb("zero", [P, P], F32R)
        arena = sb("arena", [P, A_END])
        bank = [ctx.enter_context(nc.psum_tensor(f"bank{i}", [P, 512], F32)) for i in range(8)]
        GB = (4, 5)
        ATB, MB = 6, 7

        ident = con[:, C_ID:C_ID + P]
        tri = con[:, C_TRI:C_TRI + P]
        ones = con[:, C_ONES:C_ONES + P]
        ones_col = con[:, C_ONES:C_ONES + 1]

        def ar(off, n):
            return arena[:, off:off + n]

        hf = ar(A_T, 1024).rearrange("p (r n) -> p r n", r=2)
        act_t = ar(A_T + 1024, 512).rearrange("p (t n) -> p t n", t=NT)
        sg_t = ar(A_T + 1536, 512).rearrange("p (t n) -> p t n", t=NT)
        gate_b = ar(A_S, 1024)
        modw = ar(A_MOD, MOD_RING * D).rearrange("p (r n) -> p r n", r=MOD_RING)
        xn = ar(A_X, 2048).rearrange("p (t n) -> p t n", t=NT)
        pos_i = ar(A_BIAS, 2).bitcast(I32)
        pos_q = ar(A_BIAS + 2, SEQ).bitcast(I32)
        pos_k = ar(A_BIAS + 258, 64).bitcast(I32).rearrange("p (t n) -> p t n", t=NT)
        relb, relb1 = ar(A_BIAS + 322, WH), ar(A_BIAS + 328, WH)
        posf_i, posf_q = ar(A_BIAS + 334, 2), ar(A_BIAS + 336, SEQ)
        posf_k = ar(A_BIAS + 592, 64).rearrange("p (t n) -> p t n", t=NT)
        bstep, ang = ar(A_BIAS + 656, WH), ar(A_BIAS + 662, 32).rearrange("p (t n) -> p t n", t=NT)
        bparts = ar(A_BIAS + 760, 10).bitcast(BF16)[:, 0:3 * WH].rearrange("p (q h) -> p q h", q=3)
        turns = ar(A_BIAS + 694, 64).rearrange("p (a t n) -> p a t n", a=2, t=NT)
        reached = ar(A_T, 1024).bitcast(BF16).rearrange("p (k q) -> p k q", k=16)
        proj = ar(A_PROJ, NT * D_IN).rearrange("p (t n) -> p t n", t=NT)
        qk1 = ar(A_QK, NT * 12 * MQK).rearrange("p (t h n) -> p t h n", t=NT, h=12)
        mix = ar(A_QK, 2048).rearrange("p (t n) -> p t n", t=NT)
        kv = ar(A_KV, NT * MH * 128).rearrange("p (t h n) -> p t h n", t=NT, h=MH)
        mlaT = ar(A_T, 12 * SEQ).rearrange("p (h n) -> p h n", h=12)
        pairT = ar(A_T2, 9 * SEQ).rearrange("p (h n) -> p h n", h=9)
        kdup = ar(A_KDUP, NT * 256).rearrange("p (t k r n) -> p t k r n", t=NT, k=WKV, r=2)
        lat = ar(A_T2, NT * 384).rearrange("p (t n) -> p t n", t=NT)
        sc_t = ar(A_S, 768).rearrange("p (r n) -> p r n", r=2)
        pt_t = ar(A_S + 768, 768).rearrange("p (r n) -> p r n", r=2)
        qk2 = ar(A_QK2, 2048).rearrange("p (t n) -> p t n", t=NT)
        v2 = ar(A_V2, 2048).rearrange("p (t n) -> p t n", t=NT)
        gates = ar(A_QK2, 4096).rearrange("p (t n) -> p t n", t=NT)
        ret = ar(A_RET, 2048).rearrange("p (t n) -> p t n", t=NT)
        p2 = ar(A_P2, 1024).rearrange("p (t n) -> p t n", t=NT)
        qkT2 = ar(A_T, 2048).rearrange("p (h n) -> p h n", h=8)
        con2 = ar(A_C2, C2_END)

        n = RING
        phases = []
        ffn = dict(first=[], second=[])
        t_index = 0
        for blk in range(2):
            for l in range(DEPTH):
                m0 = MOD_FIRST[2 * blk + l]
                if blk == 0:
                    phases.append(("ffn", n, dict(f=2 * l, gu=A["w_ffn1_gu"][l], down=A["w_ffn1_down"][l], g=V_NORMG + 24 * l, mod=m0, half=0.5)))
                    n += UNITS_FFN
                    phases.append(("mid1", n, dict(l=l, g=V_NORMG + 24 * l + 8, mod=m0 + 3)))
                    n += UNITS_MID1
                    phases.append(("ffn", n, dict(f=2 * l + 1, gu=A["w_ffn2_gu"][l], down=A["w_ffn2_down"][l], g=V_NORMG + 24 * l + 16, mod=m0 + 6, half=0.5)))
                    n += UNITS_FFN
                else:
                    phases.append(("mid2", n, dict(l=l, g=V_N1 + 8 * l, mod=m0)))
                    n += UNITS_MID2
                    phases.append(("ffn", n, dict(f=4 + l, gu=A["w_ffn_in_2"][l], down=A["w_ffn_out_2"][l], g=V_N2 + 8 * l, mod=m0 + 3, half=1.0)))
                    n += UNITS_FFN

        def copy_qk(copy, g):
            if g < 6:
                return copy(mlaT[0:MQK, 2 * g:2 * g + 2, :].rearrange("p h n -> p (h n)"), bank[g % 4][0:MQK, :])
            k = min(2, 9 - 2 * (g - 6))
            return copy(pairT[:, 2 * (g - 6):2 * (g - 6) + k, :].rearrange("p h n -> p (h n)"), bank[g % 4][:, 0:256 * k])

        block = ctx.enter_context(nc.Block())

        @block.sync
        def _(sp):
            sp.dma_start(con[:, :], A["con"]).then_inc(S("const_loaded"), 16)
            sp.dma_start(x[:, :, :], A["x"][0].rearrange("(t p) n -> p t n", p=P)).then_inc(S("x_loaded"), 16)

            def gu_pair(slot, wait, w, k0, col):
                sp.wait_ge(S("lo_done"), wait)
                for half in range(2):
                    src = w.rearrange("(k p) (s n) -> p k s n", p=P, s=2)[:, k0:k0 + 4, half, bass.ds(col, 256)]
                    dst = raw[:, slot:slot + 2, :].rearrange("p u (k s n) -> p (u k) s n", k=2, s=2)[:, :, half, :]
                    sp.dma_start(dst, src).then_inc(S(f"w_loaded{slot // 2}"), 16)

            def rows_pair(slot, wait, w, k0):
                sp.wait_ge(S("lo_done"), wait)
                for u in range(2):
                    src = w[bass.ds(k0 + u * P, P), :]
                    sp.dma_start(raw[:, slot + u, :], src).then_inc(S(f"w_loaded{slot // 2}"), 16)

            def gu_strip(n0, i6, w, col):
                for h in range(2):
                    gu_pair((n0 + 2 * h) % RING, i6 + n0 + 2 * h - RING + 2, w, 4 * h, col)

            def strip_pairs(n0, w, k_chunks, col, width):
                wv = w.rearrange("(k p) n -> p k n", p=P)
                for u in range(k_chunks // 2):
                    nn = n0 + u
                    if u % 2 == 0:
                        sp.wait_ge(S("lo_done"), nn - RING + 2)
                    dst = raw[:, nn % RING, 0:2 * width].rearrange("p (k n) -> p k n", k=2)
                    sp.dma_start(dst, wv[:, 2 * u:2 * u + 2, col:col + width]).then_inc(S(f"w_loaded{nn % RING // 2}"), 16)

            for kind, n0, a in phases:
                if kind == "ffn":
                    gu_strip(n0, 0, a["gu"], 0)
                    with sp.Fori(0, STRIPS // 2) as i:
                        for s in range(2):
                            c = n0 + 4 + 6 * s
                            gu_strip(c, 12 * i, a["gu"], 512 * i + 256 * (s + 1))
                            rows_pair((c + 4) % RING, 12 * i + c + 4 - RING + 2, a["down"], 512 * i + 256 * s)
                    c = n0 + 4 + 12 * (STRIPS // 2)
                    rows_pair(c % RING, c - RING + 2, a["down"], 256 * (STRIPS - 1))
                elif kind == "mid1":
                    l = a["l"]
                    for s in range(3):
                        strip_pairs(n0 + 4 * s, A["w_in"][l], KD, 512 * s, 512)
                    strip_pairs(n0 + 12, A["w_in"][l], KD, 1536, D_IN - 1536)
                    nn = n0 + 16
                    sp.wait_ge(S("lo_done"), nn - RING + 2)
                    wv = A["w_uq"][l].rearrange("(k p) n -> p k n", p=P)
                    for u in range(2):
                        dst = raw[:, (nn + u) % RING, 0:576].rearrange("p (k n) -> p k n", k=2)
                        sp.dma_start(dst, wv[:, :, 288 * u:288 * (u + 1)]).then_inc(S(f"w_loaded{nn % RING // 2}"), 16)
                    nn = n0 + 18
                    sp.wait_ge(S("lo_done"), nn - RING + 2)
                    for u in range(2):
                        sp.dma_start(raw[:, (nn + u) % RING, 0:384], A["w_ukv"][l][:, 384 * u:384 * (u + 1)])\
                            .then_inc(S(f"w_loaded{nn % RING // 2}"), 16)
                    for k in range(0, KD, 2):
                        nn = n0 + 20 + k
                        rows_pair(nn % RING, nn - RING + 2, A["w_out"][l], P * k)
                else:
                    l = a["l"]
                    for s in range(11):
                        strip_pairs(n0 + 4 * s, A["w_in_2"][l], KD, 512 * s, 512)
                    for k in range(0, KD, 2):
                        nn = n0 + 44 + k
                        rows_pair(nn % RING, nn - RING + 2, A["w_ret_o_2"][l], P * k)
                    nn = n0 + 52
                    sp.wait_ge(S("lo_done"), nn - RING + 2)
                    for u in range(2):
                        dst = raw[:, (nn + u) % RING, 0:256].rearrange("p (g n) -> p g n", g=2)
                        sp.dma_start(dst, A["w_pool_grp_2"][l, 2 * u:2 * u + 2].rearrange("g p n -> p g n"))\
                            .then_inc(S(f"w_loaded{nn % RING // 2}"), 16)
                    for k in range(0, 4, 2):
                        nn = n0 + 54 + k
                        rows_pair(nn % RING, nn - RING + 2, A["w_pool_o_2"][l], P * k)
                    for k in range(0, KD, 2):
                        nn = n0 + 58 + k
                        rows_pair(nn % RING, nn - RING + 2, A["w_out_2"][l], P * k)
            sp.wait_ge(S("x_done"), len(phases) + 1)
            sp.dma_start(gate_b, A["final_norm_2"].partition_broadcast(P)).then_inc(S("final_gain"), 16)
            sp.wait_ge(S("out_ready"), 1)
            sp.dma_start(out[0].rearrange("(t p) n -> p t n", p=P), xn).then_inc(S("out_stored"), 16)
            sp.wait_ge(S("out_stored"), 16)

        @block.gpsimd
        def _(pool):
            rows = ar(A_X, 3 * P).rearrange("p (t n) -> p t n", t=3)

            def vec_rows(tile, at, src, r):
                pool.dma_start(rows[at:at + r, tile, :], src).then_inc(S("rows_loaded"), 16)

            vec_rows(0, 0, A["b_mod"][0].rearrange("(r n) -> r n", n=P), 72)
            vec_rows(0, 72, A["b_mod"][1].rearrange("(r n) -> r n", n=P)[0:56], 56)
            vec_rows(1, 0, A["b_mod"][1].rearrange("(r n) -> r n", n=P)[56:72], 16)
            vec_rows(1, 16, A["b_ada_2"].rearrange("l (r n) -> (l r) n", n=P), 96)
            vec_rows(1, V_C1 - P, A["c"].rearrange("a (r n) -> (a r) n", n=P), 8)
            vec_rows(1, V_C2 - P, A["c_2"].rearrange("a (r n) -> (a r) n", n=P), 8)
            vec_rows(2, 0, A["norm_g"].rearrange("l i (r n) -> (l i r) n", n=P), 48)
            vec_rows(2, V_N1 - 256, A["norm1_2"].rearrange("l (r n) -> (l r) n", n=P), 16)
            vec_rows(2, V_N2 - 256, A["norm2_2"].rearrange("l (r n) -> (l r) n", n=P), 16)
            vec_rows(2, V_ON - 256, A["out_norm"].rearrange("l (r n) -> (l r) n", n=P), 16)
            vec_rows(2, V_QA - 256, A["q_a_norm"].rearrange("l (r n) -> (l r) n", n=P), 4)
            vec_rows(2, V_KVA - 256, A["kv_a_norm"].rearrange("l (r n) -> (l r) n", n=P), 2)
            vec_rows(2, V_PS - 256, A["pool_scale_2"].rearrange("l (r n) -> (l r) n", n=P), 8)

            def mod_load(w, k, col, slot, wait):
                need(pool, S("mod_used"), wait)
                pool.dma_start(modw[:, slot, :], w[k * P:(k + 1) * P, bass.ds(col, D)]).then_inc(S(f"mod_loaded{slot}"), 16)

            m = 0
            f = 0
            for k, (kind, _, _) in enumerate([("start", 0, 0)] + phases):
                if kind == "mid1" or kind == "mid2":
                    continue
                need(pool, S("x_done"), k if k > 1 else 0)
                for w, c0, c1 in (MOD_START if kind == "start" else MOD_BESIDE[f]):
                    if m == 0:
                        for c in range(c0, c1):
                            for q in range(KD):
                                mod_load(A[w[0]][w[1]], q, D * c, q % MOD_RING, 8 * c + q - MOD_RING + 1)
                    elif c1 - c0 == 1:
                        for q in range(KD):
                            mod_load(A[w[0]][w[1]], q, D * c0, q % MOD_RING, 8 * m + q - MOD_RING + 1)
                    else:
                        with pool.Fori(0, c1 - c0) as c:
                            for q in range(KD):
                                mod_load(A[w[0]][w[1]], q, D * c + D * c0, q % MOD_RING, 8 * c + 8 * m + q - MOD_RING + 1)
                    m += c1 - c0
                f += kind == "ffn"

        @block.scalar
        def _(act):
            seq = [0]

            def then(ins):
                seq[0] += 1
                ins.then_inc(S("act_step"), 1)
                act.wait_ge(S("act_step"), seq[0])

            def hi(slot, width, loaded, free):
                act.wait_ge(S(f"w_loaded{slot // 2}"), loaded)
                act.wait_ge(S("mm_done"), free)
                nc.scalar.activation(whi[:, slot, 0:width], raw[:, slot, 0:width], ACT.Copy).then_inc(S("hi_done"), 1)

            def hi_static(n, width):
                hi(n % RING, width, 32 * (n // RING), n - RING + 1)

            act.dma_start(gq96[:, 0, :], A["mla_q_norm"][0].partition_broadcast(P)).then_inc(S("gains_loaded"), 16)
            act.dma_start(gq96[:, 1, :], A["mla_k_norm"][0].partition_broadcast(P)).then_inc(S("gains_loaded"), 16)
            act.dma_start(gw64[:, 0, :], A["swa_q_norm"][0].partition_broadcast(P)).then_inc(S("gains_loaded"), 16)
            act.dma_start(gw64[:, 1, :], A["swa_k_norm"][0].partition_broadcast(P)).then_inc(S("gains_loaded"), 16)
            act.dma_start(sink[:, :], A["sinks"][0].partition_broadcast(P)).then_inc(S("gains_loaded"), 16)
            act.dma_start(pos_i, A["positions"][0].rearrange("(t p) -> p t", p=P), allow_slow_non_contiguous=True).then_inc(S("pos_loaded"), 16)
            act.dma_start(pos_q, A["positions"][0].partition_broadcast(P)).then_inc(S("pos_loaded"), 16)
            act.wait_ge(S("zero_ready"), 2)
            for g in range(4):
                r = slice(NBUCKET * g, NBUCKET * (g + 1))
                act.dma_start(pos_k[r], A["positions"][0].rearrange("(t g n) -> g t n", t=NT, g=4)[g].partition_broadcast(NBUCKET)).then_inc(S("pos_loaded"), 16)
                act.dma_start(relb[r], A["rel_bias"]).then_inc(S("pos_loaded"), 16)
                act.dma_start(relb1[NBUCKET * g + 1:NBUCKET * (g + 1)], A["rel_bias"][0:NBUCKET - 1]).then_inc(S("pos_loaded"), 16)
            act.wait_ge(S("vec_ready"), 1)
            nc.scalar.activation(silc[:, 0:8], vec[:, V_C1:V_C1 + 8], ACT.Silu)
            nc.scalar.activation(silc[:, 8:16], vec[:, V_C2:V_C2 + 8], ACT.Silu).then_inc(S("cond_ready"), 1)
            act.wait_ge(S("angles_ready"), 1)
            r1 = rope1[:, :, :, :].rearrange("p a t n -> p (a t n)")
            nc.scalar.activation(r1, r1, ACT.Sin).then_inc(S("rope_ready"), 1)

            tr = [0]

            def norm_stage(k):
                act.wait_ge(S("x_done"), k)
                for t in range(NT):
                    ins = nc.scalar.activation(xn[:, t, :], x[:, t, :], ACT.Square, accum_out=stat[:, t:t + 1])
                ins.then_inc(S("ss_ready"), 1)
                act.wait_ge(S("ms_ready"), k)
                nc.scalar.activation(stat[:, 2:4], stat[:, 2:4], ACT.Sqrt).then_inc(S("rms_ready"), 1)
                act.wait_ge(S("rstd_ready"), k)
                nc.scalar.activation(xn[:, 0, :], x[:, 0, :], ACT.Copy, scale=stat[:, 4:5]).then_inc(S("xn0_ready"), 1)

            def split_groups(dst0, chunks):
                for c in range(0, chunks, 2):
                    w = min(2, chunks - c) * SEQ
                    act.wait_ge(S("hf_ready"), tr[0] + 1)
                    nc.scalar.activation(hhi[:, dst0 + c:dst0 + c + w // SEQ, :].rearrange("p k n -> p (k n)"),
                                         hf[:, tr[0] % 2, 0:w], ACT.Copy).then_inc(S("hhi_done"), 1)
                    tr[0] += 1

            ffn_n, x_n, o_n, mid1_n, mid2_n = [0], [0], [0], [0], [0]

            def gate_rows(half):
                x_n[0] += 1
                act.wait_ge(S("gate_rows"), x_n[0])
                for h in range(2):
                    ins = nc.scalar.activation(gate_b[:, 512 * h:512 * (h + 1)], bank[6 + h][:, :], ACT.Copy, scale=half)
                ins.then_inc(S("gate_ready"), 1)

            def rms_sqrt(name, ap):
                cnt[name] = cnt.get(name, 0) + 1
                act.wait_ge(S(name), cnt[name])
                nc.scalar.activation(ap, ap, ACT.Sqrt).then_inc(S(name + "_root"), 1)

            cnt = {}

            for kind, n0, a in phases:
                o_n[0] += 1
                norm_stage(o_n[0])
                split_groups(0, KD)
                if kind == "ffn":
                    f = ffn_n[0]
                    ffn_n[0] += 1

                    def silu(j, end):
                        act.wait_ge(S("mm_done"), end)
                        need(act, S("act_ready"), STRIPS * f + j)
                        for t in range(NT):
                            nc.scalar.activation(sg_t[:, t, :], bank[GB[t]][:, 0:256], ACT.Silu).then_inc(S("silu_done"), 1)

                    def act_hi(j, used):
                        act.wait_ge(S("actT_ready"), STRIPS * f + j + 1)
                        act.wait_ge(S("mm_done"), used)
                        nc.scalar.activation(ahi[:, :, :].rearrange("p k n -> p (k n)"), bank[ATB][:, :], ACT.Copy)\
                            .then_inc(S("ahi_done"), 1)

                    def units(c, i, lo_, hi_):
                        for u in range(lo_, hi_):
                            m = c + u
                            hi(m % RING, SLOT, 64 * i + 32 * (m // RING), 12 * i + m - RING + 1)

                    units(n0, 0, 0, 4)
                    silu(0, n0 + 4)
                    with act.Fori(0, STRIPS // 2) as i:
                        for s in range(2):
                            c = n0 + 4 + 6 * s
                            units(c, i, 0, 4)
                            act_hi(2 * i + s, 12 * i + c)
                            units(c, i, 4, 6)
                            silu(2 * i + s + 1, 12 * i + c + 4)
                    c = n0 + 4 + 12 * (STRIPS // 2)
                    act_hi(STRIPS - 1, c)
                    units(c, 0, 0, 2)
                    gate_rows(a["half"])
                elif kind == "mid1":
                    l = a["l"]
                    m = mid1_n[0]
                    mid1_n[0] += 1
                    if l > 0:
                        act.wait_ge(S("heads_normed"), l)
                        act.wait_ge(S("mix_ready"), l)
                        for dst, src in ((gq96[:, 0, :], "mla_q_norm"), (gq96[:, 1, :], "mla_k_norm"),
                                         (gw64[:, 0, :], "swa_q_norm"), (gw64[:, 1, :], "swa_k_norm"), (sink[:, :], "sinks")):
                            act.dma_start(dst, A[src][l].partition_broadcast(P)).then_inc(S("gains_loaded"), 16)
                    widths = [512, 512, 512, D_IN - 1536]
                    for s in range(4):
                        for u in range(4):
                            hi_static(n0 + 4 * s + u, 2 * widths[s])
                        if s >= 1:
                            act.wait_ge(S("mm_done"), n0 + 4 * s)
                            nc.scalar.activation(proj[:, 0, 512 * (s - 1):512 * s], bank[2 * (s - 1)][:, :], ACT.Copy).then_inc(S("strip_copied0"), 1)
                    act.wait_ge(S("mm_done"), n0 + 16)
                    nc.scalar.activation(proj[:, 0, 1536:D_IN], bank[6][:, 0:D_IN - 1536], ACT.Copy).then_inc(S("strip_copied0"), 1)
                    act.wait_ge(S("strip_copied1"), 4 * m + 4)
                    act.wait_ge(S("strip_copied0"), 4 * m + 4)
                    sq = ar(A_QK, NT * 928).rearrange("p (t n) -> p t n", t=NT)
                    nc.scalar.activation(sq, proj[:, :, 0:928], ACT.Square).then_inc(S("sq_ready"), 1)
                    rms_sqrt("lat_ms", stat[:, 8:28])
                    split_groups(0, 3)
                    hi_static(n0 + 16, 576)
                    hi_static(n0 + 17, 576)
                    hi_static(n0 + 18, 384)
                    hi_static(n0 + 19, 384)
                    act.wait_ge(S("mm_done"), n0 + 20)
                    for u in range(2):
                        nc.scalar.activation(qk1[:, 0, 3 * u:3 * u + 3, :].rearrange("p h n -> p (h n)"), bank[2 * u][:, 0:288], ACT.Copy)
                        ins = nc.scalar.activation(kv[:, 0, 3 * u:3 * u + 3, :].rearrange("p h n -> p (h n)"), bank[4 + 2 * u][:, 0:384], ACT.Copy)
                    ins.then_inc(S("up_copied0"), 1)
                    act.wait_ge(S("up_copied1"), m + 1)
                    act.wait_ge(S("up_copied0"), m + 1)
                    sqq = ar(A_T, NT * 576).rearrange("p (t h n) -> p t h n", t=NT, h=MH)
                    sqk = ar(A_T + NT * 576, NT * 384).rearrange("p (t h n) -> p t h n", t=NT, h=MH)
                    for t in range(NT):
                        nc.scalar.activation(sqq[:, t], qk1[:, t, 0:MH, :], ACT.Square)
                        ins = nc.scalar.activation(sqk[:, t], kv[:, t, :, 0:64], ACT.Square)
                    ins.then_inc(S("sqh_ready"), 1)
                    rms_sqrt("head_ms", stat[:, 32:56])
                    for g in range(1, 11, 2):
                        act.wait_ge(S("qkT_ready"), 11 * m + g + 1)
                        copy_qk(nc.scalar.copy, g).then_inc(S("qkT_copied_act"), 1)
                    for h in range(12):
                        k = 12 * m + h
                        act.wait_ge(S("max_ready"), k + 1)
                        r = h % 2
                        for b, (c0, c1) in enumerate(((0, P), (P, 3 * P))):
                            ins = nc.scalar.activation(sc_t[:, r, c0:c1], sc_t[:, r, c0:c1], ACT.Exp,
                                                       bias=nmax[:, 2 * h + b:2 * h + b + 1], accum_out=rsum[:, 2 * h + b:2 * h + b + 1])
                        ins.then_inc(S("probs_ready"), 1)
                        if h >= 1:
                            act.wait_ge(S("probsT_ready"), k)
                            if h >= 3:
                                act.wait_ge(S("pv_done"), 16 * m + h - 2)
                            nc.scalar.activation(pt_t[:, (h - 1) % 2, :], bank[2 + (h - 1) % 2][:, 0:384], ACT.Copy).then_inc(S("pt_copied"), 1)
                    k = 12 * m + 12
                    act.wait_ge(S("probsT_ready"), k)
                    act.wait_ge(S("pv_done"), 16 * m + 10)
                    nc.scalar.activation(pt_t[:, 1, :], bank[3][:, 0:384], ACT.Copy).then_inc(S("pt_copied"), 1)
                    act.wait_ge(S("sink_diff"), m + 1)
                    nc.scalar.activation(esink, esink, ACT.Exp).then_inc(S("sink_exp"), 1)
                    for h in range(SH):
                        k = SH * m + h
                        r = h % 2
                        act.wait_ge(S("absz_ready"), k + 1)
                        then(nc.scalar.activation(pt_t[:, r, :], pt_t[:, r, :], ACT.Exp, scale=-1.0))
                        nc.scalar.activation(pt_t[:, r, :], pt_t[:, r, :], ACT.Ln, bias=1.0).then_inc(S("ln_ready"), 1)
                        act.wait_ge(S("zs_ready"), k + 1)
                        nc.scalar.activation(pt_t[:, r, :], sc_t[:, r, :], ACT.Exp).then_inc(S("sb_probs"), 1)
                    act.wait_ge(S("heads_out"), m + 1)
                    sqm = ar(A_PROJ, 2048).rearrange("p (t n) -> p t n", t=NT)
                    nc.scalar.activation(sqm, mix, ACT.Square).then_inc(S("sqm_ready"), 1)
                    rms_sqrt("mix_ms", stat[:, 8:14])
                    split_groups(0, KD)
                    for u in range(8):
                        hi_static(n0 + 20 + u, SLOT)
                    gate_rows(1.0)
                else:
                    m = mid2_n[0]
                    mid2_n[0] += 1

                    def strip(s):
                        act.wait_ge(S("mm_done"), n0 + 4 * s + 4)
                        b = bank[2 * (s % 3)]
                        if s in (4, 5):
                            for t in range(NT):
                                ins = nc.scalar.activation(ret[:, t, 512 * (s - 4):512 * (s - 3)], bank[2 * (s % 3) + t][:, :], ACT.Silu)
                            ins.then_inc(S("strip2_copied0"), 1)
                        elif s >= 7:
                            if s == 7:
                                act.wait_ge(S("ret_pv"), RH * (m + 1))
                            for t in range(NT):
                                ins = nc.scalar.activation(gates[:, t, 512 * (s - 7):512 * (s - 6)], bank[2 * (s % 3) + t][:, :], ACT.Sigmoid)
                            ins.then_inc(S("strip2_copied0"), 1)
                        else:
                            dst = {0: qk2[:, 0, 0:512], 1: qk2[:, 0, 512:1024], 2: v2[:, 0, 0:512], 3: v2[:, 0, 512:1024], 6: p2[:, 0, :]}[s]
                            nc.scalar.activation(dst, b[:, :], ACT.Copy).then_inc(S("strip2_copied0"), 1)

                    def split_strip(s):
                        for u in range(4):
                            hi_static(n0 + 4 * s + u, SLOT)

                    if m == 0:
                        act.dma_start(con2, A["con2"]).then_inc(S("const2_loaded"), 16)
                    for s in range(7):
                        split_strip(s)
                        if s >= 1:
                            strip(s - 1)
                        if s == 4:
                            for g in (1, 3):
                                act.wait_ge(S("qkT2_ready"), 4 * m + g + 1)
                                nc.scalar.activation(qkT2[:, 2 * g:2 * g + 2, :].rearrange("p h n -> p (h n)"), bank[6 + g % 2][:, :], ACT.Copy)\
                                    .then_inc(S("qkT2_copied_act"), 1)
                    strip(6)
                    act.wait_ge(S("ret_pv"), RH * (m + 1))
                    sqr = ar(A_T, 2048).rearrange("p (t n) -> p t n", t=NT)
                    for t in range(NT):
                        for hh in range(2):
                            ins = nc.scalar.activation(sqr[:, t, 512 * hh:512 * (hh + 1)], bank[2 * t + hh][:, :], ACT.Square)
                    ins.then_inc(S("sqr_ready"), 1)
                    rms_sqrt("ret_ms", stat[:, 8:24])
                    for s in range(7, 11):
                        split_strip(s)
                        if s >= 8:
                            strip(s - 1)
                    strip(10)
                    split_groups(0, KD)
                    for u in range(8):
                        hi_static(n0 + 44 + u, SLOT)
                    act.wait_ge(S("mm_done"), n0 + 52)
                    for g in range(2):
                        act.wait_ge(S("pool_ready"), 2 * m + g + 1)
                        nc.scalar.activation(hhi[:, 2 * g:2 * g + 2, :].rearrange("p k n -> p (k n)"), bank[6 + g][:, :], ACT.Copy)\
                            .then_inc(S("phi_done"), 1)
                    hi_static(n0 + 52, 256)
                    hi_static(n0 + 53, 256)
                    split_groups(4, 4)
                    for u in range(4):
                        hi_static(n0 + 54 + u, SLOT)
                    split_groups(0, KD)
                    for u in range(8):
                        hi_static(n0 + 58 + u, SLOT)
                    gate_rows(1.0)
            norm_stage(o_n[0] + 1)

        @block.vector
        def _(dve):
            V = nc.vector
            seq = [0]

            def then(ins):
                seq[0] += 1
                ins.then_inc(S("dve_step"), 1)
                dve.wait_ge(S("dve_step"), seq[0])

            def lo(slot, width, ready):
                dve.wait_ge(S("hi_done"), ready)
                V.tensor_tensor(wlo[:, slot, 0:width], raw[:, slot, 0:width], whi[:, slot, 0:width].bitcast(F32),
                                ALU.subtract).then_inc(S("lo_done"), 1)

            def lo_static(n, width):
                lo(n % RING, width, n + 1)

            V.memset(stat[:, 0:4], 0.0).then_inc(S("lo_done"), RING)
            V.memset(stat[:, 4:8], 0.0).then_inc(S("mm_done"), RING)
            V.memset(stat[:, 8:12], 0.0).then_inc(S("hi_done"), RING)
            V.memset(zero_hi[:, :].bitcast(F32), 0.0).then_inc(S("zero_ready"), 1)
            V.memset(relb1, 0.0).then_inc(S("zero_ready"), 1)

            def mod_unit(k, m, chunk, cond, first_free):
                dve.wait_ge(S(f"mod_loaded{k % MOD_RING}"), 16 * (8 // MOD_RING) * chunk + 16 * (k // MOD_RING + 1))
                w = modw[:, k % MOD_RING, :]
                sc = silc[:, 8 * cond + k:8 * cond + k + 1]
                if k == 0:
                    need(dve, S("mod_summed"), first_free)
                    V.tensor_scalar(modacc[:, :], w, sc, None, ALU.mult).then_inc(S("mod_used"), 1)
                else:
                    dve.wait_ge(S("mod_used"), m)
                    V.scalar_tensor_tensor(modacc[:, :], w, sc, modacc[:, :], ALU.mult, ALU.add).then_inc(S("mod_used"), 1)

            def mod_units(k0, k1, chunk, cond):
                for k in range(k0, k1):
                    mod_unit(k, 8 * chunk + k, chunk, cond, chunk)

            def mod_store(chunk):
                dve.wait_ge(S("mod_summed"), chunk + 1)
                at = bass.ds(8 * chunk, 8)
                V.tensor_tensor(modc[:, at], bank[MB][:, 0:8], vec[:, at], ALU.add).then_inc(S("mod_stored"), 1)

            for t in range(3):
                dve.wait_ge(S("vecT_ready"), t + 1)
                r = P if t < 2 else V_ROWS2
                ins = V.tensor_copy(vec[:, t * P:t * P + r], bank[t][:, 0:r])
            ins.then_inc(S("vec_ready"), 1)

            dve.wait_ge(S("pos_loaded"), 14 * 16)
            dve.wait_ge(S("const_loaded"), 16)
            V.tensor_copy(posf_i, pos_i)
            V.tensor_copy(posf_q, pos_q)
            V.tensor_copy(posf_k, pos_k)
            then(V.tensor_tensor(bstep, relb, relb1, ALU.subtract))
            freq = con[:, C_FREQ:C_FREQ + 16]
            for t in range(NT):
                ins = V.tensor_scalar(ang[:, t, :], freq, posf_i[:, t:t + 1], None, ALU.mult)
            then(V.tensor_scalar(posf_q, posf_q, con[:, C_THR:C_THR + 1], None, ALU.subtract))

            for q in range(3):
                then(V.tensor_copy(bparts[:, q, :], bstep))
                if q < 2:
                    then(V.tensor_tensor(bstep, bstep, bparts[:, q, :], ALU.subtract))
            magic = 1.5 * 2.0 ** 23
            c1 = 6.28125
            c2 = float(np.float32(2 * math.pi - c1))
            c3 = 2 * math.pi - c1 - c2
            for s in range(2):
                V.tensor_scalar(turns[:, s], ang, 1.0 / (2 * math.pi), 0.25 if s == 0 else 0.0, ALU.mult, ALU.add)
            then(V.memset(stat[:, 12:16], 0.0))
            tf = turns.rearrange("p a t n -> p (a t n)")
            then(V.tensor_scalar(tf, tf, magic, None, ALU.add))
            then(V.tensor_scalar(tf, tf, magic, None, ALU.subtract))
            for s in range(2):
                then(V.scalar_tensor_tensor(rope1[:, s], turns[:, s], -c1, ang, ALU.mult, ALU.add))
                then(V.scalar_tensor_tensor(rope1[:, s], turns[:, s], -c2, rope1[:, s], ALU.mult, ALU.add))
                then(V.scalar_tensor_tensor(rope1[:, s], turns[:, s], -c3, rope1[:, s], ALU.mult, ALU.add))
            then(V.tensor_scalar(rope1[:, 0], rope1[:, 0], math.pi / 2, None, ALU.add))
            r1 = rope1[:, :, :, :].rearrange("p a t n -> p (a t n)")
            V.tensor_scalar(r1, r1, 3.1415925, -3.1415925, ALU.min, ALU.max).then_inc(S("angles_ready"), 1)

            dve.wait_ge(S("cond_ready"), 1)
            done = 0
            for q in range(6):
                need(dve, S("bias_summed"), q)
                q0, kb, c0 = (0, P, P)[q // 2], (0, 0, 1)[q // 2], 16 * (q % 2)
                V.tensor_tensor(reached, posf_q[:, q0:q0 + P].unsqueeze(1).broadcast_to([P, 16, P]),
                                posf_k[:, kb, c0:c0 + 16].unsqueeze(2).broadcast_to([P, 16, P]), ALU.is_ge).then_inc(S("reached"), 1)
                for u in range(done, min(done + 3, 16)):
                    if u == 8:
                        mod_store(0)
                    mod_units(u % 8, u % 8 + 1, u // 8, 0)
                done += 3
                dve.wait_ge(S("bias_summed"), q + 1)
                for g in range(4):
                    c = P * (q // 2) + 32 * g + c0
                    ins = V.tensor_reduce(bias[:, :, c:c + 16], bank[3 + g][:, 0:288].rearrange("p (k q h) -> p h k q", q=3, h=WH), AX, ALU.add)
                ins.then_inc(S("bias_taken"), 1)
            dve.wait_ge(S("bias_taken"), 6)
            V.tensor_tensor(bias[:, :, :], bias[:, :, :], con[:, C_MASKW:C_MASKW + 384].unsqueeze(1).broadcast_to([P, WH, 384]), ALU.add)
            mod_store(1)

            tr, turned = [0], [0]
            cnt = {}

            def rope(tiles, cos, sin, heads, half, sem):
                tmp = ar(A_T, 4 * heads * half).rearrange("p (q h n) -> p q h n", q=4, h=heads)
                for t in range(NT):
                    x1, x2 = tiles[t][:, :, 0:half], tiles[t][:, :, half:2 * half]
                    c = cos[t].unsqueeze(1).broadcast_to([P, heads, half])
                    s = sin[t].unsqueeze(1).broadcast_to([P, heads, half])
                    V.tensor_tensor(tmp[:, 0], x1, c, ALU.mult)
                    V.tensor_tensor(tmp[:, 1], x2, s, ALU.mult)
                    V.tensor_tensor(tmp[:, 2], x2, c, ALU.mult)
                    then(V.tensor_tensor(tmp[:, 3], x1, s, ALU.mult))
                    V.tensor_tensor(x1, tmp[:, 0], tmp[:, 1], ALU.subtract)
                    ins = V.tensor_tensor(x2, tmp[:, 2], tmp[:, 3], ALU.add)
                    if t < NT - 1:
                        then(ins)
                ins.then_inc(S(sem), 1)

            def mean_eps(ap, count):
                then(V.tensor_scalar(ap, ap, 1.0 / count, EPS, ALU.mult, ALU.add))

            def rooted(name, ap):
                cnt[name] = cnt.get(name, 0) + 1
                dve.wait_ge(S(name + "_root"), cnt[name])
                then(V.reciprocal(ap, ap))

            def norm_stage(k):
                dve.wait_ge(S("ss_ready"), k)
                V.tensor_scalar(stat[:, 2:4], stat[:, 0:2], 1.0 / D, EPS, ALU.mult, ALU.add).then_inc(S("ms_ready"), 1)
                dve.wait_ge(S("rms_ready"), k)
                V.reciprocal(stat[:, 4:6], stat[:, 2:4]).then_inc(S("rstd_ready"), 1)
                dve.wait_ge(S("rstd_ready"), k)
                V.tensor_scalar(xn[:, 1, :], x[:, 1, :], stat[:, 5:6], None, ALU.mult).then_inc(S("xn1_ready"), 1)

            def split_groups(dst0, chunks, scale, shift, products=None):
                def scaled(c):
                    g = tr[0] + c // 2
                    if products is None:
                        dve.wait_ge(S("tr_ready"), turned[0] + c // 2 + 1)
                    else:
                        dve.wait_ge(S("mm_done"), products + c // 2)
                    need(dve, S("hlo_done"), g - 1)
                    for k in range(c, min(c + 2, chunks)):
                        src = bank[TRB[g % 4]][:, 256 * (k - c):256 * (k - c + 1)]
                        dst = hf[:, g % 2, 256 * (k - c):256 * (k - c + 1)]
                        if shift is None:
                            ins = V.tensor_scalar(dst, src, scale[:, k:k + 1], None, ALU.mult) if scale is not None else V.tensor_copy(dst, src)
                        else:
                            ins = V.tensor_scalar(dst, src, scale[:, k:k + 1], shift[:, k:k + 1], ALU.mult, ALU.add)
                    ins.then_inc(S("hf_ready"), 1)

                def low(c):
                    g = tr[0] + c // 2
                    w = min(2, chunks - c) * SEQ
                    dve.wait_ge(S("hhi_done"), g + 1)
                    dve.wait_ge(S("hf_ready"), g + 1)
                    V.tensor_tensor(hlo[:, dst0 + c:dst0 + c + w // SEQ, :].rearrange("p k n -> p (k n)"), hf[:, g % 2, 0:w],
                                    hhi[:, dst0 + c:dst0 + c + w // SEQ, :].rearrange("p k n -> p (k n)").bitcast(F32),
                                    ALU.subtract).then_inc(S("hlo_done"), 1)

                for c in range(0, chunks, 2):
                    scaled(c)
                    if c >= 2:
                        low(c - 2)
                low(2 * ((chunks - 1) // 2))
                tr[0] += (chunks + 1) // 2
                if products is None:
                    turned[0] += (chunks + 1) // 2

            def finish_x(k, end):
                dve.wait_ge(S("gate_ready"), k)
                dve.wait_ge(S("mm_done"), end)
                tmp = ar(A_X, 2048).rearrange("p (t n) -> p t n", t=NT)
                for t in range(NT):
                    for h in range(2):
                        c = slice(512 * h, 512 * (h + 1))
                        ins = V.tensor_tensor(tmp[:, t, c], bank[2 * t + h][:, :], gate_b[:, c], ALU.mult)
                then(ins)
                V.tensor_tensor(x[:, :, :], x[:, :, :], tmp, ALU.add).then_inc(S("x_done"), 1)

            def scale_cols(a):
                dve.wait_ge(S("mod_stored"), a["mod"] + 2)
                sc = modc[:, 8 * (a["mod"] + 1):8 * (a["mod"] + 2)]
                then(V.scalar_tensor_tensor(sclA[:, :], sc, 1.0, vec[:, a["g"]:a["g"] + 8], ALU.add, ALU.mult))

            dve.wait_ge(S("x_loaded"), 16)
            V.memset(stat[:, 16:20], 0.0).then_inc(S("x_done"), 1)
            phase = [0]
            ffn_n, mid1_n, mid2_n = [0], [0], [0]
            for kind, n0, a in phases:
                phase[0] += 1
                scale_cols(a)
                norm_stage(phase[0])
                split_groups(0, KD, sclA, modc[:, 8 * a["mod"]:8 * (a["mod"] + 1)])
                if kind == "ffn":
                    f = ffn_n[0]
                    ffn_n[0] += 1
                    before, in_loop = MOD_PLAN[f]

                    def cond_of(c):
                        return 0 if c < 18 else 1

                    def gated(j):
                        for t in range(NT):
                            dve.wait_ge(S("silu_done"), 2 * (STRIPS * f + j) + t + 1)
                            if t == 0:
                                need(dve, S("actT_ready"), STRIPS * f + j)
                            ins = V.tensor_tensor(act_t[:, t, :], sg_t[:, t, :], bank[GB[t]][:, 256:512], ALU.mult)
                        ins.then_inc(S("act_ready"), 1)

                    def act_lo(j):
                        dve.wait_ge(S("ahi_done"), STRIPS * f + j + 1)
                        V.tensor_tensor(alo[:, :, :].rearrange("p k n -> p (k n)"), bank[ATB][:, :],
                                        ahi[:, :, :].rearrange("p k n -> p (k n)").bitcast(F32), ALU.subtract).then_inc(S("alo_done"), 1)

                    def units(c, i, lo_, hi_):
                        for u in range(lo_, hi_):
                            m = c + u
                            lo(m % RING, SLOT, 12 * i + m + 1)

                    units(n0, 0, 0, 4)
                    if before is not None:
                        mod_units(0, 8, before, cond_of(before))
                    gated(0)
                    if before is not None:
                        mod_store(before)
                    with dve.Fori(0, STRIPS // 2) as i:
                        for s in range(2):
                            c = n0 + 4 + 6 * s
                            units(c, i, 0, 4)
                            act_lo(2 * i + s)
                            units(c, i, 4, 6)
                            if in_loop is not None:
                                mod_units(4 * s, 4 * s + 4, i + in_loop, cond_of(in_loop + 4))
                            gated(2 * i + s + 1)
                        if in_loop is not None:
                            mod_store(i + in_loop)
                    c = n0 + 4 + 12 * (STRIPS // 2)
                    act_lo(STRIPS - 1)
                    units(c, 0, 0, 2)
                    finish_x(phase[0], n0 + {"ffn": UNITS_FFN, "mid1": UNITS_MID1, "mid2": UNITS_MID2}[kind])
                elif kind == "mid1":
                    m = mid1_n[0]
                    l = a["l"]
                    mid1_n[0] += 1
                    widths = [512, 512, 512, D_IN - 1536]
                    for s in range(4):
                        for u in range(4):
                            lo_static(n0 + 4 * s + u, 2 * widths[s])
                        if s >= 1:
                            dve.wait_ge(S("mm_done"), n0 + 4 * s)
                            V.tensor_copy(proj[:, 1, 512 * (s - 1):512 * s], bank[2 * (s - 1) + 1][:, :]).then_inc(S("strip_copied1"), 1)
                    dve.wait_ge(S("mm_done"), n0 + 16)
                    V.tensor_copy(proj[:, 1, 1536:D_IN], bank[7][:, 0:D_IN - 1536]).then_inc(S("strip_copied1"), 1)
                    sq = ar(A_QK, NT * 928).rearrange("p (t n) -> p t n", t=NT)
                    dve.wait_ge(S("sq_ready"), m + 1)
                    V.tensor_reduce(stat[:, 8:10], sq[:, :, 0:QL], AX, ALU.add)
                    V.tensor_reduce(stat[:, 10:12], sq[:, :, QL:QL + KVL], AX, ALU.add)
                    V.tensor_reduce(stat[:, 28:30], sq[:, :, O_KPE:O_KPE + MROPE], AX, ALU.add)
                    then(V.tensor_reduce(stat[:, 12:28].rearrange("p (t h) -> p t h", t=NT),
                                         sq[:, :, O_WQ:O_WQ + 512].rearrange("p t (h n) -> p t h n", n=HD), AX, ALU.add))
                    mean_eps(stat[:, 8:10], QL)
                    mean_eps(stat[:, 10:12], KVL)
                    V.tensor_scalar(stat[:, 12:28], stat[:, 12:28], 1.0 / HD, EPS, ALU.mult, ALU.add).then_inc(S("lat_ms"), 1)
                    rooted("lat_ms", stat[:, 8:28])
                    for t in range(NT):
                        V.tensor_scalar(lat[:, t, 0:QL], proj[:, t, 0:QL], stat[:, 8 + t:9 + t], None, ALU.mult)
                        ins = V.tensor_scalar(lat[:, t, QL:], proj[:, t, QL:QL + KVL], stat[:, 10 + t:11 + t], None, ALU.mult)
                    ins.then_inc(S("lat_ready"), 1)
                    wq = proj[:, :, O_WQ:O_WQ + 512].rearrange("p t (h n) -> p t h n", n=HD)
                    for t in range(NT):
                        ins = V.tensor_tensor(wq[:, t], wq[:, t], stat[:, 12 + 8 * t:20 + 8 * t].unsqueeze(2).broadcast_to([P, 8, HD]), ALU.mult)
                    V.tensor_copy(latg[:, 0:2], vec[:, V_QA + 2 * l:V_QA + 2 * l + 2])
                    then(V.tensor_copy(latg[:, 2:3], vec[:, V_KVA + l:V_KVA + l + 1]))
                    dve.wait_ge(S("gains_loaded"), 16 * 5 * (l + 1))
                    for t in range(NT):
                        V.tensor_tensor(wq[:, t, 0:WH], wq[:, t, 0:WH], gw64[:, 0:1, :].broadcast_to([P, WH, HD]), ALU.mult)
                        for kvh in range(WKV):
                            ins = V.tensor_tensor(kdup[:, t, kvh], wq[:, t, WH + kvh:WH + kvh + 1].broadcast_to([P, 2, HD]),
                                                  gw64[:, 1:2, :].broadcast_to([P, 2, HD]), ALU.mult)
                    then(ins)
                    split_groups(0, 3, latg, None)
                    lo_static(n0 + 16, 576)
                    lo_static(n0 + 17, 576)
                    lo_static(n0 + 18, 384)
                    lo_static(n0 + 19, 384)
                    dve.wait_ge(S("mm_done"), n0 + 20)
                    for u in range(2):
                        V.tensor_copy(qk1[:, 1, 3 * u:3 * u + 3, :].rearrange("p h n -> p (h n)"), bank[2 * u + 1][:, 0:288])
                        ins = V.tensor_copy(kv[:, 1, 3 * u:3 * u + 3, :].rearrange("p h n -> p (h n)"), bank[5 + 2 * u][:, 0:384])
                    ins.then_inc(S("up_copied1"), 1)
                    sqq = ar(A_T, NT * 576).rearrange("p (t h n) -> p t h n", t=NT, h=MH)
                    sqk = ar(A_T + NT * 576, NT * 384).rearrange("p (t h n) -> p t h n", t=NT, h=MH)
                    hs = stat[:, 32:56].rearrange("p (t h) -> p t h", t=NT)
                    dve.wait_ge(S("sqh_ready"), m + 1)
                    V.tensor_reduce(hs[:, :, 0:MH], sqq, AX, ALU.add)
                    then(V.tensor_reduce(hs[:, :, MH:12], sqk, AX, ALU.add))
                    for t in range(NT):
                        ins = V.tensor_scalar(hs[:, t, MH:12], hs[:, t, MH:12], stat[:, 28 + t:29 + t], None, ALU.add)
                    then(ins)
                    V.tensor_scalar(stat[:, 32:56], stat[:, 32:56], 1.0 / MQK, EPS, ALU.mult, ALU.add).then_inc(S("head_ms"), 1)
                    rooted("head_ms", stat[:, 32:56])
                    for t in range(NT):
                        V.tensor_copy(qk1[:, t, MH:12, 0:MNOPE], kv[:, t, :, 0:MNOPE])
                        ins = V.tensor_copy(qk1[:, t, MH:12, MNOPE:MQK], proj[:, t, O_KPE:O_KPE + MROPE].unsqueeze(1).broadcast_to([P, MH, MROPE]))
                    then(ins)
                    for t in range(NT):
                        ins = V.tensor_tensor(qk1[:, t], qk1[:, t], hs[:, t].unsqueeze(2).broadcast_to([P, 12, MQK]), ALU.mult)
                    then(ins)
                    for t in range(NT):
                        V.tensor_tensor(qk1[:, t, 0:MH], qk1[:, t, 0:MH], gq96[:, 0:1, :].broadcast_to([P, MH, MQK]), ALU.mult)
                        ins = V.tensor_tensor(qk1[:, t, MH:12], qk1[:, t, MH:12], gq96[:, 1:2, :].broadcast_to([P, MH, MQK]), ALU.mult)
                    then(ins)
                    if m == 0:
                        dve.wait_ge(S("rope_ready"), 1)
                    rope([qk1[:, t, :, MNOPE:MQK] for t in range(NT)], [rope1[:, 0, t] for t in range(NT)],
                         [rope1[:, 1, t] for t in range(NT)], 12, 16, "heads_normed")
                    for g in range(0, 11, 2):
                        dve.wait_ge(S("qkT_ready"), 11 * m + g + 1)
                        copy_qk(V.tensor_copy, g).then_inc(S("qkT_copied_dve"), 1)
                    for h in range(12):
                        k = 12 * m + h
                        r = h % 2
                        dve.wait_ge(S("scores_ready"), 16 * m + h + 1)
                        if h >= 2:
                            dve.wait_ge(S("probsT_ready"), k - 1)
                        mask = con[:, C_MASKC:C_MASKC + 384] if h < MH else bias[:, h - MH, :]
                        scale = MQK ** -0.5 if h < MH else HD ** -0.5
                        then(V.scalar_tensor_tensor(sc_t[:, r, :], bank[r][:, 0:384], scale, mask, ALU.mult, ALU.add))
                        mx = nmax[:, 2 * h:2 * h + 2]
                        V.tensor_reduce(mx[:, 0:1], sc_t[:, r, 0:P], AX, ALU.max)
                        then(V.tensor_reduce(mx[:, 1:2], sc_t[:, r, P:384], AX, ALU.max))
                        if h < MH:
                            V.tensor_scalar(mx, mx, -1.0, None, ALU.mult).then_inc(S("max_ready"), 1)
                        else:
                            V.tensor_scalar(mx, mx, sink[:, h - MH:h - MH + 1], -1.0, ALU.max, ALU.mult).then_inc(S("max_ready"), 1)
                    dve.wait_ge(S("max_ready"), 12 * m + 12)
                    for h in range(WH):
                        ins = V.tensor_scalar(esink[:, 2 * h:2 * h + 2], nmax[:, 2 * (MH + h):2 * (MH + h) + 2], sink[:, h:h + 1], None, ALU.add)
                    ins.then_inc(S("sink_diff"), 1)
                    dve.wait_ge(S("probs_ready"), 12 * m + 12)
                    dve.wait_ge(S("sink_exp"), m + 1)
                    then(V.tensor_tensor(rsum[:, 12:24], rsum[:, 12:24], esink, ALU.add))
                    then(V.reciprocal(rsum[:, 0:24], rsum[:, 0:24]))
                    for h in range(SH):
                        k = SH * m + h
                        r = h % 2
                        dve.wait_ge(S("scores_ready"), 16 * m + 12 + h + 1)
                        if h < 2:
                            dve.wait_ge(S("pv_done"), 16 * m + 12)
                        else:
                            dve.wait_ge(S("pv_done"), 16 * m + 12 + h - 1)
                        z = sc_t[:, r, :]
                        u_ = pt_t[:, r, :]
                        then(V.tensor_scalar(z, bank[r][:, 0:384], HD ** -0.5, None, ALU.mult))
                        V.scalar_tensor_tensor(u_, z, -1.0, z, ALU.mult, ALU.max).then_inc(S("absz_ready"), 1)
                        dve.wait_ge(S("ln_ready"), k + 1)
                        then(V.scalar_tensor_tensor(u_, z, 0.0, u_, ALU.max, ALU.add))
                        V.tensor_tensor(u_, u_, con[:, C_MASKS:C_MASKS + 384], ALU.mult).then_inc(S("stick_ready"), 1)
                        dve.wait_ge(S("stick_sum"), k + 1)
                        then(V.tensor_tensor(z, z, bank[2 + r][:, 0:384], ALU.subtract))
                        V.tensor_tensor(z, z, con[:, C_MASKA:C_MASKA + 384], ALU.add).then_inc(S("zs_ready"), 1)
                    dve.wait_ge(S("pv_done"), 16 * m + 16)
                    rs = rsum[:, 0:24].rearrange("p (h t) -> p t h", t=NT)
                    for t in range(NT):
                        b0, b1 = bank[4 + t], bank[6 + t]
                        V.tensor_tensor(mix[:, t, 0:512].rearrange("p (h n) -> p h n", n=64), b0[:, :].rearrange("p (h n) -> p h n", n=64),
                                        rs[:, t, 0:8].unsqueeze(2).broadcast_to([P, 8, 64]), ALU.mult)
                        V.tensor_tensor(mix[:, t, 512:768].rearrange("p (h n) -> p h n", n=64), b1[:, 0:256].rearrange("p (h n) -> p h n", n=64),
                                        rs[:, t, 8:12].unsqueeze(2).broadcast_to([P, 4, 64]), ALU.mult)
                        ins = V.tensor_copy(mix[:, t, 768:1024], b1[:, 256:512])
                    ins.then_inc(S("heads_out"), 1)
                    sqm = ar(A_PROJ, 2048).rearrange("p (t n) -> p t n", t=NT)
                    dve.wait_ge(S("sqm_ready"), m + 1)
                    ms = stat[:, 8:14].rearrange("p (g t) -> p g t", t=NT)
                    V.tensor_reduce(ms[:, 0, :], sqm[:, :, 0:384], AX, ALU.add)
                    V.tensor_reduce(ms[:, 1, :], sqm[:, :, 384:768], AX, ALU.add)
                    then(V.tensor_reduce(ms[:, 2, :], sqm[:, :, 768:1024], AX, ALU.add))
                    V.tensor_scalar(stat[:, 8:12], stat[:, 8:12], 1.0 / 384, EPS, ALU.mult, ALU.add)
                    V.tensor_scalar(stat[:, 12:14], stat[:, 12:14], 1.0 / 256, EPS, ALU.mult, ALU.add).then_inc(S("mix_ms"), 1)
                    rooted("mix_ms", stat[:, 8:14])
                    for t in range(NT):
                        for g, (c0, c1) in enumerate(((0, 384), (384, 768), (768, 1024))):
                            ins = V.tensor_scalar(mix[:, t, c0:c1], mix[:, t, c0:c1], stat[:, 8 + 2 * g + t:9 + 2 * g + t], None, ALU.mult)
                    ins.then_inc(S("mix_ready"), 1)
                    split_groups(0, KD, vec[:, V_ON + 8 * l:V_ON + 8 * l + 8], None)
                    for u in range(8):
                        lo_static(n0 + 20 + u, SLOT)
                    finish_x(phase[0], n0 + {"ffn": UNITS_FFN, "mid1": UNITS_MID1, "mid2": UNITS_MID2}[kind])
                else:
                    m = mid2_n[0]
                    l = a["l"]
                    mid2_n[0] += 1

                    def split_strip(s):
                        for u in range(4):
                            lo_static(n0 + 4 * s + u, SLOT)

                    def strip(s):
                        if s in (0, 1, 2, 3, 6):
                            dve.wait_ge(S("mm_done"), n0 + 4 * s + 4)
                            dst = {0: qk2[:, 1, 0:512], 1: qk2[:, 1, 512:1024], 2: v2[:, 1, 0:512], 3: v2[:, 1, 512:1024], 6: p2[:, 1, :]}[s]
                            V.tensor_copy(dst, bank[2 * (s % 3) + 1][:, :]).then_inc(S("strip2_copied1"), 1)

                    for s in range(7):
                        split_strip(s)
                        if s >= 1:
                            strip(s - 1)
                        if s == 2:
                            dve.wait_ge(S("strip2_copied0"), 11 * m + 2)
                            dve.wait_ge(S("strip2_copied1"), 5 * m + 2)
                            rp = [qk2[:, t, :].rearrange("p (h n) -> p h n", n=RQK) for t in range(NT)]
                            cs = [con[:, C_ROPE2 + 32 * t:C_ROPE2 + 32 * (t + 1)] for t in range(NT)]
                            sn = [con[:, C_ROPE2 + 64 + 32 * t:C_ROPE2 + 64 + 32 * (t + 1)] for t in range(NT)]
                            rope(rp, cs, sn, 16, 32, "rope2_done")
                        if s == 4:
                            for g in (0, 2):
                                dve.wait_ge(S("qkT2_ready"), 4 * m + g + 1)
                                V.tensor_copy(qkT2[:, 2 * g:2 * g + 2, :].rearrange("p h n -> p (h n)"), bank[6 + g % 2][:, :])\
                                    .then_inc(S("qkT2_copied_dve"), 1)
                    strip(6)
                    if m == 0:
                        dve.wait_ge(S("const2_loaded"), 16)
                    for h in range(RH):
                        k = RH * m + h
                        dve.wait_ge(S("ret_scores"), k + 1)
                        if h >= 2:
                            dve.wait_ge(S("ret_pv"), k - 1)
                        dec = con2[:, C2_DECAY + 256 * h:C2_DECAY + 256 * (h + 1)]
                        V.tensor_tensor(sc_t[:, h % 2, 0:256], bank[6 + h % 2][:, 0:256], dec, ALU.mult)
                        V.tensor_tensor(sc_t[:, h % 2, 256:384], bank[6 + h % 2][:, 256:384], dec[:, 0:P], ALU.mult).then_inc(S("ret_probs"), 1)
                    sqr = ar(A_T, 2048).rearrange("p (t n) -> p t n", t=NT)
                    dve.wait_ge(S("sqr_ready"), m + 1)
                    rr = stat[:, 8:24].rearrange("p (t h) -> p t h", t=NT)
                    then(V.tensor_reduce(rr, sqr.rearrange("p t (h n) -> p t h n", n=RV), AX, ALU.add))
                    V.tensor_scalar(stat[:, 8:24], stat[:, 8:24], 1.0 / RV, EPS, ALU.mult, ALU.add).then_inc(S("ret_ms"), 1)
                    for t in range(NT):
                        for hh in range(2):
                            c = slice(512 * hh, 512 * (hh + 1))
                            ins = V.tensor_tensor(ret[:, t, c], ret[:, t, c], bank[2 * t + hh][:, :], ALU.mult)
                    ins.then_inc(S("ret_taken"), 1)
                    rooted("ret_ms", stat[:, 8:24])
                    dve.wait_ge(S("ret_taken"), m + 1)
                    rv = ret.rearrange("p t (h n) -> p t h n", n=RV)
                    for t in range(NT):
                        ins = V.tensor_tensor(rv[:, t], rv[:, t], rr[:, t].unsqueeze(2).broadcast_to([P, RH, RV]), ALU.mult)
                    ins.then_inc(S("ret_ready"), 1)
                    for s in range(7, 11):
                        split_strip(s)
                    split_groups(0, KD, None, None)
                    for u in range(8):
                        lo_static(n0 + 44 + u, SLOT)
                    for g in range(2):
                        dve.wait_ge(S("phi_done"), 2 * m + g + 1)
                        V.tensor_tensor(hlo[:, 2 * g:2 * g + 2, :].rearrange("p k n -> p (k n)"), bank[6 + g][:, :],
                                        hhi[:, 2 * g:2 * g + 2, :].rearrange("p k n -> p (k n)").bitcast(F32), ALU.subtract)\
                            .then_inc(S("plo_done"), 1)
                    lo_static(n0 + 52, 256)
                    lo_static(n0 + 53, 256)
                    dve.wait_ge(S("strip2_copied0"), 11 * (m + 1))
                    dve.wait_ge(S("mm_done"), n0 + 52)
                    for t in range(NT):
                        for h in range(2):
                            c = slice(512 * h, 512 * (h + 1))
                            ins = V.tensor_tensor(gates[:, t, c], gates[:, t, c], bank[2 * t + h][:, :], ALU.mult)
                    ins.then_inc(S("ret_gated"), 1)
                    split_groups(4, 4, vec[:, V_PS + 4 * l:V_PS + 4 * l + 4], None, products=n0 + 53)
                    for u in range(4):
                        lo_static(n0 + 54 + u, SLOT)
                    dve.wait_ge(S("mm_done"), n0 + 58)
                    for t in range(NT):
                        for h in range(2):
                            c = slice(1024 + 512 * h, 1024 + 512 * (h + 1))
                            ins = V.tensor_tensor(gates[:, t, c], gates[:, t, c], bank[2 * t + h][:, :], ALU.mult)
                    then(ins)
                    V.tensor_tensor(gates[:, :, 0:D], gates[:, :, 0:D], gates[:, :, D:2 * D], ALU.add).then_inc(S("merged_ready"), 1)
                    split_groups(0, KD, None, None)
                    for u in range(8):
                        lo_static(n0 + 58 + u, SLOT)
                    finish_x(phase[0], n0 + {"ffn": UNITS_FFN, "mid1": UNITS_MID1, "mid2": UNITS_MID2}[kind])
            k = phase[0] + 1
            norm_stage(k)
            dve.wait_ge(S("xn0_ready"), k)
            dve.wait_ge(S("xn1_ready"), k)
            dve.wait_ge(S("final_gain"), 16)
            V.tensor_tensor(xn, xn, gate_b.unsqueeze(1).broadcast_to([P, NT, D]), ALU.mult).then_inc(S("out_ready"), 1)

        @block.tensor
        def _(pe):
            T = nc.tensor

            def products(o, c, t, wh, wl, start, stop, hi_=hhi, lo_=hlo):
                sh, sl = hi_[:, c, P * t:P * (t + 1)], lo_[:, c, P * t:P * (t + 1)]
                T.matmul(o, sh, wh, start=start, stop=False)
                T.matmul(o, sh, wl, start=False, stop=False)
                return T.matmul(o, sl, wh, start=False, stop=stop)

            def strip_unit(slot, ready, u, last, banks, width, hi_=hhi, lo_=hlo):
                pe.wait_ge(S("lo_done"), ready)
                for k in range(2):
                    wh = whi[:, slot, k * width:(k + 1) * width]
                    wl = wlo[:, slot, k * width:(k + 1) * width]
                    for t in range(NT):
                        ins = products(bank[banks[t]][:, 0:width], 2 * u + k, t, wh, wl, u == 0 and k == 0, last and k == 1)
                ins.then_inc(S("mm_done"), 1)

            def rows_unit(slot, ready, c, first, last, hi_, lo_):
                pe.wait_ge(S("lo_done"), ready)
                for t in range(NT):
                    for h in range(2):
                        wh = whi[:, slot, 512 * h:512 * (h + 1)]
                        wl = wlo[:, slot, 512 * h:512 * (h + 1)]
                        ins = products(bank[2 * t + h][:, :], c, t, wh, wl, first, last, hi_, lo_)
                ins.then_inc(S("mm_done"), 1)

            pe.wait_ge(S("const_loaded"), 16)
            pe.wait_ge(S("rows_loaded"), 13 * 16)
            rows = ar(A_X, 3 * P).rearrange("p (t n) -> p t n", t=3)
            for t in range(3):
                r = P if t < 2 else V_ROWS2
                T.transpose(bank[t][:, 0:r], rows[0:r, t, :], ident[0:r, 0:r]).then_inc(S("vecT_ready"), 1)

            def mod_sum(chunk):
                pe.wait_ge(S("mod_used"), 8 * chunk + 8)
                need(pe, S("mod_stored"), chunk)
                for k in range(KD):
                    ins = T.matmul(bank[MB][:, k:k + 1], modacc[:, P * k:P * (k + 1)], ones_col, start=True, stop=True)
                ins.then_inc(S("mod_summed"), 1)

            for q in range(6):
                pe.wait_ge(S("reached"), q + 1)
                need(pe, S("bias_taken"), q)
                for k in range(16):
                    for g in range(4):
                        r = slice(NBUCKET * g, NBUCKET * (g + 1))
                        ins = T.matmul(bank[3 + g][:, 3 * WH * k:3 * WH * (k + 1)], reached[r, k, :], bparts[r].rearrange("p q h -> p (q h)"),
                                       start=True, stop=True)
                ins.then_inc(S("bias_summed"), 1)
                if q == 2:
                    mod_sum(0)
            mod_sum(1)

            tr = [0]

            def transposes(src, chunks):
                for c in range(0, chunks, 2):
                    g = tr[0]
                    need(pe, S("hf_ready"), g - 3)
                    for k in range(c, min(c + 2, chunks)):
                        for t in range(NT):
                            ins = T.transpose(bank[TRB[g % 4]][:, 256 * (k - c) + P * t:256 * (k - c) + P * (t + 1)],
                                              src[:, t, P * k:P * (k + 1)], ident)
                    ins.then_inc(S("tr_ready"), 1)
                    tr[0] += 1

            def gate_rows(chunk):
                pe.wait_ge(S("mod_stored"), chunk + 1)
                pe.wait_ge(S("hf_ready"), tr[0])
                for k in range(KD):
                    col = modc[:, 8 * chunk + k:8 * chunk + k + 1].broadcast_to([P, P])
                    ins = T.matmul(bank[6 + k // 4][:, P * (k % 4):P * (k % 4 + 1)], col, ident, start=True, stop=True)
                ins.then_inc(S("gate_rows"), 1)

            ph, ffn_n, mid1_n, mid2_n = [0], [0], [0], [0]
            pe.wait_ge(S("zero_ready"), 1)
            for kind, n0, a in phases:
                ph[0] += 1
                pe.wait_ge(S("xn0_ready"), ph[0])
                pe.wait_ge(S("xn1_ready"), ph[0])
                transposes(xn, KD)
                pe.wait_ge(S("hlo_done"), tr[0])
                if kind == "ffn":
                    f = ffn_n[0]
                    ffn_n[0] += 1
                    before, in_loop = MOD_PLAN[f]

                    def gate_up(c, i, lo_, hi_):
                        for u in range(lo_, hi_):
                            strip_unit((c + u) % RING, 12 * i + c + u + 1, u, u == 3, GB, 512)

                    def down(c, i, j, last):
                        pe.wait_ge(S("alo_done"), STRIPS * f + j + 1)
                        for u in range(2):
                            rows_unit((c + u) % RING, 12 * i + c + u + 1, u, False, last and u == 1, ahi, alo)

                    def turn(j):
                        pe.wait_ge(S("act_ready"), STRIPS * f + j + 1)
                        for k in range(2):
                            for t in range(NT):
                                ins = T.transpose(bank[ATB][:, 256 * k + P * t:256 * k + P * (t + 1)], act_t[:, t, P * k:P * (k + 1)], ident)
                        ins.then_inc(S("actT_ready"), 1)

                    for b in range(4):
                        T.matmul(bank[b][:, :], zero_hi[:, :], hhi[:, 0:2, :].rearrange("p k n -> p (k n)"), start=True, stop=False)
                    gate_up(n0, 0, 0, 4)
                    if before is not None:
                        mod_sum(before)
                    with pe.Fori(0, STRIPS // 2) as i:
                        for s in range(2):
                            c = n0 + 4 + 6 * s
                            pe.wait_ge(S("act_ready"), STRIPS * f + 2 * i + s + 1)
                            gate_up(c, i, 0, 2)
                            turn(2 * i + s)
                            gate_up(c, i, 2, 4)
                            down(c + 4, i, 2 * i + s, False)
                        if in_loop is not None:
                            mod_sum(i + in_loop)
                    c = n0 + 4 + 12 * (STRIPS // 2)
                    turn(STRIPS - 1)
                    down(c, 0, STRIPS - 1, True)
                    gate_rows(a["mod"] + 2)
                elif kind == "mid1":
                    m = mid1_n[0]
                    mid1_n[0] += 1
                    widths = [512, 512, 512, D_IN - 1536]
                    for s in range(4):
                        for u in range(4):
                            n = n0 + 4 * s + u
                            strip_unit(n % RING, n + 1, u, u == 3, (2 * s, 2 * s + 1), widths[s])
                    pe.wait_ge(S("lat_ready"), m + 1)
                    transposes(lat, 3)
                    pe.wait_ge(S("hlo_done"), tr[0])
                    for u in range(2):
                        n = n0 + 16 + u
                        strip_unit(n % RING, n + 1, 0, True, (2 * u, 2 * u + 1), 288)
                    for u in range(2):
                        n = n0 + 18 + u
                        pe.wait_ge(S("lo_done"), n + 1)
                        for t in range(NT):
                            ins = products(bank[4 + 2 * u + t][:, 0:384], 2, t, whi[:, n % RING, 0:384], wlo[:, n % RING, 0:384], True, True)
                        ins.then_inc(S("mm_done"), 1)
                    pe.wait_ge(S("heads_normed"), m + 1)
                    pe.wait_ge(S("up_copied0"), m + 1)
                    sources = [[qk1[:, t, h, :] for t in range(NT)] for h in range(12)]
                    sources += [[proj[:, t, O_WQ + P * j:O_WQ + P * (j + 1)] for t in range(NT)] for j in range(3)]
                    sources += [[kdup[:, t, j].rearrange("p r n -> p (r n)") for t in range(NT)] for j in range(WKV)]
                    sources += [[proj[:, t, O_SB + P * j:O_SB + P * (j + 1)] for t in range(NT)] for j in range(4)]
                    for g in range(11):
                        if g >= 4:
                            pe.wait_ge(S("qkT_copied_act" if g % 2 else "qkT_copied_dve"), (5 if g % 2 else 6) * m + (g - 4) // 2 + 1)
                        for k, src in enumerate(sources[2 * g:2 * g + 2]):
                            for t in range(NT):
                                rows_out = MQK if g < 6 else P
                                ins = T.transpose(bank[g % 4][0:rows_out, 256 * k + P * t:256 * k + P * (t + 1)], src[t], ident)
                        ins.then_inc(S("qkT_ready"), 1)
                    pe.wait_ge(S("qkT_copied_dve"), 6 * (m + 1))
                    pe.wait_ge(S("qkT_copied_act"), 5 * (m + 1))

                    def head(h):
                        if h < MH:
                            return mlaT[0:MQK, h, :], mlaT[0:MQK, MH + h, :], [kv[:, t, h, 64:128] for t in range(NT)]
                        w = h - MH if h < 12 else h - 12
                        r0 = 64 * (w % 2)
                        if h < 12:
                            q, k, v = w // 2, 3 + w // 3, O_WV + 64 * (w // 3)
                        else:
                            q, k, v = 5 + w // 2, 7 + w // 2, O_SB + 512 + 64 * w
                        return pairT[r0:r0 + 64, q, :], pairT[r0:r0 + 64, k, :], [proj[:, t, v:v + 64] for t in range(NT)]

                    def pv(h, probs):
                        v = head(h)[2]
                        c = slice(64 * (h % 8), 64 * (h % 8 + 1))
                        b = 4 + 2 * (h // 8)
                        T.matmul(bank[b][:, c], probs[:, 0:P], v[0], start=True, stop=True)
                        T.matmul(bank[b + 1][:, c], probs[:, P:2 * P], v[0], start=True, stop=False)
                        T.matmul(bank[b + 1][:, c], probs[:, 2 * P:3 * P], v[1], start=False, stop=True).then_inc(S("pv_done"), 1)

                    for i in range(14):
                        if i < 12:
                            q, k, _ = head(i)
                            if i >= 2:
                                pe.wait_ge(S("max_ready"), 12 * m + i - 1)
                            T.matmul(bank[i % 2][:, 0:P], q[:, 0:P], k[:, 0:P], start=True, stop=True)
                            T.matmul(bank[i % 2][:, P:384], q[:, P:SEQ], k, start=True, stop=True).then_inc(S("scores_ready"), 1)
                        if 1 <= i < 13:
                            h = i - 1
                            pe.wait_ge(S("probs_ready"), 12 * m + h + 1)
                            if h >= 2:
                                pe.wait_ge(S("pt_copied"), 12 * m + h - 1)
                            for j in range(3):
                                ins = T.transpose(bank[2 + h % 2][:, P * j:P * (j + 1)], sc_t[:, h % 2, P * j:P * (j + 1)], ident)
                            ins.then_inc(S("probsT_ready"), 1)
                        if i >= 2:
                            h = i - 2
                            pe.wait_ge(S("pt_copied"), 12 * m + h + 1)
                            pv(h, pt_t[:, h % 2, :])
                    for i in range(SH + 2):
                        if i < SH:
                            q, k, _ = head(12 + i)
                            if i >= 2:
                                pe.wait_ge(S("absz_ready"), SH * m + i - 1)
                            else:
                                pe.wait_ge(S("max_ready"), 12 * (m + 1))
                            T.matmul(bank[i % 2][:, 0:SEQ], k[:, 0:P], q, start=True, stop=True)
                            T.matmul(bank[i % 2][:, SEQ:384], k[:, P:SEQ], q[:, P:SEQ], start=True, stop=True).then_inc(S("scores_ready"), 1)
                        if 1 <= i <= SH:
                            h = i - 1
                            pe.wait_ge(S("stick_ready"), SH * m + h + 1)
                            if h >= 2:
                                pe.wait_ge(S("zs_ready"), SH * m + h - 1)
                            b, u = bank[2 + h % 2], pt_t[:, h % 2, :]
                            T.matmul(b[:, 0:P], tri, u[:, 0:P], start=True, stop=True)
                            T.matmul(b[:, P:2 * P], tri, u[:, P:2 * P], start=True, stop=False)
                            T.matmul(b[:, P:2 * P], ones, u[:, 2 * P:3 * P], start=False, stop=True)
                            T.matmul(b[:, 2 * P:3 * P], tri, u[:, 2 * P:3 * P], start=True, stop=True).then_inc(S("stick_sum"), 1)
                        if i >= 2:
                            h = i - 2
                            pe.wait_ge(S("sb_probs"), SH * m + h + 1)
                            pv(12 + h, pt_t[:, h % 2, :])
                    pe.wait_ge(S("mix_ready"), m + 1)
                    transposes(mix, KD)
                    pe.wait_ge(S("hlo_done"), tr[0])
                    for u in range(8):
                        n = n0 + 20 + u
                        rows_unit(n % RING, n + 1, u, u == 0, u == 7, hhi, hlo)
                    gate_rows(a["mod"] + 2)
                else:
                    m = mid2_n[0]
                    mid2_n[0] += 1
                    by_dve = [0, 1, 2, 3, 6]

                    def copied(s):
                        pe.wait_ge(S("strip2_copied0"), 11 * m + s + 1)
                        if s in by_dve:
                            pe.wait_ge(S("strip2_copied1"), 5 * m + by_dve.index(s) + 1)

                    def strip(s):
                        if s >= 3:
                            copied(s - 3)
                        for u in range(4):
                            n = n0 + 4 * s + u
                            strip_unit(n % RING, n + 1, u, u == 3, (2 * (s % 3), 2 * (s % 3) + 1), 512)

                    for s in range(4):
                        strip(s)
                    pe.wait_ge(S("rope2_done"), m + 1)
                    for g in range(4):
                        if g >= 2:
                            pe.wait_ge(S("qkT2_copied_act" if g % 2 else "qkT2_copied_dve"), 2 * m + 1)
                        for k in range(2):
                            for t in range(NT):
                                j = 2 * g + k
                                ins = T.transpose(bank[6 + g % 2][:, 256 * k + P * t:256 * k + P * (t + 1)], qk2[:, t, P * j:P * (j + 1)], ident)
                        ins.then_inc(S("qkT2_ready"), 1)
                    for s in range(4, 7):
                        strip(s)
                    copied(6)
                    pe.wait_ge(S("qkT2_copied_dve"), 2 * (m + 1))
                    pe.wait_ge(S("qkT2_copied_act"), 2 * (m + 1))
                    for i in range(RH + 1):
                        if i < RH:
                            r0 = 64 * (i % 2)
                            q, k = qkT2[r0:r0 + 64, i // 2, :], qkT2[r0:r0 + 64, 4 + i // 2, :]
                            if i >= 2:
                                pe.wait_ge(S("ret_probs"), RH * m + i - 1)
                            T.matmul(bank[6 + i % 2][:, 0:SEQ], k[:, 0:P], q, start=True, stop=True)
                            T.matmul(bank[6 + i % 2][:, SEQ:384], k[:, P:SEQ], q[:, P:SEQ], start=True, stop=True).then_inc(S("ret_scores"), 1)
                        if i >= 1:
                            h = i - 1
                            pe.wait_ge(S("ret_probs"), RH * m + h + 1)
                            pr = sc_t[:, h % 2, :]
                            c = slice(RV * (h % 4), RV * (h % 4 + 1))
                            v0, v1 = (v2[:, t, RV * h:RV * (h + 1)] for t in range(NT))
                            T.matmul(bank[h // 4][:, c], pr[:, 0:P], v0, start=True, stop=True)
                            T.matmul(bank[2 + h // 4][:, c], pr[:, P:2 * P], v0, start=True, stop=False)
                            T.matmul(bank[2 + h // 4][:, c], pr[:, 2 * P:3 * P], v1, start=False, stop=True).then_inc(S("ret_pv"), 1)
                    pe.wait_ge(S("ret_taken"), m + 1)
                    for s in range(7, 11):
                        strip(s)
                    pe.wait_ge(S("ret_ready"), m + 1)
                    for s in range(8, 11):
                        copied(s)
                    transposes(ret, KD)
                    pe.wait_ge(S("hlo_done"), tr[0])
                    for u in range(8):
                        n = n0 + 44 + u
                        rows_unit(n % RING, n + 1, u, u == 0, u == 7, hhi, hlo)
                    for g in range(4):
                        b, c0 = bank[6 + g // 2], 256 * (g % 2)
                        w = con2[:, C2_POOL + 384 * g:C2_POOL + 384 * (g + 1)]
                        s0, s1 = (p2[:, t, P * g:P * (g + 1)] for t in range(NT))
                        T.matmul(b[:, c0:c0 + P], s0, w[:, 0:P], start=True, stop=True)
                        T.matmul(b[:, c0 + P:c0 + 2 * P], s0, w[:, P:2 * P], start=True, stop=False)
                        ins = T.matmul(b[:, c0 + P:c0 + 2 * P], s1, w[:, 2 * P:3 * P], start=False, stop=True)
                        if g % 2:
                            ins.then_inc(S("pool_ready"), 1)
                    pe.wait_ge(S("plo_done"), 2 * (m + 1))
                    for u in range(2):
                        n = n0 + 52 + u
                        pe.wait_ge(S("lo_done"), n + 1)
                        for k in range(2):
                            g = 2 * u + k
                            o = bank[TRB[tr[0] % 4]][:, 256 * k:256 * (k + 1)]
                            wh, wl = (w[:, n % RING, P * k:P * (k + 1)] for w in (whi, wlo))
                            T.matmul(o, wh, hhi[:, g, :], start=True, stop=False)
                            T.matmul(o, wh, hlo[:, g, :], start=False, stop=False)
                            ins = T.matmul(o, wl, hhi[:, g, :], start=False, stop=True)
                        ins.then_inc(S("mm_done"), 1)
                        tr[0] += 1
                    pe.wait_ge(S("ret_gated"), m + 1)
                    pe.wait_ge(S("hlo_done"), tr[0])
                    for u in range(4):
                        n = n0 + 54 + u
                        rows_unit(n % RING, n + 1, 4 + u, u == 0, u == 3, hhi, hlo)
                    pe.wait_ge(S("merged_ready"), m + 1)
                    transposes(gates, KD)
                    pe.wait_ge(S("hlo_done"), tr[0])
                    for u in range(8):
                        n = n0 + 58 + u
                        rows_unit(n % RING, n + 1, u, u == 0, u == 7, hhi, hlo)
                    gate_rows(a["mod"] + 2)


INPUTS = ["x", "c", "positions", "rel_bias", "norm_g", "w_mod", "b_mod", "w_ffn1_gu", "w_ffn1_down", "w_in", "q_a_norm",
          "kv_a_norm", "w_uq", "w_ukv", "mla_q_norm", "mla_k_norm", "swa_q_norm", "swa_k_norm", "sinks", "out_norm",
          "w_out", "w_ffn2_gu", "w_ffn2_down", "c_2", "w_ada_2", "b_ada_2", "norm1_2", "w_in_2", "w_ret_o_2",
          "w_pool_grp_2", "pool_scale_2", "w_pool_o_2", "w_out_2", "norm2_2", "w_ffn_in_2", "w_ffn_out_2", "final_norm_2"]


def kernel(**inputs):
    import concourse.bacc as bacc
    from concourse.bass_utils import run_bass_kernel_spmd

    nc = bacc.Bacc("TRN2", target_bir_lowering=False, num_devices=1)
    arrays, A = {}, {}
    con, con2 = constants()
    for name, a in [(k, inputs[k]) for k in INPUTS] + [("con", con), ("con2", con2)]:
        a = np.ascontiguousarray(a)
        arrays["in_" + name] = a
        A[name] = nc.dram_tensor("in_" + name, a.shape, mybir.dt.from_np(a.dtype), kind="ExternalInput").ap()
    out = nc.dram_tensor("out_0", (1, SEQ, D), F32, kind="ExternalOutput").ap()
    build(nc, A, out)
    r = run_bass_kernel_spmd(nc, [arrays], core_ids=[0])
    return r.results[0]["out_0"]
```

```python
from contextlib import ExitStack
import math

import numpy as np

import concourse.bass as bass
from concourse import mybir

F32 = mybir.dt.float32
F32R = mybir.dt.float32r
I32 = mybir.dt.int32
BF16 = mybir.dt.bfloat16
ALU = mybir.AluOpType
ACT = mybir.ActivationFunctionType
AX = mybir.AxisListType.X

P = 128
SEQ = 256
NT = SEQ // P
D = 1024
KD = D // P
DFF = 2816
DEPTH = 2
EPS = 1e-6

MH, MQK, MNOPE, MROPE, MV = 6, 96, 64, 32, 64
QL, KVL = 256, 128
WH, WKV, HD = 6, 2, 64
SH = 4
D_IN = QL + KVL + MROPE + (WH + 2 * WKV) * HD + 3 * SH * HD
O_CKV, O_KPE = QL, QL + KVL
O_WQ = O_KPE + MROPE
O_WK = O_WQ + WH * HD
O_WV = O_WK + WKV * HD
O_SB = O_WV + WKV * HD
NBUCKET, MAXDIST = 32, 128
MASKED = -1e30

RH, RQK, RV = 8, 64, 128
POOLW = (2, 4, 8, 16)
D_IN2 = 2 * RH * RQK + 2 * RH * RV + 512 + 2 * D

SLOT = 1024
RING = 6
STRIPS = DFF // 256
UNITS_FFN = 4 * STRIPS + 2 * STRIPS
UNITS_MID1 = 16 + 2 + 2 + 8
UNITS_MID2 = 44 + 8 + 2 + 4 + 8
MOD_RING = 4

MOD_FIRST = [0, 9, 18, 24]
N_MOD = 30

MOD_START = [(("w_mod", 0), 0, 2)]
MOD_BESIDE = [[(("w_mod", 0), 2, 8)],
              [(("w_mod", 0), 8, 9), (("w_mod", 1), 0, 4)],
              [(("w_mod", 1), 4, 9)],
              [(("w_ada_2", 0), 0, 5)],
              [(("w_ada_2", 0), 5, 6), (("w_ada_2", 1), 0, 5)],
              [(("w_ada_2", 1), 5, 6)]]
MOD_PLAN = [(2, 3), (None, 8), (None, 13), (None, 18), (23, 24), (29, None)]

C_ID, C_TRI, C_ONES = 0, 128, 256
C_MASKC, C_MASKW, C_MASKS = 384, 768, 1152
C_MASKA = 1536
C_FREQ = 1920
C_ROPE2 = C_FREQ + 16
C_THR = C_ROPE2 + 4 * 32
C_END = C_THR + 1
C2_DECAY, C2_POOL = 0, RH * 256
C2_END = C2_POOL + 4 * 384

A_T = 0
A_S = 3072
A_X = 4608
A_MOD = A_X + 2048
A_BIAS = A_MOD + 4096
A_PROJ = A_X
A_QK = A_PROJ + NT * D_IN
A_KV = A_QK + NT * 2 * MH * MQK
A_T2 = A_KV + NT * MH * 128
A_KDUP = A_T2 + 9 * 256
A_END1 = A_KDUP + 768
A_QK2 = A_X
A_V2 = A_QK2 + 2048
A_RET = A_V2 + 2048
A_P2 = A_RET + 2048
A_C2 = A_P2 + 1024
A_END = max(A_END1, A_C2 + C2_END)


def bucket_thresholds():
    n = np.arange(0, MAXDIST + 1)
    half = NBUCKET // 2
    large = half + (np.log(np.maximum(n, 1).astype(np.float32) / half) / math.log(MAXDIST / half)
                    * (NBUCKET - half)).astype(np.int32)
    b = np.where(n < half, n, np.minimum(large, NBUCKET - 1))
    return [int(np.argmax(b >= k)) for k in range(NBUCKET)]


def constants():
    c = np.zeros((P, C_END), np.float32)
    i = np.arange(P)
    row, col = i[:, None], i[None, :]
    c[:, C_ID:C_ID + P] = row == col
    c[:, C_TRI:C_TRI + P] = row >= col
    c[:, C_ONES:C_ONES + P] = 1.0
    causal = np.where(col <= row, 0.0, MASKED)
    c[:, C_MASKC:C_MASKC + P] = causal
    c[:, C_MASKC + 2 * P:C_MASKC + 3 * P] = causal
    c[:, C_MASKW:C_MASKW + P] = causal
    c[:, C_MASKW + P:C_MASKW + 2 * P] = np.where(col > row, 0.0, MASKED)
    c[:, C_MASKW + 2 * P:C_MASKW + 3 * P] = causal
    c[:, C_MASKS:C_MASKS + P] = row < col
    c[:, C_MASKS + P:C_MASKS + 2 * P] = 1.0
    c[:, C_MASKS + 2 * P:C_MASKS + 3 * P] = row < col
    c[:, C_MASKA:C_MASKA + 384] = np.where(c[:, C_MASKS:C_MASKS + 384] > 0, 0.0, MASKED)
    half = MROPE // 2
    c[:, C_FREQ:C_FREQ + half] = np.float32(10000.0) ** (-np.arange(half, dtype=np.float32) / np.float32(half))
    thr = bucket_thresholds()
    thr[0] = -2.0 ** 30
    c[:, C_THR] = np.tile(np.array(thr, np.float32), P // NBUCKET)
    half = RQK // 2
    f = np.float32(10000.0) ** (-np.arange(half, dtype=np.float32) / np.float32(half))
    ang = (np.arange(SEQ, dtype=np.float32)[:, None] * f[None, :]).astype(np.float64).reshape(NT, P, half)
    c[:, C_ROPE2:C_ROPE2 + 64] = np.cos(ang).transpose(1, 0, 2).reshape(P, 64)
    c[:, C_ROPE2 + 64:C_ROPE2 + 128] = np.sin(ang).transpose(1, 0, 2).reshape(P, 64)

    c2 = np.zeros((P, C2_END), np.float32)
    q = np.arange(SEQ)[None, :]
    for h in range(RH):
        g = np.log1p(-(2.0 ** (-5.0 - h)))
        d = q - row
        c2[:, C2_DECAY + 256 * h:C2_DECAY + 256 * (h + 1)] = np.where(d >= 0, np.exp(g * np.maximum(d, 0)), 0.0) * RQK ** -0.5
    for n, w in enumerate(POOLW):
        t = np.arange(SEQ)
        m = ((t[:, None] <= t[None, :]) & (t[None, :] - t[:, None] < w)) / np.minimum(t + 1.0, w)[None, :] - np.eye(SEQ)
        c2[:, C2_POOL + 384 * n:C2_POOL + 384 * n + 256] = m[0:P, :]
        c2[:, C2_POOL + 384 * n + 256:C2_POOL + 384 * (n + 1)] = m[P:, P:]
    return c, c2


V_C1, V_C2 = 240, 248
V_NORMG = 256
V_N1, V_N2, V_ON = V_NORMG + 48, V_NORMG + 64, V_NORMG + 80
V_QA, V_KVA, V_PS = V_NORMG + 96, V_NORMG + 100, V_NORMG + 102
V_ROWS2 = V_PS + 8 - 256
TRB = (6, 7, 4, 5)
TRB_FFN = (6, 0, 2, 3)
TRB_LATENT = (0, 1)
TRB_MERGED = (4, 6, 5, 7)
PAIR_GROUPS = ((5, 2), (7, 2), (0, 2), (2, 2), (4, 1))
STRIP_BANKS = [2 * (s % 3) for s in range(7)] + [4, 6, 0, 2]
PREFETCH = 4


def need(eng, sem, value):
    if not isinstance(value, int) or value > 0:
        eng.wait_ge(sem, value)


def build(nc, A, out):
    with ExitStack() as ctx:
        def sb(name, shape, dt=F32):
            return ctx.enter_context(nc.sbuf_tensor(name, shape, dt))

        sems = {}

        def S(name):
            if name not in sems:
                sems[name] = ctx.enter_context(nc.semaphore(name))
            return sems[name]

        raw = sb("weights_raw", [P, RING, SLOT])
        whi = sb("weights_hi", [P, RING, SLOT], F32R)
        wlo = sb("weights_lo", [P, RING, SLOT], F32R)
        hhi = sb("hT_hi", [P, KD, SEQ], F32R)
        hlo = sb("hT_lo", [P, KD, SEQ], F32R)
        ahi = sb("actT_hi", [P, 2, SEQ], F32R)
        alo = sb("actT_lo", [P, 2, SEQ], F32R)
        x = sb("x", [P, NT, D])
        con = sb("con", [P, C_END])
        bias = sb("window_bias", [P, WH, 384])
        modacc = sb("mod_acc", [P, D])
        modc = sb("mod_cols", [P, 8 * N_MOD])
        vec = sb("vectors", [P, 3 * P])
        silc = sb("silu_cond", [P, 16])
        gq96 = sb("gain_mla", [P, 2, MQK])
        gw64 = sb("gain_window", [P, 2, HD])
        sink = sb("sinks_row", [P, WH])
        rope1 = sb("rope_first", [P, 2, NT, 16])
        stat = sb("stat", [P, 96])
        sclA = sb("scale_cols", [P, 8])
        nmax = sb("neg_max", [P, 24])
        rsum = sb("row_sums", [P, 24])
        table_col = sb("table_col", [P, 1])
        esink = sb("sink_exp_t", [P, 12])[:, :]
        latg = sb("latent_gains", [P, 3])
        kvhi = sb("latent_kv_hi", [P, 1, SEQ], F32R)
        kvlo = sb("latent_kv_lo", [P, 1, SEQ], F32R)
        zero_hi = sb("zero", [P, P], F32R)
        arena = sb("arena", [P, A_END])
        bank = [ctx.enter_context(nc.psum_tensor(f"bank{i}", [P, 512], F32)) for i in range(8)]
        GB = (4, 5)
        ATB, MB = 6, 7

        ident = con[:, C_ID:C_ID + P]
        tri = con[:, C_TRI:C_TRI + P]
        ones = con[:, C_ONES:C_ONES + P]
        ones_col = con[:, C_ONES:C_ONES + 1]

        def ar(off, n):
            return arena[:, off:off + n]

        hf = ar(A_T, 1024).rearrange("p (r n) -> p r n", r=2)
        act_t = ar(A_T + 1024, 512).rearrange("p (t n) -> p t n", t=NT)
        sg_t = ar(A_T + 1536, 512).rearrange("p (t n) -> p t n", t=NT)
        gate_b = ar(A_S, 1024)
        modw = ar(A_MOD, MOD_RING * D).rearrange("p (r n) -> p r n", r=MOD_RING)
        xn = ar(A_X, 2048).rearrange("p (t n) -> p t n", t=NT)
        pos_i = ar(A_BIAS, 2).bitcast(I32)
        pos_q = ar(A_BIAS + 2, SEQ).bitcast(I32)
        pos_k = ar(A_BIAS + 258, 64).bitcast(I32).rearrange("p (t n) -> p t n", t=NT)
        relb, relb1 = ar(A_BIAS + 322, WH), ar(A_BIAS + 328, WH)
        posf_i, posf_q = ar(A_BIAS + 334, 2), ar(A_BIAS + 336, SEQ)
        posf_k = ar(A_BIAS + 592, 64).rearrange("p (t n) -> p t n", t=NT)
        bstep, ang = ar(A_BIAS + 656, WH), ar(A_BIAS + 662, 32).rearrange("p (t n) -> p t n", t=NT)
        bparts = ar(A_BIAS + 760, 10).bitcast(BF16)[:, 0:3 * WH].rearrange("p (q h) -> p q h", q=3)
        turns = ar(A_BIAS + 694, 64).rearrange("p (a t n) -> p a t n", a=2, t=NT)
        reached = ar(A_T, 1024).bitcast(BF16).rearrange("p (k q) -> p k q", k=16)
        proj = ar(A_PROJ, NT * D_IN).rearrange("p (t n) -> p t n", t=NT)
        qk1 = ar(A_QK, NT * 12 * MQK).rearrange("p (t h n) -> p t h n", t=NT, h=12)
        mix = ar(A_QK, 2048).rearrange("p (t n) -> p t n", t=NT)
        kv = ar(A_KV, NT * MH * 128).rearrange("p (t h n) -> p t h n", t=NT, h=MH)
        mlaT = ar(A_T, 12 * SEQ).rearrange("p (h n) -> p h n", h=12)
        pairT = ar(A_T2, 9 * SEQ).rearrange("p (h n) -> p h n", h=9)
        kdup = ar(A_KDUP, NT * 256).rearrange("p (t k r n) -> p t k r n", t=NT, k=WKV, r=2)
        lat = ar(A_T2, NT * 384).rearrange("p (t n) -> p t n", t=NT)
        sc_t = ar(A_S, 768).rearrange("p (r n) -> p r n", r=2)
        pt_t = ar(A_S + 768, 768).rearrange("p (r n) -> p r n", r=2)
        qk2 = ar(A_QK2, 2048).rearrange("p (t n) -> p t n", t=NT)
        v2 = ar(A_V2, 2048).rearrange("p (t n) -> p t n", t=NT)
        gates = ar(A_QK2, 4096).rearrange("p (t n) -> p t n", t=NT)
        ret = ar(A_RET, 2048).rearrange("p (t n) -> p t n", t=NT)
        p2 = ar(A_P2, 1024).rearrange("p (t n) -> p t n", t=NT)
        qkT2 = ar(A_T, 2048).rearrange("p (h n) -> p h n", h=8)
        con2 = ar(A_C2, C2_END)

        def pool_parts(w, n, g):
            return w[:, (n + g) % RING, 256:768]


        n = RING
        phases = []
        for blk in range(2):
            for l in range(DEPTH):
                m0 = MOD_FIRST[2 * blk + l]
                if blk == 0:
                    phases.append(("ffn", n, dict(f=2 * l, gu=A["w_ffn1_gu"][l], down=A["w_ffn1_down"][l], g=V_NORMG + 24 * l, mod=m0, half=0.5)))
                    n += UNITS_FFN
                    phases.append(("mid1", n, dict(l=l, g=V_NORMG + 24 * l + 8, mod=m0 + 3)))
                    n += UNITS_MID1
                    phases.append(("ffn", n, dict(f=2 * l + 1, gu=A["w_ffn2_gu"][l], down=A["w_ffn2_down"][l], g=V_NORMG + 24 * l + 16, mod=m0 + 6, half=0.5)))
                    n += UNITS_FFN
                else:
                    phases.append(("mid2", n, dict(l=l, g=V_N1 + 8 * l, mod=m0)))
                    n += UNITS_MID2
                    phases.append(("ffn", n, dict(f=4 + l, gu=A["w_ffn_in_2"][l], down=A["w_ffn_out_2"][l], g=V_N2 + 8 * l, mod=m0 + 3, half=1.0)))
                    n += UNITS_FFN

        def copy_mla(copy, g):
            return copy(mlaT[0:MQK, 2 * g:2 * g + 2, :].rearrange("p h n -> p (h n)"), bank[g % 4][0:MQK, :])

        def sb_z(h):
            return proj[:, h // 2, O_WQ * (h % 2):O_WQ * (h % 2) + 384]

        sb_u_pairs = [ar(A_KDUP, 768), modacc[:, 0:768]]

        def sb_u(h):
            return sb_u_pairs[h // 2][:, 384 * (h % 2):384 * (h % 2 + 1)]

        total_units = n

        def parts_at(tiles, c, w):
            return tiles[c // 2][:, c % 2:c % 2 + w, :].rearrange("p k n -> p (k n)")

        def hT_tiles(tile, dst0):
            return [tile[:, dst0 + c:dst0 + c + 2, :] for c in range(0, KD - dst0, 2)]

        latent_hi, latent_lo = [ahi, kvhi], [alo, kvlo]

        rows = ar(A_X, 3 * P).rearrange("p (t n) -> p t n", t=3)

        def load_rows(eng, first, end):
            vectors = [
                (0, 0, A["b_mod"][0].rearrange("(r n) -> r n", n=P), 72),
                (0, 72, A["b_mod"][1].rearrange("(r n) -> r n", n=P)[0:56], 56),
                (1, 0, A["b_mod"][1].rearrange("(r n) -> r n", n=P)[56:72], 16),
                (1, 16, A["b_ada_2"].rearrange("l (r n) -> (l r) n", n=P), 96),
                (1, V_C1 - P, A["c"].rearrange("a (r n) -> (a r) n", n=P), 8),
                (1, V_C2 - P, A["c_2"].rearrange("a (r n) -> (a r) n", n=P), 8),
                (2, 0, A["norm_g"].rearrange("l i (r n) -> (l i r) n", n=P), 48),
                (2, V_N1 - 256, A["norm1_2"].rearrange("l (r n) -> (l r) n", n=P), 16),
                (2, V_N2 - 256, A["norm2_2"].rearrange("l (r n) -> (l r) n", n=P), 16),
                (2, V_ON - 256, A["out_norm"].rearrange("l (r n) -> (l r) n", n=P), 16),
                (2, V_QA - 256, A["q_a_norm"].rearrange("l (r n) -> (l r) n", n=P), 4),
                (2, V_KVA - 256, A["kv_a_norm"].rearrange("l (r n) -> (l r) n", n=P), 2),
                (2, V_PS - 256, A["pool_scale_2"].rearrange("l (r n) -> (l r) n", n=P), 8),
            ]
            for tile, at, src, r in vectors[first:end]:
                eng.dma_start(rows[at:at + r, tile, :], src).then_inc(S("rows_loaded"), 16)

        block = ctx.enter_context(nc.Block())

        @block.sync
        def _(sp):
            load_rows(sp, 0, 6)
            sp.dma_start(con[:, :], A["con"]).then_inc(S("const_loaded"), 16)
            sp.dma_start(x[:, :, :], A["x"][0].rearrange("(t p) n -> p t n", p=P)).then_inc(S("x_loaded"), 16)
            sp.dma_start(pos_i, A["positions"][0].rearrange("(t p) -> p t", p=P), allow_slow_non_contiguous=True).then_inc(S("pos_loaded"), 16)
            sp.dma_start(pos_q, A["positions"][0].partition_broadcast(P)).then_inc(S("pos_loaded"), 16)
            sp.wait_ge(S("zero_ready"), 2)
            for g in range(4):
                r = slice(NBUCKET * g, NBUCKET * (g + 1))
                sp.dma_start(pos_k[r], A["positions"][0].rearrange("(t g n) -> g t n", t=NT, g=4)[g].partition_broadcast(NBUCKET)).then_inc(S("pos_loaded"), 16)
                sp.dma_start(relb[r], A["rel_bias"]).then_inc(S("pos_loaded"), 16)
                sp.dma_start(relb1[NBUCKET * g + 1:NBUCKET * (g + 1)], A["rel_bias"][0:NBUCKET - 1]).then_inc(S("pos_loaded"), 16)
            for dst, src in ((gq96[:, 0, :], "mla_q_norm"), (gq96[:, 1, :], "mla_k_norm"),
                             (gw64[:, 0, :], "swa_q_norm"), (gw64[:, 1, :], "swa_k_norm"), (sink[:, :], "sinks")):
                sp.dma_start(dst, A[src][0].partition_broadcast(P)).then_inc(S("gains_loaded"), 16)

            sp.wait_ge(S("mod_used"), 12)

            def gu_pair(slot, wait, w, k0, col):
                sp.wait_ge(S("lo_done"), wait)
                for half in range(2):
                    src = w.rearrange("(k p) (s n) -> p k s n", p=P, s=2)[:, k0:k0 + 4, half, bass.ds(col, 256)]
                    dst = raw[:, slot:slot + 2, :].rearrange("p u (k s n) -> p (u k) s n", k=2, s=2)[:, :, half, :]
                    sp.dma_start(dst, src).then_inc(S(f"w_loaded{slot // 2}"), 16)

            def rows_pair(slot, wait, w, k0):
                sp.wait_ge(S("lo_done"), wait)
                for u in range(2):
                    src = w[bass.ds(k0 + u * P, P), :]
                    sp.dma_start(raw[:, slot + u, :], src).then_inc(S(f"w_loaded{slot // 2}"), 16)

            def gu_strip(n0, i6, w, col):
                for h in range(2):
                    gu_pair((n0 + 2 * h) % RING, i6 + n0 + 2 * h - RING + 2, w, 4 * h, col)

            def strip_pairs(n0, w, k_chunks, col, width):
                wv = w.rearrange("(k p) n -> p k n", p=P)
                for u in range(k_chunks // 2):
                    nn = n0 + u
                    if u % 2 == 0:
                        sp.wait_ge(S("lo_done"), nn - RING + 2)
                    dst = raw[:, nn % RING, 0:2 * width].rearrange("p (k n) -> p k n", k=2)
                    sp.dma_start(dst, wv[:, 2 * u:2 * u + 2, col:col + width]).then_inc(S(f"w_loaded{nn % RING // 2}"), 16)

            for kind, n0, a in phases:
                if kind == "ffn":
                    gu_strip(n0, 0, a["gu"], 0)
                    with sp.Fori(0, STRIPS // 2) as i:
                        for s in range(2):
                            c = n0 + 4 + 6 * s
                            gu_strip(c, 12 * i, a["gu"], 512 * i + 256 * (s + 1))
                            rows_pair((c + 4) % RING, 12 * i + c + 4 - RING + 2, a["down"], 512 * i + 256 * s)
                    c = n0 + 4 + 12 * (STRIPS // 2)
                    rows_pair(c % RING, c - RING + 2, a["down"], 256 * (STRIPS - 1))
                elif kind == "mid1":
                    l = a["l"]
                    for s in range(3):
                        strip_pairs(n0 + 4 * s, A["w_in"][l], KD, 512 * s, 512)
                    strip_pairs(n0 + 12, A["w_in"][l], KD, 1536, D_IN - 1536)
                    nn = n0 + 16
                    sp.wait_ge(S("lo_done"), nn - RING + 2)
                    wv = A["w_uq"][l].rearrange("(k p) n -> p k n", p=P)
                    for u in range(2):
                        dst = raw[:, (nn + u) % RING, 0:576].rearrange("p (k n) -> p k n", k=2)
                        sp.dma_start(dst, wv[:, :, 288 * u:288 * (u + 1)]).then_inc(S(f"w_loaded{nn % RING // 2}"), 16)
                    nn = n0 + 18
                    sp.wait_ge(S("lo_done"), nn - RING + 2)
                    for u in range(2):
                        sp.dma_start(raw[:, (nn + u) % RING, 0:384], A["w_ukv"][l][:, 384 * u:384 * (u + 1)])\
                            .then_inc(S(f"w_loaded{nn % RING // 2}"), 16)
                    for k in range(0, KD, 2):
                        nn = n0 + 20 + k
                        rows_pair(nn % RING, nn - RING + 2, A["w_out"][l], P * k)
                else:
                    l = a["l"]
                    for s in range(11):
                        strip_pairs(n0 + 4 * s, A["w_in_2"][l], KD, 512 * s, 512)
                    for k in range(0, KD, 2):
                        if k == 4:
                            nn = n0 + 48
                            sp.wait_ge(S("lo_done"), nn - RING + 2)
                            for u in range(2):
                                dst = raw[:, (nn + u) % RING, 0:256].rearrange("p (g n) -> p g n", g=2)
                                sp.dma_start(dst, A["w_pool_grp_2"][l, 2 * u:2 * u + 2].rearrange("g p n -> p g n"))\
                                    .then_inc(S(f"w_loaded{nn % RING // 2}"), 16)
                        nn = n0 + 44 + k + (2 if k >= 4 else 0)
                        rows_pair(nn % RING, nn - RING + 2, A["w_ret_o_2"][l], P * k)
                    for k in range(0, 4, 2):
                        nn = n0 + 54 + k
                        rows_pair(nn % RING, nn - RING + 2, A["w_pool_o_2"][l], P * k)
                    for k in range(0, KD, 2):
                        nn = n0 + 58 + k
                        rows_pair(nn % RING, nn - RING + 2, A["w_out_2"][l], P * k)
            sp.wait_ge(S("x_done"), NT * (len(phases) + 1))
            sp.dma_start(gate_b, A["final_norm_2"].partition_broadcast(P)).then_inc(S("final_gain"), 16)
            for t in range(NT):
                sp.wait_ge(S("out_ready"), t + 1)
                sp.dma_start(out[0, t * P:(t + 1) * P, :], xn[:, t, :]).then_inc(S("out_stored"), 16)
            sp.wait_ge(S("out_stored"), 16 * NT)

        @block.gpsimd
        def _(pool):
            def mod_load(w, k, col, slot, wait):
                need(pool, S("mod_used"), wait)
                pool.dma_start(modw[:, slot, :], w[k * P:(k + 1) * P, bass.ds(col, D)]).then_inc(S(f"mod_loaded{slot}"), 16)

            m = 0
            f = 0
            for k, (kind, _, _) in enumerate([("start", 0, 0)] + phases):
                if kind == "mid1" or kind == "mid2":
                    continue
                need(pool, S("x_done"), NT * k if k > 1 else 0)
                for w, c0, c1 in (MOD_START if kind == "start" else MOD_BESIDE[f]):
                    if m == 0:
                        for c in range(c0, c1):
                            for q in range(KD):
                                mod_load(A[w[0]][w[1]], q, D * c, q % MOD_RING, 8 * c + q - MOD_RING + 1)
                    elif c1 - c0 == 1:
                        for q in range(KD):
                            mod_load(A[w[0]][w[1]], q, D * c0, q % MOD_RING, 8 * m + q - MOD_RING + 1)
                    else:
                        with pool.Fori(0, c1 - c0) as c:
                            for q in range(KD):
                                mod_load(A[w[0]][w[1]], q, D * c + D * c0, q % MOD_RING, 8 * c + 8 * m + q - MOD_RING + 1)
                    m += c1 - c0
                f += kind == "ffn"

        @block.scalar
        def _(act):
            seq = [0]

            def then(ins):
                seq[0] += 1
                ins.then_inc(S("act_step"), 1)
                act.wait_ge(S("act_step"), seq[0])

            def hi(slot, width, loaded, free):
                act.wait_ge(S(f"w_loaded{slot // 2}"), loaded)
                act.wait_ge(S("mm_done"), free)
                nc.scalar.activation(whi[:, slot, 0:width], raw[:, slot, 0:width], ACT.Copy).then_inc(S("hi_done"), 1)

            def hi_static(n, width):
                hi(n % RING, width, 32 * (n // RING), n - RING + 1)

            load_rows(act, 6, 13)
            act.wait_ge(S("vec_ready"), 1)
            nc.scalar.activation(silc[:, 0:8], vec[:, V_C1:V_C1 + 8], ACT.Silu)
            nc.scalar.activation(silc[:, 8:16], vec[:, V_C2:V_C2 + 8], ACT.Silu).then_inc(S("cond_ready"), 1)
            tr = [0]

            def norm_stage(k):
                for t in range(NT):
                    act.wait_ge(S("x_done"), NT * (k - 1) + t + 1)
                    ins = nc.scalar.activation(xn[:, t, :], x[:, t, :], ACT.Square, accum_out=stat[:, t:t + 1])
                ins.then_inc(S("ss_ready"), 1)
                act.wait_ge(S("ms_ready"), k)
                nc.scalar.activation(stat[:, 2:4], stat[:, 2:4], ACT.Sqrt).then_inc(S("rms_ready"), 1)
                act.wait_ge(S("rstd_ready"), k)
                for h in range(2):
                    c = slice(512 * h, 512 * (h + 1))
                    nc.scalar.activation(xn[:, 0, c], x[:, 0, c], ACT.Copy, scale=stat[:, 4:5]).then_inc(S("xn0_ready"), 1)

            def split_groups(dst0, chunks, tiles=None):
                for c in range(0, chunks, 2):
                    w = min(2, chunks - c) * SEQ
                    act.wait_ge(S("hf_ready"), tr[0] + 1)
                    nc.scalar.activation(parts_at(tiles or hT_tiles(hhi, dst0), c, w // SEQ),
                                         hf[:, tr[0] % 2, 0:w], ACT.Copy).then_inc(S("hhi_done"), 1)
                    tr[0] += 1

            ffn_n, x_n, o_n, mid1_n, mid2_n = [0], [0], [0], [0], [0]

            def gate_rows(half):
                x_n[0] += 1
                act.wait_ge(S("gate_rows"), x_n[0])
                for h in range(2):
                    ins = nc.scalar.activation(gate_b[:, 512 * h:512 * (h + 1)], bank[6 + h][:, :], ACT.Copy, scale=half)
                ins.then_inc(S("gate_ready"), 1)

            def rms_sqrt(name, ap):
                cnt[name] = cnt.get(name, 0) + 1
                act.wait_ge(S(name), cnt[name])
                nc.scalar.activation(ap, ap, ACT.Sqrt).then_inc(S(name + "_root"), 1)

            cnt = {}

            def prefetch(n):
                for u in range(PREFETCH if n < total_units else 0):
                    hi_static(n + u, SLOT)
                nc.scalar.activation(table_col[:, :], ones_col, ACT.Sqrt)

            norm_stage(1)
            prefetch(RING)
            act.wait_ge(S("angles_ready"), 1)
            r1 = rope1[:, :, :, :].rearrange("p a t n -> p (a t n)")
            nc.scalar.activation(r1, r1, ACT.Sin).then_inc(S("rope_ready"), 1)

            for kind, n0, a in phases:
                o_n[0] += 1
                if o_n[0] > 1:
                    norm_stage(o_n[0])
                split_groups(0, KD)
                if kind == "ffn":
                    f = ffn_n[0]
                    ffn_n[0] += 1

                    def silu(j, end):
                        act.wait_ge(S("mm_done"), end)
                        need(act, S("act_ready"), STRIPS * f + j)
                        for t in range(NT):
                            nc.scalar.activation(sg_t[:, t, :], bank[GB[t]][:, 0:256], ACT.Silu).then_inc(S("silu_done"), 1)

                    def act_hi(j, used):
                        act.wait_ge(S("actT_ready"), STRIPS * f + j + 1)
                        act.wait_ge(S("mm_done"), used)
                        nc.scalar.activation(ahi[:, :, :].rearrange("p k n -> p (k n)"), bank[ATB][:, :], ACT.Copy)\
                            .then_inc(S("ahi_done"), 1)

                    def units(c, i, lo_, hi_):
                        for u in range(lo_, hi_):
                            m = c + u
                            hi(m % RING, SLOT, 64 * i + 32 * (m // RING), 12 * i + m - RING + 1)

                    silu(0, n0 + 4)
                    with act.Fori(0, STRIPS // 2) as i:
                        for s in range(2):
                            c = n0 + 4 + 6 * s
                            units(c, i, 0, 4)
                            act_hi(2 * i + s, 12 * i + c)
                            units(c, i, 4, 6)
                            silu(2 * i + s + 1, 12 * i + c + 4)
                    c = n0 + 4 + 12 * (STRIPS // 2)
                    act_hi(STRIPS - 1, c)
                    units(c, 0, 0, 2)
                    gate_rows(a["half"])
                    prefetch(n0 + UNITS_FFN)
                elif kind == "mid1":
                    l = a["l"]
                    m = mid1_n[0]
                    mid1_n[0] += 1
                    if l > 0:
                        act.wait_ge(S("heads_normed"), 2 * l)
                        act.wait_ge(S("mix1_ready"), l)
                        for dst, src in ((gq96[:, 0, :], "mla_q_norm"), (gq96[:, 1, :], "mla_k_norm"),
                                         (gw64[:, 0, :], "swa_q_norm"), (gw64[:, 1, :], "swa_k_norm"), (sink[:, :], "sinks")):
                            act.dma_start(dst, A[src][l].partition_broadcast(P)).then_inc(S("gains_loaded"), 16)
                    widths = [512, 512, 512, D_IN - 1536]
                    for s in range(4):
                        for u in range(4 if s else 0):
                            hi_static(n0 + 4 * s + u, 2 * widths[s])
                        if s >= 1:
                            act.wait_ge(S("mm_done"), n0 + 4 * s)
                            nc.scalar.activation(proj[:, 0, 512 * (s - 1):512 * s], bank[2 * (s - 1)][:, :], ACT.Copy).then_inc(S("strip_copied0"), 1)
                        if s == 1:
                            act.wait_ge(S("strip_copied0"), 4 * m + 1)
                            act.wait_ge(S("strip_copied1"), 4 * m + 1)
                            at = A_QK + 1024
                            for t in range(NT):
                                for c0, c1, st in ((0, QL, 8 + t), (QL, O_KPE, 10 + t), (O_KPE, O_WQ, 28 + t)):
                                    ins = nc.scalar.activation(ar(at, c1 - c0), proj[:, t, c0:c1], ACT.Square, accum_out=stat[:, st:st + 1])
                                    at += c1 - c0
                            ins.then_inc(S("lat_sq"), 1)
                        if s == 2:
                            rms_sqrt("lat_ms", stat[:, 8:12])
                            act.wait_ge(S("strip_copied0"), 4 * m + 2)
                            act.wait_ge(S("strip_copied1"), 4 * m + 2)
                            sq = ar(A_QK, NT * 512).rearrange("p (t n) -> p t n", t=NT)
                            nc.scalar.activation(sq, proj[:, :, O_WQ:O_WV], ACT.Square).then_inc(S("sq_ready"), 1)
                    split_groups(0, 3, latent_hi)
                    rms_sqrt("win_ms", stat[:, 12:28])
                    hi_static(n0 + 16, 576)
                    hi_static(n0 + 17, 576)
                    act.wait_ge(S("mm_done"), n0 + 16)
                    nc.scalar.activation(proj[:, 0, 1536:D_IN], bank[6][:, 0:D_IN - 1536], ACT.Copy).then_inc(S("strip_copied0"), 1)
                    hi_static(n0 + 18, 384)
                    hi_static(n0 + 19, 384)
                    act.wait_ge(S("mm_done"), n0 + 20)
                    for u in range(2):
                        nc.scalar.activation(qk1[:, 0, 3 * u:3 * u + 3, :].rearrange("p h n -> p (h n)"), bank[2 * u][:, 0:288], ACT.Copy)
                        ins = nc.scalar.activation(kv[:, 0, 3 * u:3 * u + 3, :].rearrange("p h n -> p (h n)"), bank[4 + 2 * u][:, 0:384], ACT.Copy)
                    ins.then_inc(S("up_copied0"), 1)
                    act.wait_ge(S("up_copied1"), m + 1)
                    act.wait_ge(S("up_copied0"), m + 1)
                    sqq = ar(A_T, NT * 576).rearrange("p (t h n) -> p t h n", t=NT, h=MH)
                    sqk = ar(A_T + NT * 576, NT * 384).rearrange("p (t h n) -> p t h n", t=NT, h=MH)
                    for t in range(NT):
                        nc.scalar.activation(sqq[:, t], qk1[:, t, 0:MH, :], ACT.Square)
                        ins = nc.scalar.activation(sqk[:, t], kv[:, t, :, 0:64], ACT.Square)
                    ins.then_inc(S("sqh_ready"), 1)

                    def copy_pair(j):
                        act.wait_ge(S("pairT_ready"), 5 * m + j + 1)
                        at, w = PAIR_GROUPS[j]
                        nc.scalar.activation(pairT[:, at:at + w, :].rearrange("p h n -> p (h n)"), bank[j % 4][:, 0:256 * w], ACT.Copy)\
                            .then_inc(S("pairT_copied"), 1)

                    copy_pair(0)
                    copy_pair(1)
                    rms_sqrt("head_ms", stat[:, 32:56])
                    for j in range(2, 5):
                        copy_pair(j)
                    for h in range(SH):
                        act.wait_ge(S("sb_scores"), SH * m + h + 1)
                        nc.scalar.activation(sb_z(h), bank[4 + h][:, 0:384], ACT.Copy, scale=HD ** -0.5)
                        ins = nc.scalar.activation(sb_u(h), bank[4 + h][:, 0:384], ACT.Abs, scale=HD ** -0.5)
                    then(ins)
                    for u in sb_u_pairs:
                        ins = nc.scalar.activation(u, u, ACT.Exp, scale=-1.0)
                    then(ins)
                    for u in sb_u_pairs:
                        ins = nc.scalar.activation(u, u, ACT.Ln, bias=1.0)
                    ins.then_inc(S("sb_ln"), 1)
                    nc.scalar.activation(table_col[:, :], ones_col, ACT.Exp)
                    for g in range(1, 6, 2):
                        act.wait_ge(S("qkT_ready"), 6 * m + g + 1)
                        copy_mla(nc.scalar.copy, g).then_inc(S("qkT_copied_act"), 1)

                    def copy_probs(h):
                        act.wait_ge(S("probsT_ready"), 12 * m + h + 1)
                        if h >= 2:
                            act.wait_ge(S("pv_done"), 12 * m + h - 1)
                        nc.scalar.activation(pt_t[:, h % 2, :], bank[2 + h % 2][:, 0:384], ACT.Copy).then_inc(S("pt_copied"), 1)

                    for h in range(12):
                        k = 12 * m + h
                        act.wait_ge(S("max_ready"), k + 1)
                        r = h % 2
                        for b, (c0, c1) in enumerate(((0, P), (P, 3 * P))):
                            ins = nc.scalar.activation(sc_t[:, r, c0:c1], sc_t[:, r, c0:c1], ACT.Exp,
                                                       bias=nmax[:, 2 * h + b:2 * h + b + 1], accum_out=rsum[:, 2 * h + b:2 * h + b + 1])
                        ins.then_inc(S("probs_ready"), 1)
                        if h >= MH:
                            w = h - MH
                            nc.scalar.activation(esink[:, 2 * w:2 * w + 2], nmax[:, 2 * h:2 * h + 2], ACT.Exp, bias=sink[:, w:w + 1])\
                                .then_inc(S("sink_exp"), 1)
                        if h >= 1:
                            copy_probs(h - 1)
                        if 3 <= h < 3 + SH:
                            j = h - 3
                            act.wait_ge(S("zs_ready"), SH * m + j + 1)
                            nc.scalar.activation(sb_u(j), sb_z(j), ACT.Exp).then_inc(S("sb_probs"), 1)
                        if h >= 8:
                            hi_static(n0 + 20 + h - 8, SLOT)
                    nc.scalar.activation(table_col[:, :], ones_col, ACT.Sqrt)
                    copy_probs(11)

                    def square(at, g, t, src):
                        w = src.shape[-1]
                        return nc.scalar.activation(ar(A_T + 1024 + at, w), src, ACT.Square, accum_out=stat[:, 8 + 2 * g + t:9 + 2 * g + t])

                    act.wait_ge(S("heads_out"), 3 * m + 1)
                    for t in range(NT):
                        square(384 * t, 0, t, mix[:, t, 0:384])
                    act.wait_ge(S("pv_done"), 12 * (m + 1))
                    act.wait_ge(S("sb_pv_done"), SH * (m + 1))
                    for t in range(NT):
                        if t == 1:
                            act.wait_ge(S("heads_out"), 3 * m + 2)
                        nc.scalar.activation(mix[:, t, 768:1024], bank[6 + t][:, 256:512], ACT.Copy)
                        ins = square(768 + 256 * t, 2, t, bank[6 + t][:, 256:512])
                        if t == 0:
                            ins.then_inc(S("bank6_read"), 1)
                    act.wait_ge(S("heads_out"), 3 * m + 3)
                    for t in range(NT):
                        ins = square(1280 + 384 * t, 1, t, mix[:, t, 384:768])
                    ins.then_inc(S("sqm_ready"), 1)
                    rms_sqrt("mix_ms", stat[:, 8:14])
                    act.wait_ge(S("mix_rstd"), m + 1)
                    for g, (c0, c1) in enumerate(((0, 384), (384, 768), (768, 1024))):
                        ins = nc.scalar.activation(mix[:, 0, c0:c1], mix[:, 0, c0:c1], ACT.Copy, scale=stat[:, 8 + 2 * g:9 + 2 * g])
                    ins.then_inc(S("mix0_ready"), 1)
                    split_groups(0, KD)
                    gate_rows(1.0)
                    for u in range(4, 8):
                        hi_static(n0 + 20 + u, SLOT)
                    prefetch(n0 + UNITS_MID1)
                else:
                    m = mid2_n[0]
                    mid2_n[0] += 1

                    def strip(s):
                        act.wait_ge(S("mm_done"), n0 + 4 * s + 4)
                        b = bank[STRIP_BANKS[s]]
                        if s in (4, 5):
                            for t in range(NT):
                                ins = nc.scalar.activation(ret[:, t, 512 * (s - 4):512 * (s - 3)], bank[STRIP_BANKS[s] + t][:, :], ACT.Silu)
                            ins.then_inc(S("strip2_copied0"), 1)
                        elif s >= 7:
                            if s == 7:
                                act.wait_ge(S("ret_pv"), RH * (m + 1))
                            for t in range(NT):
                                ins = nc.scalar.activation(gates[:, t, 512 * (s - 7):512 * (s - 6)], bank[STRIP_BANKS[s] + t][:, :], ACT.Sigmoid)
                            ins.then_inc(S("strip2_copied0"), 1)
                        else:
                            dst = {0: qk2[:, 0, 0:512], 1: qk2[:, 0, 512:1024], 2: v2[:, 0, 0:512], 3: v2[:, 0, 512:1024], 6: p2[:, 0, :]}[s]
                            nc.scalar.activation(dst, b[:, :], ACT.Copy).then_inc(S("strip2_copied0"), 1)

                    def split_strip(s):
                        for u in range(4):
                            hi_static(n0 + 4 * s + u, SLOT)

                    if m == 0:
                        act.dma_start(con2, A["con2"]).then_inc(S("const2_loaded"), 16)
                    for s in range(8):
                        if s >= 1:
                            split_strip(s)
                            strip(s - 1)
                        if s == 4:
                            for g in (1, 3):
                                act.wait_ge(S("qkT2_ready"), 4 * m + g + 1)
                                nc.scalar.activation(qkT2[:, 2 * g:2 * g + 2, :].rearrange("p h n -> p (h n)"), bank[6 + g % 2][:, :], ACT.Copy)\
                                    .then_inc(S("qkT2_copied_act"), 1)
                    for u in range(32, 34):
                        hi_static(n0 + u, SLOT)
                    act.wait_ge(S("ret_pv"), RH * (m + 1))
                    sqr = ar(A_T, 2048).rearrange("p (t n) -> p t n", t=NT)
                    for t in range(NT):
                        for hh in range(2):
                            ins = nc.scalar.activation(sqr[:, t, 512 * hh:512 * (hh + 1)], bank[2 * t + hh][:, :], ACT.Square)
                    ins.then_inc(S("sqr_ready"), 1)
                    rms_sqrt("ret_ms", stat[:, 8:24])
                    for u in range(34, 36):
                        hi_static(n0 + u, SLOT)
                    for s in range(9, 12):
                        strip(s - 2)
                        split_strip(s)
                    strip(10)
                    split_groups(0, KD)
                    for g in range(2):
                        act.wait_ge(S("pool_ready"), 2 * m + g + 1)
                        nc.scalar.activation(pool_parts(whi, n0 + 48, g), bank[6 + g][:, :], ACT.Copy)\
                            .then_inc(S("phi_done"), 1)
                    hi_static(n0 + 48, 256)
                    hi_static(n0 + 49, 256)
                    for u in range(50, 54):
                        hi_static(n0 + u, SLOT)
                    split_groups(0, 4)
                    for u in range(54, 62):
                        hi_static(n0 + u, SLOT)
                    split_groups(0, KD)
                    gate_rows(1.0)
                    for u in range(4, 8):
                        hi_static(n0 + 58 + u, SLOT)
                    prefetch(n0 + UNITS_MID2)
            norm_stage(o_n[0] + 1)

        @block.vector
        def _(dve):
            V = nc.vector
            seq = [0]

            def then(ins):
                seq[0] += 1
                ins.then_inc(S("dve_step"), 1)
                dve.wait_ge(S("dve_step"), seq[0])

            def lo(slot, width, ready):
                dve.wait_ge(S("hi_done"), ready)
                V.tensor_tensor(wlo[:, slot, 0:width], raw[:, slot, 0:width], whi[:, slot, 0:width].bitcast(F32),
                                ALU.subtract).then_inc(S("lo_done"), 1)

            def lo_static(n, width):
                lo(n % RING, width, n + 1)

            V.memset(stat[:, 0:4], 0.0).then_inc(S("lo_done"), RING)
            V.memset(stat[:, 4:8], 0.0).then_inc(S("mm_done"), RING)
            V.memset(stat[:, 8:12], 0.0).then_inc(S("hi_done"), RING)
            V.memset(zero_hi[:, :].bitcast(F32), 0.0).then_inc(S("zero_ready"), 1)
            V.memset(relb1, 0.0).then_inc(S("zero_ready"), 1)

            def mod_unit(k, m, chunk, cond, first_free):
                dve.wait_ge(S(f"mod_loaded{k % MOD_RING}"), 16 * (8 // MOD_RING) * chunk + 16 * (k // MOD_RING + 1))
                w = modw[:, k % MOD_RING, :]
                sc = silc[:, 8 * cond + k:8 * cond + k + 1]
                if k == 0:
                    need(dve, S("mod_summed"), first_free)
                    V.tensor_scalar(modacc[:, :], w, sc, None, ALU.mult).then_inc(S("mod_used"), 1)
                else:
                    dve.wait_ge(S("mod_used"), m)
                    V.scalar_tensor_tensor(modacc[:, :], w, sc, modacc[:, :], ALU.mult, ALU.add).then_inc(S("mod_used"), 1)

            def mod_units(k0, k1, chunk, cond):
                for k in range(k0, k1):
                    mod_unit(k, 8 * chunk + k, chunk, cond, chunk)

            def mod_store(chunk):
                dve.wait_ge(S("mod_summed"), chunk + 1)
                at = bass.ds(8 * chunk, 8)
                V.tensor_tensor(modc[:, at], bank[MB][:, 0:8], vec[:, at], ALU.add).then_inc(S("mod_stored"), 1)

            for t in range(3):
                dve.wait_ge(S("vecT_ready"), t + 1)
                r = P if t < 2 else V_ROWS2
                ins = V.tensor_copy(vec[:, t * P:t * P + r], bank[t][:, 0:r])
            ins.then_inc(S("vec_ready"), 1)

            def window_bias(n):
                for q in range(6):
                    need(dve, S("bias_summed"), q)
                    q0, kb, c0 = (0, P, P)[q // 2], (0, 0, 1)[q // 2], 16 * (q % 2)
                    V.tensor_tensor(reached, posf_q[:, q0:q0 + P].unsqueeze(1).broadcast_to([P, 16, P]),
                                    posf_k[:, kb, c0:c0 + 16].unsqueeze(2).broadcast_to([P, 16, P]), ALU.is_ge).then_inc(S("reached"), 1)
                    if q < 4:
                        lo_static(n + q, SLOT)
                    dve.wait_ge(S("bias_summed"), q + 1)
                    for g in range(4):
                        c = P * (q // 2) + 32 * g + c0
                        ins = V.tensor_reduce(bias[:, :, c:c + 16], bank[4 + g][:, 0:288].rearrange("p (k q h) -> p h k q", q=3, h=WH), AX, ALU.add)
                    ins.then_inc(S("bias_taken"), 1)
                dve.wait_ge(S("bias_taken"), 6)
                V.tensor_tensor(bias[:, :, :], bias[:, :, :], con[:, C_MASKW:C_MASKW + 384].unsqueeze(1).broadcast_to([P, WH, 384]), ALU.add)\
                    .then_inc(S("bias_taken"), 1)

            tr, turned = [0], [0]
            cnt = {}

            def rope(tiles, cos, sin, heads, half, sem):
                tmp = ar(A_T, 4 * heads * half).rearrange("p (q h n) -> p q h n", q=4, h=heads)
                for t in range(NT):
                    x1, x2 = tiles[t][:, :, 0:half], tiles[t][:, :, half:2 * half]
                    c = cos[t].unsqueeze(1).broadcast_to([P, heads, half])
                    s = sin[t].unsqueeze(1).broadcast_to([P, heads, half])
                    V.tensor_tensor(tmp[:, 0], x1, c, ALU.mult)
                    V.tensor_tensor(tmp[:, 1], x2, s, ALU.mult)
                    V.tensor_tensor(tmp[:, 2], x2, c, ALU.mult)
                    then(V.tensor_tensor(tmp[:, 3], x1, s, ALU.mult))
                    V.tensor_tensor(x1, tmp[:, 0], tmp[:, 1], ALU.subtract)
                    ins = V.tensor_tensor(x2, tmp[:, 2], tmp[:, 3], ALU.add)
                    if t < NT - 1:
                        then(ins)
                ins.then_inc(S(sem), 1)

            def mean_eps(ap, count):
                then(V.tensor_scalar(ap, ap, 1.0 / count, EPS, ALU.mult, ALU.add))

            def rooted(name, ap):
                cnt[name] = cnt.get(name, 0) + 1
                dve.wait_ge(S(name + "_root"), cnt[name])
                then(V.reciprocal(ap, ap))

            def norm_stage(k):
                dve.wait_ge(S("ss_ready"), k)
                V.tensor_scalar(stat[:, 2:4], stat[:, 0:2], 1.0 / D, EPS, ALU.mult, ALU.add).then_inc(S("ms_ready"), 1)
                dve.wait_ge(S("rms_ready"), k)
                V.reciprocal(stat[:, 4:6], stat[:, 2:4]).then_inc(S("rstd_ready"), 1)
                dve.wait_ge(S("rstd_ready"), k)
                for h in range(2):
                    c = slice(512 * h, 512 * (h + 1))
                    V.tensor_scalar(xn[:, 1, c], x[:, 1, c], stat[:, 5:6], None, ALU.mult).then_inc(S("xn1_ready"), 1)

            def split_groups(dst0, chunks, scale, shift, products=None, banks=TRB, tiles=(None, None)):
                def scaled(c):
                    g = tr[0] + c // 2
                    if products is None:
                        dve.wait_ge(S("tr_ready"), turned[0] + c // 2 + 1)
                    else:
                        dve.wait_ge(S("mm_done"), products + c // 2)
                    need(dve, S("hlo_done"), g - 1)
                    for k in range(c, min(c + 2, chunks)):
                        src = bank[banks[c // 2]][:, 256 * (k - c):256 * (k - c + 1)]
                        dst = hf[:, g % 2, 256 * (k - c):256 * (k - c + 1)]
                        if shift is None:
                            ins = V.tensor_scalar(dst, src, scale[:, k:k + 1], None, ALU.mult) if scale is not None else V.tensor_copy(dst, src)
                        else:
                            ins = V.tensor_scalar(dst, src, scale[:, k:k + 1], shift[:, k:k + 1], ALU.mult, ALU.add)
                    ins.then_inc(S("hf_ready"), 1)

                def low(c):
                    g = tr[0] + c // 2
                    w = min(2, chunks - c) * SEQ
                    dve.wait_ge(S("hhi_done"), g + 1)
                    dve.wait_ge(S("hf_ready"), g + 1)
                    V.tensor_tensor(parts_at(tiles[1] or hT_tiles(hlo, dst0), c, w // SEQ), hf[:, g % 2, 0:w],
                                    parts_at(tiles[0] or hT_tiles(hhi, dst0), c, w // SEQ).bitcast(F32),
                                    ALU.subtract).then_inc(S("hlo_done"), 1)

                for c in range(0, chunks, 2):
                    scaled(c)
                    if c >= 2:
                        low(c - 2)
                low(2 * ((chunks - 1) // 2))
                tr[0] += (chunks + 1) // 2
                if products is None:
                    turned[0] += (chunks + 1) // 2

            def finish_x(k, end):
                more = end < total_units
                if more:
                    lo_static(end, SLOT)
                    lo_static(end + 1, SLOT)
                dve.wait_ge(S("gate_ready"), k)
                tmp = ar(A_X, 2048).rearrange("p (t n) -> p t n", t=NT)
                for t in range(NT):
                    if t == 0:
                        dve.wait_ge(S("block0_done"), k)
                    else:
                        dve.wait_ge(S("mm_done"), end)
                    for h in range(2):
                        c = slice(512 * h, 512 * (h + 1))
                        ins = V.tensor_tensor(tmp[:, t, c], bank[2 * t + h][:, :], gate_b[:, c], ALU.mult)
                    then(ins)
                    V.tensor_tensor(x[:, t, :], x[:, t, :], tmp[:, t, :], ALU.add).then_inc(S("x_done"), 1)
                if more:
                    lo_static(end + 2, SLOT)

            def scale_cols(a):
                dve.wait_ge(S("mod_stored"), a["mod"] + 2)
                sc = modc[:, 8 * (a["mod"] + 1):8 * (a["mod"] + 2)]
                then(V.scalar_tensor_tensor(sclA[:, :], sc, 1.0, vec[:, a["g"]:a["g"] + 8], ALU.add, ALU.mult))

            dve.wait_ge(S("cond_ready"), 1)
            mod_units(0, 8, 0, 0)
            dve.wait_ge(S("x_loaded"), 16)
            V.memset(stat[:, 16:20], 0.0).then_inc(S("x_done"), NT)

            dve.wait_ge(S("pos_loaded"), 14 * 16)
            dve.wait_ge(S("const_loaded"), 16)
            V.tensor_copy(posf_i, pos_i)
            V.tensor_copy(posf_q, pos_q)
            V.tensor_copy(posf_k, pos_k)
            then(V.tensor_tensor(bstep, relb, relb1, ALU.subtract))
            freq = con[:, C_FREQ:C_FREQ + 16]
            for t in range(NT):
                ins = V.tensor_scalar(ang[:, t, :], freq, posf_i[:, t:t + 1], None, ALU.mult)
            then(V.tensor_scalar(posf_q, posf_q, con[:, C_THR:C_THR + 1], None, ALU.subtract))

            for q in range(3):
                then(V.tensor_copy(bparts[:, q, :], bstep))
                if q < 2:
                    then(V.tensor_tensor(bstep, bstep, bparts[:, q, :], ALU.subtract))
            magic = 1.5 * 2.0 ** 23
            c1 = 6.28125
            c2 = float(np.float32(2 * math.pi - c1))
            c3 = 2 * math.pi - c1 - c2
            for s in range(2):
                V.tensor_scalar(turns[:, s], ang, 1.0 / (2 * math.pi), 0.25 if s == 0 else 0.0, ALU.mult, ALU.add)
            then(V.memset(stat[:, 12:16], 0.0))
            tf = turns.rearrange("p a t n -> p (a t n)")
            then(V.tensor_scalar(tf, tf, magic, None, ALU.add))
            then(V.tensor_scalar(tf, tf, magic, None, ALU.subtract))
            for s in range(2):
                then(V.scalar_tensor_tensor(rope1[:, s], turns[:, s], -c1, ang, ALU.mult, ALU.add))
                then(V.scalar_tensor_tensor(rope1[:, s], turns[:, s], -c2, rope1[:, s], ALU.mult, ALU.add))
                then(V.scalar_tensor_tensor(rope1[:, s], turns[:, s], -c3, rope1[:, s], ALU.mult, ALU.add))
            then(V.tensor_scalar(rope1[:, 0], rope1[:, 0], math.pi / 2, None, ALU.add))
            r1 = rope1[:, :, :, :].rearrange("p a t n -> p (a t n)")
            V.tensor_scalar(r1, r1, 3.1415925, -3.1415925, ALU.min, ALU.max).then_inc(S("angles_ready"), 1)

            norm_stage(1)
            mod_store(0)
            mod_units(0, 8, 1, 0)
            for u in range(PREFETCH):
                lo_static(RING + u, SLOT)
            mod_store(1)
            phase = [0]
            ffn_n, mid1_n, mid2_n = [0], [0], [0]
            for kind, n0, a in phases:
                phase[0] += 1
                scale_cols(a)
                if phase[0] > 1:
                    norm_stage(phase[0])
                    lo_static(n0 + 3, SLOT)
                split_groups(0, KD, sclA, modc[:, 8 * a["mod"]:8 * (a["mod"] + 1)], banks=TRB_FFN if kind == "ffn" else TRB)
                if kind == "ffn":
                    f = ffn_n[0]
                    ffn_n[0] += 1
                    before, in_loop = MOD_PLAN[f]

                    def cond_of(c):
                        return 0 if c < 18 else 1

                    def gated(j):
                        for t in range(NT):
                            dve.wait_ge(S("silu_done"), 2 * (STRIPS * f + j) + t + 1)
                            if t == 0:
                                need(dve, S("actT_ready"), STRIPS * f + j)
                            ins = V.tensor_tensor(act_t[:, t, :], sg_t[:, t, :], bank[GB[t]][:, 256:512], ALU.mult)
                        ins.then_inc(S("act_ready"), 1)

                    def act_lo(j):
                        dve.wait_ge(S("ahi_done"), STRIPS * f + j + 1)
                        V.tensor_tensor(alo[:, :, :].rearrange("p k n -> p (k n)"), bank[ATB][:, :],
                                        ahi[:, :, :].rearrange("p k n -> p (k n)").bitcast(F32), ALU.subtract).then_inc(S("alo_done"), 1)

                    def units(c, i, lo_, hi_):
                        for u in range(lo_, hi_):
                            m = c + u
                            lo(m % RING, SLOT, 12 * i + m + 1)

                    if before is not None:
                        mod_units(0, 8, before, cond_of(before))
                    gated(0)
                    if before is not None:
                        mod_store(before)
                    with dve.Fori(0, STRIPS // 2) as i:
                        for s in range(2):
                            c = n0 + 4 + 6 * s
                            units(c, i, 0, 4)
                            if in_loop is not None:
                                mod_units(4 * s, 4 * s + 4, i + in_loop, cond_of(in_loop + 4))
                            act_lo(2 * i + s)
                            units(c, i, 4, 6)
                            gated(2 * i + s + 1)
                        if in_loop is not None:
                            mod_store(i + in_loop)
                    c = n0 + 4 + 12 * (STRIPS // 2)
                    act_lo(STRIPS - 1)
                    units(c, 0, 0, 2)
                    finish_x(phase[0], n0 + {"ffn": UNITS_FFN, "mid1": UNITS_MID1, "mid2": UNITS_MID2}[kind])
                elif kind == "mid1":
                    m = mid1_n[0]
                    l = a["l"]
                    mid1_n[0] += 1
                    widths = [512, 512, 512, D_IN - 1536]
                    if m == 0:
                        dve.wait_ge(S("hlo_done"), tr[0])
                        window_bias(n0 + 4)
                    for s in range(4):
                        for u in range(0 if s == 0 or (s == 1 and m == 0) else 4):
                            lo_static(n0 + 4 * s + u, 2 * widths[s])
                        if s >= 1:
                            dve.wait_ge(S("mm_done"), n0 + 4 * s)
                            V.tensor_copy(proj[:, 1, 512 * (s - 1):512 * s], bank[2 * (s - 1) + 1][:, :]).then_inc(S("strip_copied1"), 1)
                        if s == 1:
                            V.tensor_copy(latg[:, 0:2], vec[:, V_QA + 2 * l:V_QA + 2 * l + 2])
                            V.tensor_copy(latg[:, 2:3], vec[:, V_KVA + l:V_KVA + l + 1])
                        if s == 2:
                            dve.wait_ge(S("lat_sq"), m + 1)
                            V.tensor_scalar(stat[:, 8:10], stat[:, 8:10], 1.0 / QL, EPS, ALU.mult, ALU.add)
                            V.tensor_scalar(stat[:, 10:12], stat[:, 10:12], 1.0 / KVL, EPS, ALU.mult, ALU.add).then_inc(S("lat_ms"), 1)
                            rooted("lat_ms", stat[:, 8:12])
                            for t in range(NT):
                                V.tensor_scalar(lat[:, t, 0:QL], proj[:, t, 0:QL], stat[:, 8 + t:9 + t], None, ALU.mult)
                                ins = V.tensor_scalar(lat[:, t, QL:], proj[:, t, QL:QL + KVL], stat[:, 10 + t:11 + t], None, ALU.mult)
                            ins.then_inc(S("lat_ready"), 1)
                            dve.wait_ge(S("lat_ready"), m + 1)
                    split_groups(0, 3, latg, None, banks=TRB_LATENT, tiles=(latent_hi, latent_lo))
                    sq = ar(A_QK, NT * 512).rearrange("p (t n) -> p t n", t=NT)
                    dve.wait_ge(S("sq_ready"), m + 1)
                    then(V.tensor_reduce(stat[:, 12:28].rearrange("p (t h) -> p t h", t=NT), sq.rearrange("p t (h n) -> p t h n", n=HD), AX, ALU.add))
                    V.tensor_scalar(stat[:, 12:28], stat[:, 12:28], 1.0 / HD, EPS, ALU.mult, ALU.add).then_inc(S("win_ms"), 1)
                    rooted("win_ms", stat[:, 12:28])
                    lo_static(n0 + 16, 576)
                    lo_static(n0 + 17, 576)
                    dve.wait_ge(S("mm_done"), n0 + 16)
                    V.tensor_copy(proj[:, 1, 1536:D_IN], bank[7][:, 0:D_IN - 1536]).then_inc(S("strip_copied1"), 1)
                    lo_static(n0 + 18, 384)
                    lo_static(n0 + 19, 384)
                    wq = proj[:, :, O_WQ:O_WQ + 512].rearrange("p t (h n) -> p t h n", n=HD)
                    for t in range(NT):
                        ins = V.tensor_tensor(wq[:, t], wq[:, t], stat[:, 12 + 8 * t:20 + 8 * t].unsqueeze(2).broadcast_to([P, 8, HD]), ALU.mult)
                    then(ins)
                    dve.wait_ge(S("gains_loaded"), 16 * 5 * (l + 1))
                    for t in range(NT):
                        V.tensor_tensor(wq[:, t, 0:WH], wq[:, t, 0:WH], gw64[:, 0:1, :].broadcast_to([P, WH, HD]), ALU.mult)
                        for kvh in range(WKV):
                            ins = V.tensor_tensor(kdup[:, t, kvh], wq[:, t, WH + kvh:WH + kvh + 1].broadcast_to([P, 2, HD]),
                                                  gw64[:, 1:2, :].broadcast_to([P, 2, HD]), ALU.mult)
                    then(ins)
                    dve.wait_ge(S("mm_done"), n0 + 20)
                    for u in range(2):
                        V.tensor_copy(qk1[:, 1, 3 * u:3 * u + 3, :].rearrange("p h n -> p (h n)"), bank[2 * u + 1][:, 0:288])
                        ins = V.tensor_copy(kv[:, 1, 3 * u:3 * u + 3, :].rearrange("p h n -> p (h n)"), bank[5 + 2 * u][:, 0:384])
                    ins.then_inc(S("up_copied1"), 1)
                    sqq = ar(A_T, NT * 576).rearrange("p (t h n) -> p t h n", t=NT, h=MH)
                    sqk = ar(A_T + NT * 576, NT * 384).rearrange("p (t h n) -> p t h n", t=NT, h=MH)
                    hs = stat[:, 32:56].rearrange("p (t h) -> p t h", t=NT)
                    dve.wait_ge(S("sqh_ready"), m + 1)
                    V.tensor_reduce(hs[:, :, 0:MH], sqq, AX, ALU.add)
                    then(V.tensor_reduce(hs[:, :, MH:12], sqk, AX, ALU.add))
                    for t in range(NT):
                        ins = V.tensor_scalar(hs[:, t, MH:12], hs[:, t, MH:12], stat[:, 28 + t:29 + t], None, ALU.add)
                    then(ins)
                    V.tensor_scalar(stat[:, 32:56], stat[:, 32:56], 1.0 / MQK, EPS, ALU.mult, ALU.add).then_inc(S("head_ms"), 1)
                    rooted("head_ms", stat[:, 32:56])
                    for r in range(2):
                        heads = slice(MH * r, MH * (r + 1))
                        for t in range(NT):
                            rstd = hs[:, t, heads].unsqueeze(2)
                            if r == 0:
                                ins = V.tensor_tensor(qk1[:, t, heads], qk1[:, t, heads], rstd.broadcast_to([P, MH, MQK]), ALU.mult)
                            else:
                                V.tensor_tensor(qk1[:, t, heads, 0:MNOPE], kv[:, t, :, 0:MNOPE], rstd.broadcast_to([P, MH, MNOPE]), ALU.mult)
                                shared = proj[:, t, O_KPE:O_KPE + MROPE].unsqueeze(1).broadcast_to([P, MH, MROPE])
                                ins = V.tensor_tensor(qk1[:, t, heads, MNOPE:MQK], shared, rstd.broadcast_to([P, MH, MROPE]), ALU.mult)
                        then(ins)
                        for t in range(NT):
                            ins = V.tensor_tensor(qk1[:, t, heads], qk1[:, t, heads], gq96[:, r:r + 1, :].broadcast_to([P, MH, MQK]), ALU.mult)
                        then(ins)
                        if m == 0:
                            dve.wait_ge(S("rope_ready"), 1)
                        rope([qk1[:, t, heads, MNOPE:MQK] for t in range(NT)], [rope1[:, 0, t] for t in range(NT)],
                             [rope1[:, 1, t] for t in range(NT)], MH, 16, "heads_normed")
                        dve.wait_ge(S("heads_normed"), 2 * m + r + 1)
                    for g in range(0, 6, 2):
                        dve.wait_ge(S("qkT_ready"), 6 * m + g + 1)
                        copy_mla(V.tensor_copy, g).then_inc(S("qkT_copied_dve"), 1)
                    rs = rsum[:, 0:24].rearrange("p (h t) -> p t h", t=NT)
                    for h in range(12):
                        k = 12 * m + h
                        r = h % 2
                        dve.wait_ge(S("scores_ready"), k + 1)
                        if h >= 2:
                            dve.wait_ge(S("probsT_ready"), k - 1)
                        mask = con[:, C_MASKC:C_MASKC + 384] if h < MH else bias[:, h - MH, :]
                        if m == 0 and h == MH:
                            dve.wait_ge(S("bias_taken"), 7)
                        scale = MQK ** -0.5 if h < MH else HD ** -0.5
                        then(V.scalar_tensor_tensor(sc_t[:, r, :], bank[r][:, 0:384], scale, mask, ALU.mult, ALU.add))
                        mx = nmax[:, 2 * h:2 * h + 2]
                        V.tensor_reduce(mx[:, 0:1], sc_t[:, r, 0:P], AX, ALU.max)
                        then(V.tensor_reduce(mx[:, 1:2], sc_t[:, r, P:384], AX, ALU.max))
                        if h < MH:
                            V.tensor_scalar(mx, mx, -1.0, None, ALU.mult).then_inc(S("max_ready"), 1)
                        else:
                            V.tensor_scalar(mx, mx, sink[:, h - MH:h - MH + 1], -1.0, ALU.max, ALU.mult).then_inc(S("max_ready"), 1)
                        if h < SH:
                            dve.wait_ge(S("sb_ln"), m + 1)
                            then(V.scalar_tensor_tensor(sb_u(h), sb_z(h), 0.0, sb_u(h), ALU.max, ALU.add))
                            V.tensor_tensor(sb_u(h), sb_u(h), con[:, C_MASKS:C_MASKS + 384], ALU.mult).then_inc(S("stick_ready"), 1)
                        if 2 <= h < 2 + SH:
                            j = h - 2
                            z = sb_z(j)
                            dve.wait_ge(S("stick_sum"), SH * m + j + 1)
                            then(V.tensor_tensor(z, z, bank[6 + j % 2][:, 0:384], ALU.subtract))
                            V.tensor_tensor(z, z, con[:, C_MASKA:C_MASKA + 384], ALU.add).then_inc(S("zs_ready"), 1)
                        if h >= 9:
                            lo_static(n0 + 20 + h - 9, SLOT)
                        if h == 10:
                            dve.wait_ge(S("probs_ready"), 12 * m + 8)
                            dve.wait_ge(S("sink_exp"), WH * m + 2)
                            then(V.tensor_tensor(rsum[:, 12:16], rsum[:, 12:16], esink[:, 0:4], ALU.add))
                            then(V.reciprocal(rsum[:, 0:16], rsum[:, 0:16]))
                            dve.wait_ge(S("pv_done"), 12 * m + 8)
                            for t in range(NT):
                                ins = V.tensor_tensor(mix[:, t, 0:512].rearrange("p (h n) -> p h n", n=64), bank[4 + t][:, :].rearrange("p (h n) -> p h n", n=64),
                                                      rs[:, t, 0:8].unsqueeze(2).broadcast_to([P, 8, 64]), ALU.mult)
                            ins.then_inc(S("heads_out"), 1)
                    dve.wait_ge(S("probs_ready"), 12 * m + 12)
                    dve.wait_ge(S("sink_exp"), WH * (m + 1))
                    then(V.tensor_tensor(rsum[:, 16:24], rsum[:, 16:24], esink[:, 4:12], ALU.add))
                    then(V.reciprocal(rsum[:, 16:24], rsum[:, 16:24]))
                    dve.wait_ge(S("pv_done"), 12 * m + 12)
                    dve.wait_ge(S("sb_pv_done"), SH * (m + 1))
                    for t in (1, 0):
                        if t == 0:
                            dve.wait_ge(S("bank6_read"), m + 1)
                        V.tensor_tensor(mix[:, t, 512:768].rearrange("p (h n) -> p h n", n=64), bank[6 + t][:, 0:256].rearrange("p (h n) -> p h n", n=64),
                                        rs[:, t, 8:12].unsqueeze(2).broadcast_to([P, 4, 64]), ALU.mult).then_inc(S("heads_out"), 1)
                    lo_static(n0 + 23, SLOT)
                    dve.wait_ge(S("sqm_ready"), m + 1)
                    V.tensor_scalar(stat[:, 8:12], stat[:, 8:12], 1.0 / 384, EPS, ALU.mult, ALU.add)
                    V.tensor_scalar(stat[:, 12:14], stat[:, 12:14], 1.0 / 256, EPS, ALU.mult, ALU.add).then_inc(S("mix_ms"), 1)
                    dve.wait_ge(S("mix_ms_root"), m + 1)
                    V.reciprocal(stat[:, 8:14], stat[:, 8:14]).then_inc(S("mix_rstd"), 1)
                    dve.wait_ge(S("mix_rstd"), m + 1)
                    for g, (c0, c1) in enumerate(((0, 384), (384, 768), (768, 1024))):
                        ins = V.tensor_scalar(mix[:, 1, c0:c1], mix[:, 1, c0:c1], stat[:, 9 + 2 * g:10 + 2 * g], None, ALU.mult)
                    ins.then_inc(S("mix1_ready"), 1)
                    split_groups(0, KD, vec[:, V_ON + 8 * l:V_ON + 8 * l + 8], None)
                    for u in range(4, 8):
                        lo_static(n0 + 20 + u, SLOT)
                    finish_x(phase[0], n0 + {"ffn": UNITS_FFN, "mid1": UNITS_MID1, "mid2": UNITS_MID2}[kind])
                else:
                    m = mid2_n[0]
                    l = a["l"]
                    mid2_n[0] += 1

                    def split_strip(s):
                        for u in range(4):
                            lo_static(n0 + 4 * s + u, SLOT)

                    def strip(s):
                        if s in (0, 1, 2, 3, 6):
                            dve.wait_ge(S("mm_done"), n0 + 4 * s + 4)
                            dst = {0: qk2[:, 1, 0:512], 1: qk2[:, 1, 512:1024], 2: v2[:, 1, 0:512], 3: v2[:, 1, 512:1024], 6: p2[:, 1, :]}[s]
                            V.tensor_copy(dst, bank[STRIP_BANKS[s] + 1][:, :]).then_inc(S("strip2_copied1"), 1)

                    for s in range(8):
                        if s >= 1:
                            split_strip(s)
                            strip(s - 1)
                        if s == 2:
                            dve.wait_ge(S("strip2_copied0"), 11 * m + 2)
                            dve.wait_ge(S("strip2_copied1"), 5 * m + 2)
                            rp = [qk2[:, t, :].rearrange("p (h n) -> p h n", n=RQK) for t in range(NT)]
                            cs = [con[:, C_ROPE2 + 32 * t:C_ROPE2 + 32 * (t + 1)] for t in range(NT)]
                            sn = [con[:, C_ROPE2 + 64 + 32 * t:C_ROPE2 + 64 + 32 * (t + 1)] for t in range(NT)]
                            rope(rp, cs, sn, 16, 32, "rope2_done")
                        if s == 4:
                            for g in (0, 2):
                                dve.wait_ge(S("qkT2_ready"), 4 * m + g + 1)
                                V.tensor_copy(qkT2[:, 2 * g:2 * g + 2, :].rearrange("p h n -> p (h n)"), bank[6 + g % 2][:, :])\
                                    .then_inc(S("qkT2_copied_dve"), 1)
                    if m == 0:
                        dve.wait_ge(S("const2_loaded"), 16)
                    for h in range(RH):
                        k = RH * m + h
                        dve.wait_ge(S("ret_scores"), k + 1)
                        if h >= 2:
                            dve.wait_ge(S("ret_pv"), k - 1)
                        dec = con2[:, C2_DECAY + 256 * h:C2_DECAY + 256 * (h + 1)]
                        V.tensor_tensor(sc_t[:, h % 2, 0:256], bank[6 + h % 2][:, 0:256], dec, ALU.mult)
                        V.tensor_tensor(sc_t[:, h % 2, 256:384], bank[6 + h % 2][:, 256:384], dec[:, 0:P], ALU.mult).then_inc(S("ret_probs"), 1)
                    for u in range(32, 34):
                        lo_static(n0 + u, SLOT)
                    sqr = ar(A_T, 2048).rearrange("p (t n) -> p t n", t=NT)
                    dve.wait_ge(S("sqr_ready"), m + 1)
                    rr = stat[:, 8:24].rearrange("p (t h) -> p t h", t=NT)
                    then(V.tensor_reduce(rr, sqr.rearrange("p t (h n) -> p t h n", n=RV), AX, ALU.add))
                    V.tensor_scalar(stat[:, 8:24], stat[:, 8:24], 1.0 / RV, EPS, ALU.mult, ALU.add).then_inc(S("ret_ms"), 1)
                    for t in range(NT):
                        for hh in range(2):
                            c = slice(512 * hh, 512 * (hh + 1))
                            ins = V.tensor_tensor(ret[:, t, c], ret[:, t, c], bank[2 * t + hh][:, :], ALU.mult)
                    ins.then_inc(S("ret_taken"), 1)
                    rooted("ret_ms", stat[:, 8:24])
                    for u in range(34, 36):
                        lo_static(n0 + u, SLOT)
                    dve.wait_ge(S("ret_taken"), m + 1)
                    rv = ret.rearrange("p t (h n) -> p t h n", n=RV)
                    for t in range(NT):
                        ins = V.tensor_tensor(rv[:, t], rv[:, t], rr[:, t].unsqueeze(2).broadcast_to([P, RH, RV]), ALU.mult)
                    ins.then_inc(S("ret_ready"), 1)
                    for s in range(9, 12):
                        split_strip(s)
                    split_groups(0, KD, None, None)
                    for g in range(2):
                        dve.wait_ge(S("phi_done"), 2 * m + g + 1)
                        V.tensor_tensor(pool_parts(wlo, n0 + 48, g), bank[6 + g][:, :],
                                        pool_parts(whi, n0 + 48, g).bitcast(F32), ALU.subtract)\
                            .then_inc(S("plo_done"), 1)
                    lo_static(n0 + 48, 256)
                    lo_static(n0 + 49, 256)
                    for u in range(50, 54):
                        lo_static(n0 + u, SLOT)
                    split_groups(0, 4, vec[:, V_PS + 4 * l:V_PS + 4 * l + 4], None, products=n0 + 49)
                    for u in range(54, 56):
                        lo_static(n0 + u, SLOT)
                    dve.wait_ge(S("strip2_copied0"), 11 * (m + 1))
                    dve.wait_ge(S("mm_done"), n0 + 54)
                    for t in range(NT):
                        for h in range(2):
                            c = slice(512 * h, 512 * (h + 1))
                            ins = V.tensor_tensor(gates[:, t, c], gates[:, t, c], bank[2 * t + h][:, :], ALU.mult)
                    ins.then_inc(S("ret_gated"), 1)
                    for u in range(56, 62):
                        lo_static(n0 + u, SLOT)
                    dve.wait_ge(S("mm_done"), n0 + 58)
                    dve.wait_ge(S("ret_gated"), m + 1)
                    for h in range(2):
                        c, cp = slice(512 * h, 512 * (h + 1)), slice(1024 + 512 * h, 1024 + 512 * (h + 1))
                        for t in range(NT):
                            ins = V.tensor_tensor(gates[:, t, cp], gates[:, t, cp], bank[4 + 2 * t + h][:, :], ALU.mult)
                        then(ins)
                        V.tensor_tensor(gates[:, :, c], gates[:, :, c], gates[:, :, cp], ALU.add).then_inc(S("merged_ready"), 1)
                    split_groups(0, KD, None, None, banks=TRB_MERGED)
                    for u in range(4, 8):
                        lo_static(n0 + 58 + u, SLOT)
                    finish_x(phase[0], n0 + {"ffn": UNITS_FFN, "mid1": UNITS_MID1, "mid2": UNITS_MID2}[kind])
            k = phase[0] + 1
            norm_stage(k)
            dve.wait_ge(S("final_gain"), 16)
            for t in range(NT):
                dve.wait_ge(S(f"xn{t}_ready"), 2 * k)
                V.tensor_tensor(xn[:, t, :], xn[:, t, :], gate_b, ALU.mult).then_inc(S("out_ready"), 1)

        @block.tensor
        def _(pe):
            T = nc.tensor

            def products(o, c, t, wh, wl, start, stop, hi_=hhi, lo_=hlo):
                sh, sl = hi_[:, c, P * t:P * (t + 1)], lo_[:, c, P * t:P * (t + 1)]
                T.matmul(o, sh, wh, start=start, stop=False)
                T.matmul(o, sh, wl, start=False, stop=False)
                return T.matmul(o, sl, wh, start=False, stop=stop)

            def strip_unit(slot, ready, u, last, banks, width, hi_=hhi, lo_=hlo):
                pe.wait_ge(S("lo_done"), ready)
                for k in range(2):
                    wh = whi[:, slot, k * width:(k + 1) * width]
                    wl = wlo[:, slot, k * width:(k + 1) * width]
                    for t in range(NT):
                        ins = products(bank[banks[t]][:, 0:width], 2 * u + k, t, wh, wl, u == 0 and k == 0, last and k == 1, hi_, lo_)
                ins.then_inc(S("mm_done"), 1)

            def rows_unit(slot, ready, c, first, last, hi_, lo_, first_bank=0):
                pe.wait_ge(S("lo_done"), ready)
                for t in range(NT):
                    for h in range(2):
                        wh = whi[:, slot, 512 * h:512 * (h + 1)]
                        wl = wlo[:, slot, 512 * h:512 * (h + 1)]
                        ins = products(bank[first_bank + 2 * t + h][:, :], c, t, wh, wl, first, last, hi_, lo_)
                ins.then_inc(S("mm_done"), 1)

            def last_rows(n, c, hi_, lo_):
                for t in range(NT):
                    for u in range(2):
                        if t == 0:
                            pe.wait_ge(S("lo_done"), n + u + 1)
                        for h in range(2):
                            wh = whi[:, (n + u) % RING, 512 * h:512 * (h + 1)]
                            wl = wlo[:, (n + u) % RING, 512 * h:512 * (h + 1)]
                            ins = products(bank[2 * t + h][:, :], c + u, t, wh, wl, False, u == 1, hi_, lo_)
                    if t == 0:
                        ins.then_inc(S("block0_done"), 1)
                ins.then_inc(S("mm_done"), 2)

            pe.wait_ge(S("const_loaded"), 16)
            pe.wait_ge(S("rows_loaded"), 13 * 16)
            for t in range(3):
                r = P if t < 2 else V_ROWS2
                T.transpose(bank[t][:, 0:r], rows[0:r, t, :], ident[0:r, 0:r]).then_inc(S("vecT_ready"), 1)

            def mod_sum(chunk):
                pe.wait_ge(S("mod_used"), 8 * chunk + 8)
                need(pe, S("mod_stored"), chunk)
                for k in range(KD):
                    ins = T.matmul(bank[MB][:, k:k + 1], modacc[:, P * k:P * (k + 1)], ones_col, start=True, stop=True)
                ins.then_inc(S("mod_summed"), 1)

            def bias_pass(q):
                pe.wait_ge(S("reached"), q + 1)
                need(pe, S("bias_taken"), q)
                for k in range(16):
                    for g in range(4):
                        r = slice(NBUCKET * g, NBUCKET * (g + 1))
                        ins = T.matmul(bank[4 + g][:, 3 * WH * k:3 * WH * (k + 1)], reached[r, k, :], bparts[r].rearrange("p q h -> p (q h)"),
                                       start=True, stop=True)
                ins.then_inc(S("bias_summed"), 1)

            tr = [0]

            def transposes(src, chunks, banks=TRB, halves=None):
                for c in range(0, chunks, 2):
                    if halves is not None and c % 4 == 0:
                        halves(c // 4)
                    for k in range(c, min(c + 2, chunks)):
                        for t in range(NT):
                            ins = T.transpose(bank[banks[c // 2]][:, 256 * (k - c) + P * t:256 * (k - c) + P * (t + 1)],
                                              src[:, t, P * k:P * (k + 1)], ident)
                    ins.then_inc(S("tr_ready"), 1)
                    tr[0] += 1

            def hT_ready(c):
                pe.wait_ge(S("hlo_done"), tr[0] - KD // 2 + c // 2 + 1)

            def gate_rows(chunk):
                pe.wait_ge(S("mod_stored"), chunk + 1)
                pe.wait_ge(S("hf_ready"), tr[0])
                for k in range(KD):
                    col = modc[:, 8 * chunk + k:8 * chunk + k + 1].broadcast_to([P, P])
                    ins = T.matmul(bank[6 + k // 4][:, P * (k % 4):P * (k % 4 + 1)], col, ident, start=True, stop=True)
                ins.then_inc(S("gate_rows"), 1)

            ph, ffn_n, mid1_n, mid2_n = [0], [0], [0], [0]
            pe.wait_ge(S("zero_ready"), 1)

            def normed(half):
                for t in range(NT):
                    pe.wait_ge(S(f"xn{t}_ready"), 2 * (ph[0] - 1) + half + 1)

            for kind, n0, a in phases:
                ph[0] += 1
                if ph[0] == 1:
                    mod_sum(0)
                transposes(xn, KD, TRB_FFN if kind == "ffn" else TRB, halves=normed)
                if ph[0] == 1:
                    mod_sum(1)
                if kind == "ffn":
                    f = ffn_n[0]
                    ffn_n[0] += 1
                    before, in_loop = MOD_PLAN[f]

                    def gate_up(c, i, lo_, hi_):
                        for u in range(lo_, hi_):
                            if isinstance(i, int):
                                hT_ready(2 * u)
                            strip_unit((c + u) % RING, 12 * i + c + u + 1, u, u == 3, GB, 512)

                    def down(c, i, j):
                        pe.wait_ge(S("alo_done"), STRIPS * f + j + 1)
                        for u in range(2):
                            rows_unit((c + u) % RING, 12 * i + c + u + 1, u, False, False, ahi, alo)

                    def turn(j):
                        pe.wait_ge(S("act_ready"), STRIPS * f + j + 1)
                        for k in range(2):
                            for t in range(NT):
                                ins = T.transpose(bank[ATB][:, 256 * k + P * t:256 * k + P * (t + 1)], act_t[:, t, P * k:P * (k + 1)], ident)
                        ins.then_inc(S("actT_ready"), 1)

                    gate_up(n0, 0, 0, 4)
                    for b in range(4):
                        T.matmul(bank[b][:, :], zero_hi[:, :], hhi[:, 0:2, :].rearrange("p k n -> p (k n)"), start=True, stop=False)
                    if before is not None:
                        mod_sum(before)
                    with pe.Fori(0, STRIPS // 2) as i:
                        for s in range(2):
                            c = n0 + 4 + 6 * s
                            pe.wait_ge(S("act_ready"), STRIPS * f + 2 * i + s + 1)
                            gate_up(c, i, 0, 2)
                            turn(2 * i + s)
                            gate_up(c, i, 2, 4)
                            if in_loop is not None and s == 1:
                                mod_sum(i + in_loop)
                            down(c + 4, i, 2 * i + s)
                    c = n0 + 4 + 12 * (STRIPS // 2)
                    turn(STRIPS - 1)
                    pe.wait_ge(S("alo_done"), STRIPS * (f + 1))
                    gate_rows(a["mod"] + 2)
                    last_rows(c, 0, ahi, alo)
                elif kind == "mid1":
                    m = mid1_n[0]
                    mid1_n[0] += 1
                    widths = [512, 512, 512, D_IN - 1536]
                    for s in range(4):
                        for u in range(4):
                            n = n0 + 4 * s + u
                            if s == 0:
                                hT_ready(2 * u)
                            strip_unit(n % RING, n + 1, u, u == 3, (2 * s, 2 * s + 1), widths[s])
                            if m == 0 and 4 * s + u < 6:
                                bias_pass(4 * s + u)
                        if m == 0 and s == 1:
                            pe.wait_ge(S("bias_taken"), 6)
                        if s == 2:
                            pe.wait_ge(S("lat_ready"), m + 1)
                            transposes(lat, 3, TRB_LATENT)
                    pe.wait_ge(S("hlo_done"), tr[0])
                    pe.wait_ge(S("strip_copied0"), 4 * m + 2)
                    pe.wait_ge(S("strip_copied1"), 4 * m + 2)
                    for u in range(2):
                        n = n0 + 16 + u
                        strip_unit(n % RING, n + 1, 0, True, (2 * u, 2 * u + 1), 288, ahi, alo)
                    pe.wait_ge(S("strip_copied0"), 4 * m + 4)
                    pe.wait_ge(S("strip_copied1"), 4 * m + 4)
                    for u in range(2):
                        n = n0 + 18 + u
                        pe.wait_ge(S("lo_done"), n + 1)
                        for t in range(NT):
                            ins = products(bank[4 + 2 * u + t][:, 0:384], 0, t, whi[:, n % RING, 0:384], wlo[:, n % RING, 0:384], True, True, kvhi, kvlo)
                        ins.then_inc(S("mm_done"), 1)
                    pe.wait_ge(S("up_copied0"), m + 1)
                    pe.wait_ge(S("up_copied1"), m + 1)
                    sources = [[proj[:, t, O_WQ + P * j:O_WQ + P * (j + 1)] for t in range(NT)] for j in range(3)]
                    sources += [[kdup[:, t, j].rearrange("p r n -> p (r n)") for t in range(NT)] for j in range(WKV)]
                    sources += [[proj[:, t, O_SB + P * j:O_SB + P * (j + 1)] for t in range(NT)] for j in range(4)]

                    def head(h):
                        if h < MH:
                            return mlaT[0:MQK, h, :], mlaT[0:MQK, MH + h, :], [kv[:, t, h, 64:128] for t in range(NT)]
                        w = h - MH if h < 12 else h - 12
                        r0 = 64 * (w % 2)
                        if h < 12:
                            q, k, v = w // 2, 3 + w // 3, O_WV + 64 * (w // 3)
                        else:
                            q, k, v = 5 + w // 2, 7 + w // 2, O_SB + 512 + 64 * w
                        return pairT[r0:r0 + 64, q, :], pairT[r0:r0 + 64, k, :], [proj[:, t, v:v + 64] for t in range(NT)]

                    for j, (at, w) in enumerate(PAIR_GROUPS):
                        if j == 4:
                            pe.wait_ge(S("pairT_copied"), 5 * m + 1)
                        for k in range(w):
                            for t in range(NT):
                                ins = T.transpose(bank[j % 4][:, 256 * k + P * t:256 * k + P * (t + 1)], sources[at + k][t], ident)
                        ins.then_inc(S("pairT_ready"), 1)
                    pe.wait_ge(S("pairT_copied"), 5 * m + 2)
                    for h in range(SH):
                        q, k, _ = head(12 + h)
                        T.matmul(bank[4 + h][:, 0:SEQ], k[:, 0:P], q, start=True, stop=True)
                        T.matmul(bank[4 + h][:, SEQ:384], k[:, P:SEQ], q[:, P:SEQ], start=True, stop=True).then_inc(S("sb_scores"), 1)
                    pe.wait_ge(S("pairT_copied"), 5 * (m + 1))
                    for g in range(6):
                        if g % 3 == 0:
                            pe.wait_ge(S("heads_normed"), 2 * m + g // 3 + 1)
                        if g >= 4:
                            pe.wait_ge(S("qkT_copied_act" if g % 2 else "qkT_copied_dve"), 3 * m + (g - 4) // 2 + 1)
                        for k in range(2):
                            for t in range(NT):
                                ins = T.transpose(bank[g % 4][0:MQK, 256 * k + P * t:256 * k + P * (t + 1)], qk1[:, t, 2 * g + k, :], ident)
                        ins.then_inc(S("qkT_ready"), 1)
                    pe.wait_ge(S("qkT_copied_dve"), 3 * (m + 1))
                    pe.wait_ge(S("qkT_copied_act"), 3 * (m + 1))

                    def pv(h, probs, sem):
                        v = head(h)[2]
                        c = slice(64 * (h % 8), 64 * (h % 8 + 1))
                        b = 4 + 2 * (h // 8)
                        T.matmul(bank[b][:, c], probs[:, 0:P], v[0], start=True, stop=True)
                        T.matmul(bank[b + 1][:, c], probs[:, P:2 * P], v[0], start=True, stop=False)
                        T.matmul(bank[b + 1][:, c], probs[:, 2 * P:3 * P], v[1], start=False, stop=True).then_inc(S(sem), 1)

                    for i in range(14):
                        if i < 12:
                            q, k, _ = head(i)
                            if i >= 2:
                                pe.wait_ge(S("max_ready"), 12 * m + i - 1)
                            T.matmul(bank[i % 2][:, 0:P], q[:, 0:P], k[:, 0:P], start=True, stop=True)
                            T.matmul(bank[i % 2][:, P:384], q[:, P:SEQ], k, start=True, stop=True).then_inc(S("scores_ready"), 1)
                        if 1 <= i < 13:
                            h = i - 1
                            pe.wait_ge(S("probs_ready"), 12 * m + h + 1)
                            if h >= 2:
                                pe.wait_ge(S("pt_copied"), 12 * m + h - 1)
                            for j in range(3):
                                ins = T.transpose(bank[2 + h % 2][:, P * j:P * (j + 1)], sc_t[:, h % 2, P * j:P * (j + 1)], ident)
                            ins.then_inc(S("probsT_ready"), 1)
                        if 1 <= i <= SH:
                            h = i - 1
                            pe.wait_ge(S("stick_ready"), SH * m + h + 1)
                            if h >= 2:
                                pe.wait_ge(S("zs_ready"), SH * m + h - 1)
                            b, u = bank[6 + h % 2], sb_u(h)
                            T.matmul(b[:, 0:P], tri, u[:, 0:P], start=True, stop=True)
                            T.matmul(b[:, P:2 * P], tri, u[:, P:2 * P], start=True, stop=False)
                            T.matmul(b[:, P:2 * P], ones, u[:, 2 * P:3 * P], start=False, stop=True)
                            T.matmul(b[:, 2 * P:3 * P], tri, u[:, 2 * P:3 * P], start=True, stop=True).then_inc(S("stick_sum"), 1)
                        if 8 <= i < 8 + SH:
                            if i == 8:
                                pe.wait_ge(S("zs_ready"), SH * (m + 1))
                            pe.wait_ge(S("sb_probs"), SH * m + i - 7)
                            pv(12 + i - 8, sb_u(i - 8), "sb_pv_done")
                        if i >= 2:
                            h = i - 2
                            pe.wait_ge(S("pt_copied"), 12 * m + h + 1)
                            pv(h, pt_t[:, h % 2, :], "pv_done")
                    pe.wait_ge(S("mix0_ready"), m + 1)
                    pe.wait_ge(S("mix1_ready"), m + 1)
                    transposes(mix, KD)
                    gate_rows(a["mod"] + 2)
                    for u in range(6):
                        n = n0 + 20 + u
                        hT_ready(u)
                        rows_unit(n % RING, n + 1, u, u == 0, False, hhi, hlo)
                    hT_ready(6)
                    last_rows(n0 + 26, 6, hhi, hlo)
                else:
                    m = mid2_n[0]
                    mid2_n[0] += 1
                    by_dve = [0, 1, 2, 3, 6]

                    def copied(s):
                        pe.wait_ge(S("strip2_copied0"), 11 * m + s + 1)
                        if s in by_dve:
                            pe.wait_ge(S("strip2_copied1"), 5 * m + by_dve.index(s) + 1)

                    def strip(s):
                        if 3 <= s < 7:
                            copied(s - 3)
                        if s == 9:
                            pe.wait_ge(S("ret_taken"), m + 1)
                        for u in range(4):
                            n = n0 + 4 * s + u
                            if s == 0:
                                hT_ready(2 * u)
                            strip_unit(n % RING, n + 1, u, u == 3, (STRIP_BANKS[s], STRIP_BANKS[s] + 1), 512)

                    for s in range(4):
                        strip(s)
                    pe.wait_ge(S("rope2_done"), m + 1)
                    for g in range(4):
                        if g >= 2:
                            pe.wait_ge(S("qkT2_copied_act" if g % 2 else "qkT2_copied_dve"), 2 * m + 1)
                        for k in range(2):
                            for t in range(NT):
                                j = 2 * g + k
                                ins = T.transpose(bank[6 + g % 2][:, 256 * k + P * t:256 * k + P * (t + 1)], qk2[:, t, P * j:P * (j + 1)], ident)
                        ins.then_inc(S("qkT2_ready"), 1)
                    for s in range(4, 7):
                        strip(s)
                    copied(6)
                    pe.wait_ge(S("qkT2_copied_dve"), 2 * (m + 1))
                    pe.wait_ge(S("qkT2_copied_act"), 2 * (m + 1))
                    for i in range(RH + 1):
                        if i < RH:
                            r0 = 64 * (i % 2)
                            q, k = qkT2[r0:r0 + 64, i // 2, :], qkT2[r0:r0 + 64, 4 + i // 2, :]
                            if i >= 2:
                                pe.wait_ge(S("ret_probs"), RH * m + i - 1)
                            T.matmul(bank[6 + i % 2][:, 0:SEQ], k[:, 0:P], q, start=True, stop=True)
                            T.matmul(bank[6 + i % 2][:, SEQ:384], k[:, P:SEQ], q[:, P:SEQ], start=True, stop=True).then_inc(S("ret_scores"), 1)
                        if i >= 1:
                            h = i - 1
                            pe.wait_ge(S("ret_probs"), RH * m + h + 1)
                            pr = sc_t[:, h % 2, :]
                            c = slice(RV * (h % 4), RV * (h % 4 + 1))
                            v0, v1 = (v2[:, t, RV * h:RV * (h + 1)] for t in range(NT))
                            T.matmul(bank[h // 4][:, c], pr[:, 0:P], v0, start=True, stop=True)
                            T.matmul(bank[2 + h // 4][:, c], pr[:, P:2 * P], v0, start=True, stop=False)
                            T.matmul(bank[2 + h // 4][:, c], pr[:, 2 * P:3 * P], v1, start=False, stop=True).then_inc(S("ret_pv"), 1)
                    for s in range(7, 11):
                        strip(s)
                    pe.wait_ge(S("ret_ready"), m + 1)
                    copied(8)
                    transposes(ret, KD)
                    ret_groups = tr[0]
                    pe.wait_ge(S("hf_ready"), ret_groups - 2)
                    for g in range(4):
                        b, c0 = bank[6 + g // 2], 256 * (g % 2)
                        w = con2[:, C2_POOL + 384 * g:C2_POOL + 384 * (g + 1)]
                        s0, s1 = (p2[:, t, P * g:P * (g + 1)] for t in range(NT))
                        T.matmul(b[:, c0:c0 + P], s0, w[:, 0:P], start=True, stop=True)
                        T.matmul(b[:, c0 + P:c0 + 2 * P], s0, w[:, P:2 * P], start=True, stop=False)
                        ins = T.matmul(b[:, c0 + P:c0 + 2 * P], s1, w[:, 2 * P:3 * P], start=False, stop=True)
                        if g % 2:
                            ins.then_inc(S("pool_ready"), 1)
                    copied(10)

                    def ret_units(k0, k1, n):
                        for k in range(k0, k1):
                            pe.wait_ge(S("hlo_done"), ret_groups - KD // 2 + k // 2 + 1)
                            rows_unit((n + k) % RING, n + k + 1, k, k == 0, k == 7, hhi, hlo)

                    ret_units(0, 4, n0 + 44)
                    pe.wait_ge(S("plo_done"), 2 * (m + 1))
                    for u in range(2):
                        n = n0 + 48 + u
                        pe.wait_ge(S("lo_done"), n + 1)
                        for k in range(2):
                            o = bank[TRB[u]][:, 256 * k:256 * (k + 1)]
                            wh, wl = (w[:, n % RING, P * k:P * (k + 1)] for w in (whi, wlo))
                            p_hi, p_lo = (pool_parts(w, n0 + 48, u)[:, 256 * k:256 * (k + 1)] for w in (whi, wlo))
                            T.matmul(o, wh, p_hi, start=True, stop=False)
                            T.matmul(o, wh, p_lo, start=False, stop=False)
                            ins = T.matmul(o, wl, p_hi, start=False, stop=True)
                        ins.then_inc(S("mm_done"), 1)
                        tr[0] += 1
                    ret_units(4, 8, n0 + 46)
                    for u in range(4):
                        n = n0 + 54 + u
                        pe.wait_ge(S("hlo_done"), tr[0] - 1 + u // 2)
                        pe.wait_ge(S("hf_ready"), tr[0])
                        rows_unit(n % RING, n + 1, u, u == 0, u == 3, hhi, hlo, first_bank=4)

                    def merged(half):
                        pe.wait_ge(S("merged_ready"), 2 * m + half + 1)

                    transposes(gates, KD, TRB_MERGED, halves=merged)
                    gate_rows(a["mod"] + 2)
                    for u in range(6):
                        n = n0 + 58 + u
                        hT_ready(u)
                        rows_unit(n % RING, n + 1, u, u == 0, False, hhi, hlo)
                    hT_ready(6)
                    last_rows(n0 + 64, 6, hhi, hlo)


INPUTS = ["x", "c", "positions", "rel_bias", "norm_g", "w_mod", "b_mod", "w_ffn1_gu", "w_ffn1_down", "w_in", "q_a_norm",
          "kv_a_norm", "w_uq", "w_ukv", "mla_q_norm", "mla_k_norm", "swa_q_norm", "swa_k_norm", "sinks", "out_norm",
          "w_out", "w_ffn2_gu", "w_ffn2_down", "c_2", "w_ada_2", "b_ada_2", "norm1_2", "w_in_2", "w_ret_o_2",
          "w_pool_grp_2", "pool_scale_2", "w_pool_o_2", "w_out_2", "norm2_2", "w_ffn_in_2", "w_ffn_out_2", "final_norm_2"]


def kernel(**inputs):
    import concourse.bacc as bacc
    from concourse.bass_utils import run_bass_kernel_spmd

    nc = bacc.Bacc("TRN2", target_bir_lowering=False, num_devices=1)
    arrays, A = {}, {}
    con, con2 = constants()
    for name, a in [(k, inputs[k]) for k in INPUTS] + [("con", con), ("con2", con2)]:
        a = np.ascontiguousarray(a)
        arrays["in_" + name] = a
        A[name] = nc.dram_tensor("in_" + name, a.shape, mybir.dt.from_np(a.dtype), kind="ExternalInput").ap()
    out = nc.dram_tensor("out_0", (1, SEQ, D), F32, kind="ExternalOutput").ap()
    build(nc, A, out)
    r = run_bass_kernel_spmd(nc, [arrays], core_ids=[0])
    return r.results[0]["out_0"]
```
